# Optimizing a Trainium2 kernel written in Bass

```python
import math
import jax, jax.numpy as jnp
from jax import lax
import numpy as np
import jax
import jax.numpy as jnp

D_MODEL = 2048
BATCH = 1
SEQ = 256
DEPTH = 1

CHUNK = 64
Q_BLOCK = 128
SB_HEADS = 8
SB_HEAD_DIM = 128
D_SB = SB_HEADS * SB_HEAD_DIM
D_CONV = D_MODEL // 2
CONV_WIDTH = 31
D_FF = 4 * D_MODEL
EPS = 1e-6
IN_SPLITS = (D_SB, D_SB, D_SB, D_CONV, D_CONV, D_MODEL, D_MODEL)
D_IN = sum(IN_SPLITS)


def rmsnorm(x, g):
    xf = x.astype(jnp.float32)
    y = xf * lax.rsqrt(jnp.mean(xf * xf, axis=-1, keepdims=True) + EPS)
    return (y * g.astype(jnp.float32)).astype(x.dtype)

def layernorm(x, g, b):
    xf = x.astype(jnp.float32)
    mu = jnp.mean(xf, axis=-1, keepdims=True)
    var = jnp.mean(jnp.square(xf - mu), axis=-1, keepdims=True)
    y = (xf - mu) * lax.rsqrt(var + EPS)
    return (y * g.astype(jnp.float32) + b.astype(jnp.float32)).astype(x.dtype)

def stick_breaking_attention(q, k, v):
    b, s, h, dh = q.shape
    scale = 1.0 / math.sqrt(dh)
    outs = []
    for i in range(s // Q_BLOCK):
        t0, t1 = i * Q_BLOCK, (i + 1) * Q_BLOCK
        qb = q[:, t0:t1]
        kb = k[:, :t1]
        vb = v[:, :t1]
        z = jnp.einsum('bqhd,bkhd->bhqk', qb, kb).astype(jnp.float32) * scale
        tq = t0 + jnp.arange(Q_BLOCK)[:, None]
        sk = jnp.arange(t1)[None, :]
        mask = sk < tq
        log_1m = jnp.where(mask, jax.nn.log_sigmoid(-z), 0.0)
        suffix = lax.cumsum(log_1m, axis=3, reverse=True) - log_1m
        a = jnp.where(mask, jnp.exp(jax.nn.log_sigmoid(z) + suffix), 0.0)
        outs.append(jnp.einsum('bhqk,bkhd->bqhd', a.astype(vb.dtype), vb))
    return jnp.concatenate(outs, axis=1)

def causal_depthwise_conv(u, w, bias):
    c = u.shape[-1]
    y = lax.conv_general_dilated(
        u, w.reshape(CONV_WIDTH, 1, c).astype(u.dtype),
        window_strides=(1,), padding=[(CONV_WIDTH - 1, 0)],
        dimension_numbers=('NWC', 'WIO', 'NWC'), feature_group_count=c)
    return y + bias

def first_inputs(seed: int = 0) -> dict:
    key = jax.random.key(seed)
    ks = jax.random.split(key, 17)
    L = DEPTH
    nrm = lambda k, shape, fan_in: jax.random.normal(k, shape, jnp.float32) * (fan_in ** -0.5)
    gain = lambda k, shape: 1.0 + 0.02 * jax.random.normal(k, shape, jnp.float32)
    small = lambda k, shape: 0.02 * jax.random.normal(k, shape, jnp.float32)
    return {
        "x": jax.random.normal(ks[0], (BATCH, SEQ, D_MODEL), jnp.float32),
        "g_pre_mix": gain(ks[1], (L, D_MODEL)),
        "w_in": nrm(ks[2], (L, D_MODEL, D_IN), D_MODEL),
        "b_in": small(ks[3], (L, D_IN)),
        "w_dw": nrm(ks[4], (L, CONV_WIDTH, D_CONV), CONV_WIDTH),
        "b_dw": small(ks[5], (L, D_CONV)),
        "g_conv_ln": gain(ks[6], (L, D_CONV)),
        "b_conv_ln": small(ks[7], (L, D_CONV)),
        "w_sb_out": nrm(ks[8], (L, D_SB, D_MODEL), D_SB),
        "w_conv_out": nrm(ks[9], (L, D_CONV, D_MODEL), D_CONV),
        "w_o": nrm(ks[10], (L, D_MODEL, D_MODEL), D_MODEL),
        "g_post_mix": gain(ks[11], (L, D_MODEL)),
        "g_pre_mlp": gain(ks[12], (L, D_MODEL)),
        "w_up": nrm(ks[13], (L, D_MODEL, D_FF), D_MODEL),
        "w_down": nrm(ks[14], (L, D_FF, D_MODEL), D_FF),
        "g_post_mlp": gain(ks[15], (L, D_MODEL)),
    }

def first_block(x, g_pre_mix, w_in, b_in, w_dw, b_dw, g_conv_ln, b_conv_ln,
              w_sb_out, w_conv_out, w_o, g_post_mix, g_pre_mlp, w_up, w_down,
              g_post_mlp):
    b, s, _ = x.shape
    offs = np.cumsum(IN_SPLITS)[:-1].tolist()
    for l in range(DEPTH):
        h = rmsnorm(x, g_pre_mix[l])
        proj = jnp.einsum('bsd,de->bse', h, w_in[l]) + b_in[l]
        q, k, v, glu_a, glu_b, gate_sb, gate_cv = jnp.split(proj, offs, axis=-1)
        hd = (b, s, SB_HEADS, SB_HEAD_DIM)
        o_sb = stick_breaking_attention(q.reshape(hd), k.reshape(hd), v.reshape(hd))
        o_sb = jnp.einsum('bse,ed->bsd', o_sb.reshape(b, s, D_SB), w_sb_out[l])
        u = glu_a * jax.nn.sigmoid(glu_b)
        u = causal_depthwise_conv(u, w_dw[l], b_dw[l])
        u = jax.nn.silu(layernorm(u, g_conv_ln[l], b_conv_ln[l]))
        o_cv = jnp.einsum('bsc,cd->bsd', u, w_conv_out[l])
        merged = jax.nn.sigmoid(gate_sb) * o_sb + jax.nn.sigmoid(gate_cv) * o_cv
        y = jnp.einsum('bsd,de->bse', merged, w_o[l])
        x = x + rmsnorm(y, g_post_mix[l])
        h = rmsnorm(x, g_pre_mlp[l])
        f = jnp.square(jax.nn.relu(jnp.einsum('bsd,df->bsf', h, w_up[l])))
        f = jnp.einsum('bsf,fd->bsd', f, w_down[l])
        x = x + rmsnorm(f, g_post_mlp[l])
    return x


MEM_LEN = 256
RMS_EPS = 1e-6
DN_HEAD_DIM = 128
DN_WIDTH = D_MODEL // 2
DN_HEADS = DN_WIDTH // DN_HEAD_DIM
DN_CONV = 4
DN_CHUNK = 64
RW_HEAD_DIM = 64
RW_WIDTH = D_MODEL - DN_WIDTH
RW_HEADS = RW_WIDTH // RW_HEAD_DIM
RW_DECAY_LORA = 64
RW_AAA_LORA = 64
RW_GATE_LORA = 128
RW_GN_EPS = 64e-5
DN_COLS = 4 * DN_WIDTH + 2 * DN_HEADS
RW_COLS = 3 * RW_WIDTH + RW_DECAY_LORA + RW_AAA_LORA + RW_GATE_LORA
IN_COLS = DN_COLS + RW_COLS
XA_HEADS = 4
XA_HEAD_DIM = 128
XA_WIDTH = XA_HEADS * XA_HEAD_DIM
FFN_HIDDEN = 4 * D_MODEL


def rmsnorm_2(x, w):
    xf = x.astype(jnp.float32)
    y = xf * lax.rsqrt(jnp.mean(xf * xf, axis=-1, keepdims=True) + RMS_EPS)
    return (y * w.astype(jnp.float32)).astype(x.dtype)

def l2norm(x):
    return x * lax.rsqrt(jnp.sum(x * x, axis=-1, keepdims=True) + 1e-6)

def causal_depthwise_conv_2(x, w):
    k = w.shape[0]
    return lax.conv_general_dilated(
        x, w[:, None, :].astype(x.dtype), window_strides=(1,), padding=[(k - 1, 0)],
        dimension_numbers=('NWC', 'WIO', 'NWC'), feature_group_count=x.shape[-1])

def token_shift(p):
    return jnp.pad(p, ((0, 0), (1, 0), (0, 0)))[:, :-1]

def chunked_gated_delta_rule(q, k, v, g, beta):
    b, s, h, dk = q.shape
    dv = v.shape[-1]
    c = DN_CHUNK
    n = s // c

    def chunks(t):
        return t.reshape(b, n, c, h, -1).transpose(0, 3, 1, 2, 4)

    q = chunks(q) * (dk ** -0.5)
    k = chunks(k)
    v = chunks(v)
    g = g.reshape(b, n, c, h).transpose(0, 3, 1, 2)
    beta = beta.reshape(b, n, c, h).transpose(0, 3, 1, 2)
    gc = jnp.cumsum(g, axis=-1)
    idx = jnp.arange(c)
    causal = idx[:, None] >= idx[None, :]
    strict = idx[:, None] > idx[None, :]
    decay = jnp.exp(jnp.where(causal, gc[..., :, None] - gc[..., None, :], -jnp.inf))
    kb = k * beta[..., None]
    a_strict = jnp.where(strict, jnp.einsum('bhncd,bhnmd->bhncm', kb, k) * decay, 0.0)
    lower = a_strict + jnp.eye(c, dtype=q.dtype)
    rhs = jnp.concatenate([v * beta[..., None], kb * jnp.exp(gc)[..., None]], axis=-1)
    sol = lax.linalg.triangular_solve(lower, rhs, left_side=True, lower=True)
    u, w = sol[..., :dv], sol[..., dv:]
    attn = jnp.einsum('bhncd,bhnmd->bhncm', q, k) * decay
    qg = q * jnp.exp(gc)[..., None]
    g_last = gc[..., -1]
    kd = k * jnp.exp(g_last[..., None] - gc)[..., None]
    xs = tuple(jnp.moveaxis(t, 2, 0) for t in (u, w, qg, attn, kd, g_last))

    def step(state, xs_n):
        u_n, w_n, qg_n, attn_n, kd_n, gl_n = xs_n
        v_new = u_n - jnp.einsum('bhcd,bhde->bhce', w_n, state)
        o_n = jnp.einsum('bhcd,bhde->bhce', qg_n, state) + jnp.einsum('bhcm,bhme->bhce', attn_n, v_new)
        state = state * jnp.exp(gl_n)[..., None, None] + jnp.einsum('bhcd,bhce->bhde', kd_n, v_new)
        return state, o_n

    s0 = jnp.zeros((b, h, dk, dv), q.dtype)
    _, o = lax.scan(step, s0, xs)
    return o.transpose(1, 0, 3, 2, 4).reshape(b, s, h, dv)

def wkv7_scan(r, w, k, v, kk, a):
    b, s, h, nd = r.shape
    xs = tuple(jnp.swapaxes(t, 0, 1) for t in (r, w, k, v, kk, a))

    def step(state, xs_t):
        r_t, w_t, k_t, v_t, kk_t, a_t = xs_t
        sa = jnp.einsum('bhvk,bhk->bhv', state, -kk_t)
        state = (state * w_t[:, :, None, :] + sa[..., None] * (kk_t * a_t)[:, :, None, :]
                 + v_t[..., None] * k_t[:, :, None, :])
        return state, jnp.einsum('bhvk,bhk->bhv', state, r_t)

    s0 = jnp.zeros((b, h, nd, nd), r.dtype)
    _, y = lax.scan(step, s0, xs)
    return jnp.swapaxes(y, 0, 1)

def deltanet_group(p, conv_w, a_log, dt_bias, norm_w):
    p = p.astype(jnp.float32)
    b, s, _ = p.shape
    qkv, z, ga, gb = jnp.split(p, [3 * DN_WIDTH, 4 * DN_WIDTH, 4 * DN_WIDTH + DN_HEADS], axis=-1)
    qkv = jax.nn.silu(causal_depthwise_conv_2(qkv, conv_w))
    q, k, v = (t.reshape(b, s, DN_HEADS, DN_HEAD_DIM) for t in jnp.split(qkv, 3, axis=-1))
    q = l2norm(q)
    k = l2norm(k)
    beta = jax.nn.sigmoid(gb)
    g = -jnp.exp(a_log) * jax.nn.softplus(ga + dt_bias)
    o = chunked_gated_delta_rule(q, k, v, g, beta)
    o = rmsnorm_2(o, norm_w) * jax.nn.silu(z.reshape(b, s, DN_HEADS, DN_HEAD_DIM))
    return o.reshape(b, s, DN_WIDTH)

def rwkv7_group(p, mu, w0, w2, a0, a2, g2, k_k, k_a, r_k, ln_w, ln_b):
    p = p.astype(jnp.float32)
    b, s, _ = p.shape
    p = p + (token_shift(p) - p) * mu
    pr, pk, pv, pw, pa, pg = jnp.split(
        p, [RW_WIDTH, 2 * RW_WIDTH, 3 * RW_WIDTH, 3 * RW_WIDTH + RW_DECAY_LORA,
            3 * RW_WIDTH + RW_DECAY_LORA + RW_AAA_LORA], axis=-1)

    def heads(t):
        return t.reshape(b, s, RW_HEADS, RW_HEAD_DIM)

    log_w = -jax.nn.softplus(-(w0 + jnp.tanh(pw) @ w2)) - 0.5
    decay = jnp.exp(-jnp.exp(log_w))
    a = jax.nn.sigmoid(a0 + pa @ a2)
    gate = jax.nn.sigmoid(pg) @ g2
    kk = heads(pk * k_k)
    kk = kk / jnp.maximum(jnp.sqrt(jnp.sum(kk * kk, axis=-1, keepdims=True)), 1e-12)
    k = pk * (1.0 + (a - 1.0) * k_a)
    r_h, k_h, v_h = heads(pr), heads(k), heads(pv)
    y = wkv7_scan(r_h, heads(decay), k_h, v_h, kk, heads(a))
    mean = jnp.mean(y, axis=-1, keepdims=True)
    var = jnp.mean(jnp.square(y - mean), axis=-1, keepdims=True)
    y = ((y - mean) * lax.rsqrt(var + RW_GN_EPS)).reshape(b, s, RW_WIDTH) * ln_w + ln_b
    bonus = jnp.sum(r_h * k_h * r_k, axis=-1, keepdims=True) * v_h
    return (y + bonus.reshape(b, s, RW_WIDTH)) * gate

def memory_cross_attention(hn, mn, wq, wk, wv, wo):
    b, s, _ = hn.shape
    m = mn.shape[1]
    q = (hn @ wq).reshape(b, s, XA_HEADS, XA_HEAD_DIM)
    k = (mn @ wk).reshape(b, m, XA_HEADS, XA_HEAD_DIM)
    v = (mn @ wv).reshape(b, m, XA_HEADS, XA_HEAD_DIM)
    scores = jnp.einsum('bshd,bmhd->bhsm', q, k).astype(jnp.float32) * (XA_HEAD_DIM ** -0.5)
    probs = jax.nn.softmax(scores, axis=-1).astype(v.dtype)
    o = jnp.einsum('bhsm,bmhd->bshd', probs, v).reshape(b, s, XA_WIDTH)
    return o @ wo

def squared_relu_mlp(u, w1, w2):
    return jnp.square(jax.nn.relu(u @ w1)) @ w2

def second_inputs(seed: int = 0) -> dict:
    key = jax.random.key(seed)
    ks = jax.random.split(key, 32)
    L = DEPTH
    D = D_MODEL

    def normal(i, shape, scale):
        return jax.random.normal(ks[i], shape, jnp.float32) * scale

    def uniform(i, shape, lo, hi):
        return jax.random.uniform(ks[i], shape, jnp.float32, lo, hi)

    dt = jnp.exp(uniform(6, (L, DN_HEADS), math.log(1e-3), math.log(1e-1)))
    return {
        'x': normal(0, (BATCH, SEQ, D), 1.0),
        'mem': normal(1, (BATCH, MEM_LEN, D), 1.0),
        'mix_norm_w': 1.0 + normal(2, (L, D), 0.02),
        'w_in': normal(3, (L, D, IN_COLS), D ** -0.5),
        'dn_conv_w': normal(4, (L, DN_CONV, 3 * DN_WIDTH), DN_CONV ** -0.5),
        'dn_a_log': jnp.log(uniform(5, (L, DN_HEADS), 1.0, 16.0)),
        'dn_dt_bias': dt + jnp.log(-jnp.expm1(-dt)),
        'dn_norm_w': 1.0 + normal(7, (L, DN_HEAD_DIM), 0.02),
        'rw_mu': uniform(8, (L, RW_COLS), 0.0, 1.0),
        'rw_w0': uniform(9, (L, RW_WIDTH), -6.0, 1.0),
        'rw_w2': normal(10, (L, RW_DECAY_LORA, RW_WIDTH), 0.1 * RW_DECAY_LORA ** -0.5),
        'rw_a0': normal(11, (L, RW_WIDTH), 0.1),
        'rw_a2': normal(12, (L, RW_AAA_LORA, RW_WIDTH), 0.1 * RW_AAA_LORA ** -0.5),
        'rw_g2': normal(13, (L, RW_GATE_LORA, RW_WIDTH), RW_GATE_LORA ** -0.5),
        'rw_k_k': 0.85 + normal(14, (L, RW_WIDTH), 0.02),
        'rw_k_a': 1.0 + normal(15, (L, RW_WIDTH), 0.02),
        'rw_r_k': normal(16, (L, RW_HEADS, RW_HEAD_DIM), 0.1),
        'rw_ln_w': 1.0 + normal(17, (L, RW_WIDTH), 0.02),
        'rw_ln_b': normal(18, (L, RW_WIDTH), 0.02),
        'w_out': normal(19, (L, D, D), D ** -0.5),
        'xa_norm_w': 1.0 + normal(20, (L, D), 0.02),
        'mem_norm_w': 1.0 + normal(21, (L, D), 0.02),
        'xa_wq': normal(22, (L, D, XA_WIDTH), D ** -0.5),
        'xa_wk': normal(23, (L, D, XA_WIDTH), D ** -0.5),
        'xa_wv': normal(24, (L, D, XA_WIDTH), D ** -0.5),
        'xa_wo': normal(25, (L, XA_WIDTH, D), XA_WIDTH ** -0.5),
        'ffn_norm_w': 1.0 + normal(26, (L, D), 0.02),
        'ffn_w1': normal(27, (L, D, FFN_HIDDEN), D ** -0.5),
        'ffn_w2': normal(28, (L, FFN_HIDDEN, D), FFN_HIDDEN ** -0.5),
        'final_norm_w': 1.0 + normal(29, (D,), 0.02),
    }

def second_block(x, mem, mix_norm_w, w_in, dn_conv_w, dn_a_log, dn_dt_bias, dn_norm_w, rw_mu, rw_w0,
              rw_w2, rw_a0, rw_a2, rw_g2, rw_k_k, rw_k_a, rw_r_k, rw_ln_w, rw_ln_b, w_out,
              xa_norm_w, mem_norm_w, xa_wq, xa_wk, xa_wv, xa_wo, ffn_norm_w, ffn_w1, ffn_w2,
              final_norm_w):
    h = x
    for l in range(DEPTH):
        u = rmsnorm_2(h, mix_norm_w[l])
        p = u @ w_in[l]
        o_dn = deltanet_group(p[..., :DN_COLS], dn_conv_w[l], dn_a_log[l], dn_dt_bias[l], dn_norm_w[l])
        o_rw = rwkv7_group(p[..., DN_COLS:], rw_mu[l], rw_w0[l], rw_w2[l], rw_a0[l], rw_a2[l], rw_g2[l],
                           rw_k_k[l], rw_k_a[l], rw_r_k[l], rw_ln_w[l], rw_ln_b[l])
        h = h + jnp.concatenate([o_dn, o_rw], axis=-1).astype(h.dtype) @ w_out[l]
        h = h + memory_cross_attention(rmsnorm_2(h, xa_norm_w[l]), rmsnorm_2(mem, mem_norm_w[l]),
                                       xa_wq[l], xa_wk[l], xa_wv[l], xa_wo[l])
        h = h + squared_relu_mlp(rmsnorm_2(h, ffn_norm_w[l]), ffn_w1[l], ffn_w2[l])
    return rmsnorm_2(h, final_norm_w)


def setup_inputs(seed=0):
    out = dict(first_inputs(seed))
    for name, value in second_inputs(seed + 1).items():
        if name != "x":
            out[name + "_2"] = value
    return out


def reference(
    x, g_pre_mix, w_in, b_in, w_dw, b_dw, g_conv_ln, b_conv_ln, w_sb_out, w_conv_out, w_o,
    g_post_mix, g_pre_mlp, w_up, w_down, g_post_mlp, mem_2, mix_norm_w_2, w_in_2, dn_conv_w_2,
    dn_a_log_2, dn_dt_bias_2, dn_norm_w_2, rw_mu_2, rw_w0_2, rw_w2_2, rw_a0_2, rw_a2_2, rw_g2_2,
    rw_k_k_2, rw_k_a_2, rw_r_k_2, rw_ln_w_2, rw_ln_b_2, w_out_2, xa_norm_w_2, mem_norm_w_2,
    xa_wq_2, xa_wk_2, xa_wv_2, xa_wo_2, ffn_norm_w_2, ffn_w1_2, ffn_w2_2, final_norm_w_2,
):
    x = first_block(
        x, g_pre_mix, w_in, b_in, w_dw, b_dw, g_conv_ln, b_conv_ln, w_sb_out, w_conv_out, w_o,
        g_post_mix, g_pre_mlp, w_up, w_down, g_post_mlp,
    )
    return second_block(
        x, mem_2, mix_norm_w_2, w_in_2, dn_conv_w_2, dn_a_log_2, dn_dt_bias_2, dn_norm_w_2,
        rw_mu_2, rw_w0_2, rw_w2_2, rw_a0_2, rw_a2_2, rw_g2_2, rw_k_k_2, rw_k_a_2, rw_r_k_2,
        rw_ln_w_2, rw_ln_b_2, w_out_2, xa_norm_w_2, mem_norm_w_2, xa_wq_2, xa_wk_2, xa_wv_2,
        xa_wo_2, ffn_norm_w_2, ffn_w1_2, ffn_w2_2, final_norm_w_2,
    )


_drawn_inputs = setup_inputs


def setup_inputs(seed=0):
    import zlib

    import numpy as np

    out = dict(_drawn_inputs(seed))
    spreads = {}
    factors = {'g_conv_ln': 3.865,
     'b_conv_ln': 4.654,
     'g_post_mix': 3.362,
     'g_pre_mlp': 3.772,
     'g_post_mlp': 4.06,
     'mix_norm_w_2': 4.854,
     'dn_norm_w_2': 64.0,
     'rw_w2_2': 64.0,
     'rw_a0_2': 5.393,
     'rw_a2_2': 5.964,
     'rw_k_k_2': 64.0,
     'rw_k_a_2': 8.0,
     'rw_ln_w_2': 175.908,
     'rw_ln_b_2': 200.0,
     'xa_norm_w_2': 42.911,
     'mem_norm_w_2': 43.053,
     'ffn_norm_w_2': 35.328,
     'final_norm_w_2': 21.082}
    for name, (base, spread) in spreads.items():
        noise = np.random.default_rng([zlib.crc32(name.encode()), seed]).standard_normal(out[name].shape)
        drawn = base * np.exp(spread * noise) if base else spread * noise
        out[name] = jnp.asarray(drawn.astype(out[name].dtype))
    for name, factor in factors.items():
        out[name] = (out[name] * factor).astype(out[name].dtype)
    return out
```

```python
from contextlib import ExitStack

import numpy as np

import concourse.bass as bass
from concourse import mybir

F32 = mybir.dt.float32
F32R = mybir.dt.float32r
ALU = mybir.AluOpType
ACT = mybir.ActivationFunctionType
AX = mybir.AxisListType

P = 128
T = 256
D = 2048
DT = D // P
EPS = 1e-6
PAD = 4
COLS = T + PAD
BW = 256
KG = 4
RING = 4
SB_H, SB_D = 8, 128
CONV = 31
UPAD = CONV - 1
UCOLS = T + UPAD
D_FF = 4 * D
FF_PIECES = 4

VEC1 = [("g_pre_mix", 16), ("b_in", 72), ("w_dw", CONV * 8), ("b_dw", 8), ("g_conv_ln", 8), ("b_conv_ln", 8),
        ("g_post_mix", 16), ("g_pre_mlp", 16), ("g_post_mlp", 16)]


def columns(spec):
    at, out = 0, {}
    for name, n in spec:
        out[name] = at
        at += n
    return out, at


VEC2 = [("mix_norm_w_2", 16), ("dn_conv_w_2", 96), ("dn_norm_w_2", 1), ("rw_mu_2", 26), ("rw_w0_2", 8), ("rw_a0_2", 8),
        ("rw_k_k_2", 8), ("rw_k_a_2", 8), ("rw_r_k_2", 8), ("rw_ln_w_2", 8), ("rw_ln_b_2", 8), ("xa_norm_w_2", 16),
        ("mem_norm_w_2", 16), ("ffn_norm_w_2", 16), ("final_norm_w_2", 16)]
V1, NV1 = columns(VEC1)
V2, NV2 = columns(VEC2)

CONSTS = ["ident", "ones", "upto", "before", "before_big", "incl", "ones_head"]
LEVELS = 7
DN_H, RW_H, RW_D = 8, 16, 64
RW_DECAY = float(np.exp(-0.5))
XA_H, XA_D = 4, 128


def constants():
    i = np.arange(P)
    later = (i[:, None] >= i[None, :]).astype(np.float32)
    before = (i[:, None] < i[None, :]).astype(np.float32)
    big = np.where(before > 0, 0.0, -1e30).astype(np.float32)
    incl = (i[:, None] <= i[None, :]).astype(np.float32)
    head = (i[:, None] // RW_D == i[None, :] // RW_D).astype(np.float32)
    return np.concatenate([np.eye(P, dtype=np.float32), np.ones((P, P), np.float32), later, before, big, incl, head],
                          axis=1)


def level_masks():
    i = np.arange(P)
    out = []
    for l in range(LEVELS):
        n = i >> l
        out.append(((n[:, None] % 2 == 0) & (n[None, :] == n[:, None] + 1)).astype(np.float32))
    return np.stack(out, axis=1)


class Gemm:

    def __init__(self, plan, name, w, k, n0, n, x, kind, dst, x_from=0, bias=None, k0=0, apart=P):
        self.name, self.w, self.n0, self.x, self.kind, self.dst = name, w, n0, x, kind, dst
        self.k0, self.x_from, self.bias, self.apart = k0, x_from, bias, apart
        self.groups = k // (P * KG)
        self.blocks = n // BW
        self.b0, self.s0, self.sum0, self.sq0 = plan.blocks, plan.slabs, plan.sums, plan.squares
        self.unroll = 4 if self.groups == 1 else 2
        self.turn = self.unroll * self.groups
        plan.blocks += self.blocks
        plan.slabs += self.blocks * self.groups
        plan.sums += self.blocks if kind != "store" else 0
        plan.squares += self.blocks if kind == "relu2" else 0
        plan.stages.append(self)
        assert self.s0 % RING == 0 and self.turn % RING == 0

    def slab(self, i, block, j):
        o = block * self.groups + j
        return o % RING, self.s0 // RING + i * (self.turn // RING) + o // RING, self.s0 + i * self.turn + o


class Steps:

    def __init__(self, sem, names):
        self.sem, self.names, self.n = sem, names, 0

    def at(self, name, r=0):
        return r * len(self.names) + self.names.index(name) + 1

    def done(self, ins, name, r=0):
        self.n += 1
        assert self.at(name, r) == self.n, (name, r, self.names[(self.n - 1) % len(self.names)])
        ins.then_inc(self.sem, 1)

    def wait(self, eng, name, r=0):
        eng.wait_ge(self.sem, self.at(name, r))


class Plan:
    def __init__(self):
        self.blocks = self.slabs = self.sums = self.squares = 0
        self.stages = []


def build_program(nc, a, out):
    plan = Plan()
    ctx = ExitStack()
    with ctx:
        base = 16640
        top = [base]

        def at(name, shape, dt, offset=None):
            size = 4 * int(np.prod(shape[1:]))
            if offset is None:
                offset = top[0]
                top[0] += (size + 31) // 32 * 32
            return nc.alloc_sbuf_tensor_at(name, shape, dt, offset=offset)

        def sem(name):
            return ctx.enter_context(nc.semaphore(name))

        raw = at("raw", [P, RING, KG, BW], F32)
        hi = at("hi", [P, RING, KG, BW], F32R)
        lo = at("lo", [P, RING, KG, BW], F32R)
        half = at("half", [P, 2, T], F32)
        sq = at("sq", [P, 2, T], F32)
        rs = at("rs", [P, T], F32)
        resid = at("resid", [P, DT, T], F32)
        xa_at = top[0]
        xa = at("xa", [P, DT, 2 * T], F32R)
        xb_at = top[0]
        xb = at("xb", [P, DT, 2 * T], F32R)
        work_at = top[0]
        work = at("work", [P, 64, COLS], F32)
        cst = at("cst", [P, len(CONSTS), P], F32)
        vec = at("vec", [P, NV1 + NV2], F32)
        small = at("small", [P, 160], F32)
        u = at("u", [P, 8, UCOLS], F32, xb_at + 16384)
        zs = at("zs", [P, 3 * P], F32, xb_at + 16384 + 8 * UCOLS * 4)
        la = at("la", [P, 3 * P], F32, xb_at + 16384 + 8 * UCOLS * 4 + 1536)
        vt = at("vt", [P, 2, P], F32, xb_at + 16384 + 8 * UCOLS * 4 + 3072)

        def const(name):
            return cst[:, CONSTS.index(name), :]

        def v1(name, i=0):
            return vec[:, V1[name] + i:V1[name] + i + 1]

        pg = ctx.enter_context(nc.psum_tensor("pg", [P, 2, 2, 2 * T], F32))
        p4 = ctx.enter_context(nc.psum_tensor("p4", [P, 4, 512], F32))
        ps = [p4[:, n] for n in range(4)]

        w_in = a["w_in"]
        TA, TB_, TQ, TK, TV, TGS, TGC, TY = 0, 8, 16, 24, 32, 0, 40, 56
        g_glu = Gemm(plan, "glu", w_in, D, 3072, 2048, xa, "store", (work, TA, PAD), bias=V1["b_in"] + 24)
        g_qkv = Gemm(plan, "qkv", w_in, D, 0, 3072, xa, "store", (work, TQ, PAD), bias=V1["b_in"])
        g_gsb = Gemm(plan, "gate_sb", w_in, D, 5120, 2048, xa, "store", (work, TGS, PAD), bias=V1["b_in"] + 40)
        g_gcv = Gemm(plan, "gate_cv", w_in, D, 7168, 2048, xa, "store", (work, TGC, PAD), bias=V1["b_in"] + 56)
        g_sbo = Gemm(plan, "sb_out", a["w_sb_out"], D // 2, 0, D, xb, "mult", (work, TGS, PAD))
        g_cvo = Gemm(plan, "conv_out", a["w_conv_out"], D // 2, 0, D, xb, "mult", (work, TGC, PAD), x_from=8)
        g_wo = Gemm(plan, "w_o", a["w_o"], D, 0, D, xa, "store", (work, 16, PAD))
        ff1 = []
        for p in range(FF_PIECES):
            up = Gemm(plan, f"up{p}", a["w_up"], D, p * D, D, xa, "relu2", (xb, 0, 0))
            down = Gemm(plan, f"down{p}", a["w_down"], D, 0, D, xb, "add" if p else "store", (work, 16, PAD), k0=p * D)
            ff1 += [up, down]

        consts_in, resid_in = sem("consts_in"), sem("resid_in")
        raw_in = [sem(f"raw_in{n}") for n in range(RING)]
        hi_ready = sem("hi_ready")
        lo_ready = sem("lo_ready")
        slab_used = sem("slab_used")
        half_out = sem("half_out")
        evacuated = sem("evacuated")
        summed = sem("summed")
        squared, rounded = sem("squared"), sem("rounded")
        x_ready = sem("x_ready")
        norm_sq, norm_used, norm_sum = sem("norm_sq"), sem("norm_used"), sem("norm_sum")
        norm_std, norm_rs, norm_nx, norm_hi = sem("norm_std"), sem("norm_rs"), sem("norm_nx"), sem("norm_hi")
        norm_res = sem("norm_res")
        dve_seq, act_seq = sem("dve_seq"), sem("act_seq")
        glu_sig, glu_u = sem("glu_sig"), sem("glu_u")
        att_z, att_zs, att_ln, att_sp, att_s, att_t = [sem("att_" + n) for n in ("z", "zs", "ln", "sp", "s", "t")]
        att_a, att_vt, att_o, att_hi, att_lo, att_vp = [sem("att_" + n) for n in ("a", "vt", "o", "hi", "lo", "vp")]
        conv_done, gates_done, merged_hi, merged = sem("conv_done"), sem("gates_done"), sem("merged_hi"), sem("merged")
        ln_sum, ln_mid, ln_sq, ln_var, ln_std = [sem("ln_" + n) for n in ("sum", "mid", "sq", "var", "std")]
        ln_y, ln_sig, ln_f, ln_hi = [sem("ln_" + n) for n in ("y", "sig", "f", "hi")]
        out_ready, out_done = sem("out_ready"), sem("out_done")
        masks_in, mem_in = sem("masks_in"), sem("mem_in")
        seq = {"dve": 0, "act": 0}

        def dve_link(ins):
            seq["dve"] += 1
            ins.then_inc(dve_seq, 1)
            nc.vector.wait_ge(dve_seq, seq["dve"])

        def act_link(ins):
            seq["act"] += 1
            ins.then_inc(act_seq, 1)
            nc.scalar.wait_ge(act_seq, seq["act"])

        def run_blocks(eng, n, unroll, body, after=None):
            whole = n // unroll
            if after is None and whole > 1:
                with eng.Fori(0, whole) as i:
                    for v in range(unroll):
                        body(i, v)
            else:
                for t in range(whole * unroll):
                    body(t // unroll, t % unroll)
                    if after:
                        after(t)
            for v in range(n - whole * unroll):
                body(whole, v)
                if after:
                    after(whole * unroll + v)

        def load_weights(sp, g):
            w = g.w.rearrange("(k p) n -> p k n", p=P)

            def block(i, v):
                first = sp.snap(g.n0 + (i * g.unroll + v) * BW) if not isinstance(i, int) else g.n0 + (i * g.unroll + v) * BW
                for j in range(g.groups):
                    slot, turn, s = g.slab(i, v, j)
                    k = g.k0 // P + j * KG
                    sp.wait_ge(lo_ready, s + 1)
                    sp.dma_start(raw[:, slot], w[:, k:k + KG, bass.ds(first, BW)]).then_inc(raw_in[slot], 16)

            run_blocks(sp, g.blocks, g.unroll, block)

        def split_hi(act, g, i, v):
            for j in range(g.groups):
                slot, turn, s = g.slab(i, v, j)
                act.wait_ge(raw_in[slot], turn * 16 + 16)
                act.wait_ge(slab_used, s + 1)
                nc.scalar.activation(hi[:, slot], raw[:, slot], ACT.Copy).then_inc(hi_ready, 1)

        def take_half(act, g, i, v):
            b = g.b0 + i * g.unroll + v
            par = (g.b0 + v) % 2
            act.wait_ge(slab_used, g.slab(i, v, g.groups - 1)[2] + 1 + RING)
            act.wait_ge(evacuated, b + 2)
            if g.bias is None:
                nc.scalar.activation(half[:, :, :], pg[:, par, :, T:2 * T], ACT.Copy).then_inc(half_out, 1)
            else:
                for t in range(2):
                    c = g.bias + 2 * (i * g.unroll + v) + t
                    ins = nc.scalar.activation(half[:, t], pg[:, par, t, T:2 * T], ACT.Identity,
                                               bias=vec[:, bass.ds(c, 1)])
                ins.then_inc(half_out, 1)

        def gemm_act(act, g, after=None, follows=None):
            def block(i, v):
                split_hi(act, g, i, v + 1)
                take_half(act, g, i, v)
            run_blocks(act, g.blocks - 1, g.unroll, block, after)
            if follows:
                split_hi(act, follows, 0, 0)
            n = g.blocks - 1
            take_half(act, g, n // g.unroll, n % g.unroll)
            if after:
                after(n)

        def split_lo(dve, g, i, v):
            for j in range(g.groups):
                slot, turn, s = g.slab(i, v, j)
                dve.wait_ge(hi_ready, s + 1)
                nc.vector.tensor_tensor(lo[:, slot], raw[:, slot], hi[:, slot].bitcast(F32),
                                        ALU.subtract).then_inc(lo_ready, 1)

        def evacuate(dve, g, i, v):
            t = i * g.unroll + v
            par = (g.b0 + v) % 2
            into, tile, off = g.dst
            dve.wait_ge(half_out, g.b0 + t + 1)
            psum = pg[:, par, :, 0:T]
            place = into[:, bass.ds(tile + 2 * t, 2), off:off + T]
            if g.kind == "store":
                nc.vector.tensor_tensor(place, psum, half[:, :, :], ALU.add).then_inc(evacuated, 1)
                return
            own = g.sum0 + t + 1
            if g.kind in ("add", "mult"):
                nc.vector.tensor_tensor(half[:, :, :], psum, half[:, :, :], ALU.add).then_inc(summed, 1)
                dve.wait_ge(summed, own)
                nc.vector.tensor_tensor(place, place, half[:, :, :],
                                        ALU.add if g.kind == "add" else ALU.mult).then_inc(evacuated, 1)
                return
            own_sq = g.sq0 + t + 1
            nc.vector.tensor_tensor(sq[:, :, :], psum, half[:, :, :], ALU.add).then_inc(summed, 1)
            dve.wait_ge(summed, own)
            nc.vector.scalar_tensor_tensor(out=sq[:, :, :], in0=sq[:, :, :], scalar=0.0, in1=sq[:, :, :],
                                           op0=ALU.max, op1=ALU.mult).then_inc(squared, 1)
            dve.wait_ge(squared, own_sq)
            nc.vector.tensor_copy(place, sq[:, :, :]).then_inc(rounded, 1)
            dve.wait_ge(rounded, own_sq)
            rest = into[:, bass.ds(tile + 2 * t, 2), T:2 * T]
            nc.vector.tensor_tensor(rest, sq[:, :, :], place.bitcast(F32), ALU.subtract).then_inc(evacuated, 1)

        def gemm_dve(dve, g, after=None, follows=None):
            def block(i, v):
                split_lo(dve, g, i, v + 1)
                evacuate(dve, g, i, v)
            run_blocks(dve, g.blocks - 1, g.unroll, block, after)
            if follows:
                split_lo(dve, follows, 0, 0)
            n = g.blocks - 1
            evacuate(dve, g, n // g.unroll, n % g.unroll)
            if after:
                after(n)

        def gemm_pe(pe, g, after=None, x_tiles=None):
            def block(i, v, waits=False):
                par = (g.b0 + v) % 2
                pe.wait_ge(evacuated, g.b0 + i * g.unroll + v + 1)
                for j in range(g.groups):
                    slot, turn, s = g.slab(i, v, j)
                    pe.wait_ge(lo_ready, s + 1 + RING)
                    if waits:
                        pe.wait_ge(x_ready, x_tiles + KG * (j + 1))
                    for t in range(2):
                        c = t * g.apart
                        for k in range(KG):
                            kk = g.x_from + j * KG + k
                            nc.tensor.matmul(pg[:, par, t, :], lhsT=hi[:, slot, k, c:c + P], rhs=g.x[:, kk, :],
                                             start=(j == 0 and k == 0), stop=False)
                            ins = nc.tensor.matmul(pg[:, par, t, 0:T], lhsT=lo[:, slot, k, c:c + P],
                                                   rhs=g.x[:, kk, 0:T], start=False,
                                                   stop=(j == g.groups - 1 and k == KG - 1))
                    ins.then_inc(slab_used, 1)

            if x_tiles is not None:
                for v in range(g.unroll):
                    block(0, v, waits=(v == 0))
                    if after:
                        after(v)
                rest = g.blocks - g.unroll
                run_blocks(pe, rest, g.unroll, lambda i, v: block(i + 1, v),
                           (lambda t: after(t + g.unroll)) if after else None)
            else:
                run_blocks(pe, g.blocks, g.unroll, block, after)

        def norm_act(act, n, src, off, tile0, ready, split=True):
            ready(act)
            for k in range(DT):
                if n or k >= 2:
                    act.wait_ge(norm_used, DT * n + k - 1)
                nc.scalar.activation(sq[:, k % 2], src[:, tile0 + k, off:off + T], ACT.Square).then_inc(norm_sq, 1)
            act.wait_ge(norm_sum, n + 1)
            nc.scalar.activation(rs[:, :], ps[0][:, 0:T], ACT.Sqrt, scale=1.0 / D, bias=EPS_C).then_inc(norm_std, 1)

        def norm_split_act(act, m, x):
            for k in range(DT):
                act.wait_ge(norm_nx, DT * m + k + 1)
                nc.scalar.activation(x[:, k, 0:T], half[:, k % 2], ACT.Copy).then_inc(norm_hi, 1)

        def norm_pe(pe, n):
            for k in range(DT):
                pe.wait_ge(norm_sq, DT * n + k + 1)
                ins = nc.tensor.matmul(ps[0][:, 0:T], lhsT=const("ones"), rhs=sq[:, k % 2],
                                       start=(k == 0), stop=(k == DT - 1))
                ins.then_inc(norm_used, 1)
            pe.wait_ge(norm_used, DT * (n + 1))
            pe.sem_inc(norm_sum, 1)

        def norm_rs_dve(dve, n):
            dve.wait_ge(norm_std, n + 1)
            dve_link(nc.vector.reciprocal(rs[:, :], rs[:, :]))

        def norm_split_dve(dve, m, x, src, off, tile0, gain, x_tiles):
            for k in range(DT + 1):
                if k < DT:
                    if k >= 2:
                        dve.wait_ge(x_ready, x_tiles + k - 1)
                    nc.vector.scalar_tensor_tensor(out=half[:, k % 2], in0=src[:, tile0 + k, off:off + T],
                                                   scalar=gain(k), in1=rs[:, :], op0=ALU.mult,
                                                   op1=ALU.mult).then_inc(norm_nx, 1)
                if k:
                    dve.wait_ge(norm_hi, DT * m + k)
                    nc.vector.tensor_tensor(x[:, k - 1, T:2 * T], half[:, (k - 1) % 2],
                                            x[:, k - 1, 0:T].bitcast(F32), ALU.subtract).then_inc(x_ready, 1)

        def norm_add_dve(dve, n, added, tile0, gain):
            norm_rs_dve(dve, n)
            for k in range(DT + 1):
                if k < DT:
                    if k >= 2:
                        dve.wait_ge(norm_res, DT * added + k - 1)
                    seq["dve"] += 1
                    nc.vector.scalar_tensor_tensor(out=half[:, k % 2], in0=work[:, tile0 + k, PAD:COLS],
                                                   scalar=gain(k), in1=rs[:, :], op0=ALU.mult,
                                                   op1=ALU.mult).then_inc(dve_seq, 1)
                if k:
                    dve.wait_ge(dve_seq, seq["dve"] - (1 if k < DT else 0))
                    nc.vector.tensor_tensor(resid[:, k - 1], resid[:, k - 1], half[:, (k - 1) % 2],
                                            ALU.add).then_inc(norm_res, 1)

        glu = lambda t: work[:, t:t + 8, PAD:COLS]
        conv_steps = [(c, j) for c in range(8) for j in range(CONV)]

        def conv(dve, lot):
            for c, j in lot:
                acc, x = work[:, TY + c, PAD:COLS], u[:, c, j:j + T]
                if j == 0:
                    ins = nc.vector.tensor_scalar(acc, x, v1("w_dw", c), v1("b_dw", c), ALU.mult, ALU.add)
                else:
                    ins = nc.vector.scalar_tensor_tensor(out=acc, in0=x, scalar=v1("w_dw", 8 * j + c), in1=acc,
                                                         op0=ALU.mult, op1=ALU.add)
                if (c, j) == conv_steps[-1]:
                    ins.then_inc(conv_done, 1)
                else:
                    dve_link(ins)

        def share(m):
            a0 = 12 * m if m < 12 else 144 + 7 * (m - 12)
            return conv_steps[a0:a0 + (12 if m < 12 else 7)]

        diag = lambda x: x[:, 0:3 * P].rearrange("p (b c) -> p b c", c=P)[:, 0:3:2, :]
        both = lambda name: const(name)[:, None, :].to_broadcast([P, 2, P])

        def att_pe(pe, m):
            h = m // 2
            if m % 2 == 0 and h > 0:
                pe.wait_ge(att_a, h)
                if h >= 2:
                    pe.wait_ge(att_lo, h - 1)
                nc.tensor.matmul(ps[3][:, 0:P], lhsT=vt[:, 0], rhs=la[:, 0:P], start=True, stop=True)
                nc.tensor.matmul(ps[3][:, P:T], lhsT=vt[:, 0], rhs=la[:, P:T], start=True, stop=False)
                nc.tensor.matmul(ps[3][:, P:T], lhsT=vt[:, 1], rhs=la[:, T:3 * P], start=False,
                                 stop=True).then_inc(att_o, 1)
            if h >= SB_H:
                return
            if m % 2 == 0:
                q, k, v = (work[:, t + h, PAD:COLS] for t in (TQ, TK, TV))
                if h:
                    pe.wait_ge(att_zs, h)
                    pe.wait_ge(att_vt, h)
                nc.tensor.matmul(ps[0][:, 0:T], lhsT=k[:, 0:P], rhs=q, start=True, stop=True)
                nc.tensor.matmul(ps[0][:, T:3 * P], lhsT=k[:, P:T], rhs=q[:, P:T], start=True,
                                 stop=True).then_inc(att_z, 1)
                nc.tensor.transpose(ps[2][:, 0:P], v[:, 0:P], const("ident"))
                nc.tensor.transpose(ps[2][:, P:T], v[:, P:T], const("ident")).then_inc(att_vp, 1)
            else:
                pe.wait_ge(att_sp, h + 1)
                nc.tensor.matmul(diag(ps[1][:, 0:3 * P]), lhsT=const("upto"), rhs=diag(la), start=True, stop=True)
                nc.tensor.matmul(ps[1][:, P:T], lhsT=const("upto"), rhs=la[:, P:T], start=True, stop=False)
                nc.tensor.matmul(ps[1][:, P:T], lhsT=const("ones"), rhs=la[:, T:3 * P], start=False,
                                 stop=True).then_inc(att_s, 1)

        def att_act(act, m):
            h = m // 2
            if m % 2 == 0 and h > 0:
                act.wait_ge(att_o, h)
                nc.scalar.activation(xb[:, h - 1, 0:T], ps[3][:, 0:T], ACT.Copy).then_inc(att_hi, 1)
            if h >= SB_H:
                return
            if m % 2 == 0:
                act.wait_ge(att_vp, h + 1)
                if h:
                    act.wait_ge(att_o, h)
                nc.scalar.activation(vt[:, :, :], ps[2][:, 0:T].rearrange("p (a b) -> p a b", a=2),
                                     ACT.Copy).then_inc(att_vt, 1)
                act.wait_ge(att_zs, h + 1)
                act_link(nc.scalar.activation(la[:, :], zs[:, :], ACT.Abs))
                act_link(nc.scalar.activation(la[:, :], la[:, :], ACT.Exp, scale=-1.0))
                nc.scalar.activation(la[:, :], la[:, :], ACT.Ln, bias=1.0).then_inc(att_ln, 1)
            else:
                act.wait_ge(att_t, h + 1)
                nc.scalar.activation(la[:, :], zs[:, :], ACT.Exp).then_inc(att_a, 1)

        def att_dve(dve, m):
            h = m // 2
            if m % 2 == 0 and h > 0:
                dve.wait_ge(att_hi, h)
                nc.vector.tensor_tensor(xb[:, h - 1, T:2 * T], ps[3][:, 0:T], xb[:, h - 1, 0:T].bitcast(F32),
                                        ALU.subtract).then_inc(att_lo, 1)
            if h >= SB_H:
                return
            if m % 2 == 0:
                dve.wait_ge(att_z, h + 1)
                if h:
                    dve.wait_ge(att_a, h)
                nc.vector.tensor_scalar(zs[:, :], ps[0][:, 0:3 * P], SB_D ** -0.5, None, ALU.mult).then_inc(att_zs, 1)
                dve.wait_ge(att_ln, h + 1)
                dve_link(nc.vector.scalar_tensor_tensor(out=la[:, :], in0=zs[:, :], scalar=0.0, in1=la[:, :],
                                                        op0=ALU.max, op1=ALU.add))
                nc.vector.tensor_tensor(diag(la), diag(la), both("before"), ALU.mult).then_inc(att_sp, 1)
            else:
                dve.wait_ge(att_s, h + 1)
                dve_link(nc.vector.tensor_tensor(zs[:, :], zs[:, :], ps[1][:, 0:3 * P], ALU.subtract))
                nc.vector.tensor_tensor(diag(zs), diag(zs), both("before_big"), ALU.add).then_inc(att_t, 1)

        CV = D // 2
        conv_y = work[:, TY:TY + 8, PAD:COLS]
        ln_tmp = work[:, 16:24, PAD:COLS]

        def ln_pe(pe, m):
            if m == 0:
                pe.wait_ge(conv_done, 1)
                for c in range(8):
                    ins = nc.tensor.matmul(ps[0][:, 0:T], lhsT=const("ones"), rhs=work[:, TY + c, PAD:COLS],
                                           start=(c == 0), stop=(c == 7))
                ins.then_inc(ln_sum, 1)
            if m == 2:
                pe.wait_ge(ln_sq, 1)
                for c in range(8):
                    ins = nc.tensor.matmul(ps[1][:, 0:T], lhsT=const("ones"), rhs=work[:, 16 + c, PAD:COLS],
                                           start=(c == 0), stop=(c == 7))
                ins.then_inc(ln_var, 1)

        def ln_act(act, m):
            if m == 0:
                act.wait_ge(ln_mid, 1)
                nc.scalar.activation(ln_tmp, conv_y, ACT.Square).then_inc(ln_sq, 1)
            if m == 2:
                act.wait_ge(ln_var, 1)
                nc.scalar.activation(rs[:, :], ps[1][:, 0:T], ACT.Sqrt, scale=1.0 / CV, bias=EPS_C).then_inc(ln_std, 1)
            if m == 3:
                act.wait_ge(ln_y, 1)
                for c in range(8):
                    ins = nc.scalar.activation(work[:, 16 + c, PAD:COLS], work[:, TY + c, PAD:COLS], ACT.Sigmoid,
                                               scale=v1("g_conv_ln", c), bias=v1("b_conv_ln", c))
                ins.then_inc(ln_sig, 1)
            if m == 5:
                act.wait_ge(ln_f, 1)
                nc.scalar.activation(xb[:, 8:16, 0:T], conv_y, ACT.Copy).then_inc(ln_hi, 1)

        def ln_dve(dve, m):
            if m == 0:
                dve.wait_ge(ln_sum, 1)
                nc.vector.scalar_tensor_tensor(out=conv_y, in0=ps[0][:, None, 0:T].to_broadcast([P, 8, T]),
                                               scalar=-1.0 / CV, in1=conv_y, op0=ALU.mult,
                                               op1=ALU.add).then_inc(ln_mid, 1)
            if m == 2:
                dve.wait_ge(ln_std, 1)
                dve_link(nc.vector.reciprocal(rs[:, :], rs[:, :]))
                nc.vector.tensor_tensor(conv_y, conv_y, rs[:, None, :].to_broadcast([P, 8, T]),
                                        ALU.mult).then_inc(ln_y, 1)
            if m == 4:
                dve.wait_ge(ln_sig, 1)
                for c in range(8):
                    ins = nc.vector.tensor_scalar(work[:, TY + c, PAD:COLS], work[:, TY + c, PAD:COLS],
                                                  v1("g_conv_ln", c), v1("b_conv_ln", c), ALU.mult, ALU.add)
                dve_link(ins)
                nc.vector.tensor_tensor(conv_y, conv_y, ln_tmp, ALU.mult).then_inc(ln_f, 1)
            if m == 6:
                dve.wait_ge(ln_hi, 1)
                nc.vector.tensor_tensor(xb[:, 8:16, T:2 * T], conv_y, xb[:, 8:16, 0:T].bitcast(F32),
                                        ALU.subtract).then_inc(x_ready, 16)

        EPS_C = EPS
        const_eps = lambda x: x
        gates = lambda t0: work[:, t0:t0 + DT, PAD:COLS]
        last = lambda g: g.slab((g.blocks - 1) // g.unroll, (g.blocks - 1) % g.unroll, g.groups - 1)[2] + 1 + RING

        def blocks_out(eng, g):
            eng.wait_ge(evacuated, g.b0 + g.blocks + 2)

        def v2(name, i=0):
            c = NV1 + V2[name] + i
            return vec[:, c:c + 1]

        w2in = a["w_in_2"]
        DQ, DK, DV, DZ, RR, RK, RV, RL, RG, GA, GB = 0, 8, 16, 24, 32, 40, 48, 56, 57, 58, 59
        g_dn = Gemm(plan, "dn", w2in, D, 0, 4096, xa, "store", (work, DQ, PAD))
        g_gab = Gemm(plan, "gab", w2in, D, 4096, BW, xa, "store", (work, GA, PAD), apart=DN_H)
        g_rw = Gemm(plan, "rw", w2in, D, 4112, 3328, xa, "store", (work, RR, PAD))
        g_mk = Gemm(plan, "mem_k", a["xa_wk_2"], D, 0, 512, xa, "store", (work, 0, PAD))
        g_mv = Gemm(plan, "mem_v", a["xa_wv_2"], D, 0, 512, xa, "store", (work, 4, PAD))
        g_out = Gemm(plan, "w_out", a["w_out_2"], D, 0, D, xb, "add", (resid, 0, 0))
        g_xq = Gemm(plan, "xa_q", a["xa_wq_2"], D, 0, 512, xa, "store", (work, 8, PAD))
        g_xo = Gemm(plan, "xa_o", a["xa_wo_2"], 512, 0, D, xb, "add", (resid, 0, 0))
        ff2 = []
        for p in range(FF_PIECES):
            ff2 += [Gemm(plan, f"w1_{p}", a["ffn_w1_2"], D, p * D, D, xa, "relu2", (xb, 0, 0)),
                    Gemm(plan, f"w2_{p}", a["ffn_w2_2"], D, 0, D, xb, "add", (resid, 0, 0), k0=p * D)]

        def over(name, shape, region, byte):
            start = {"xa": xa_at, "xb": xb_at, "work": work_at}[region]
            return at(name, shape, F32, start + byte)

        masks = over("masks", [P, LEVELS, P], "work", 60 * COLS * 4)
        dnc = over("dnc", [P, 24, T], "xb", 0)
        dn_rn = over("dn_rn", [P, 2, 2 * T], "xb", 24576)
        slot = lambda name, n: over(name, [P, 8, P], "xb", 4096 * n)
        dn_at_, dn_n, dn_x, dn_xt, dn_nm, dn_tt, dn_e, dn_v = (
            slot(f"dn_{x}", n) for n, x in enumerate(("attn", "n", "x", "xt", "nm", "tt", "e", "v")))
        dn_eq = over("dn_eq", [P, 4, P], "xb", 4096 * 2)
        dn_v0 = over("dn_v0", [P, 4, P], "xb", 4096 * 6)
        dn_s1 = over("dn_s1", [P, 4, P], "xb", 4096 * 6 + 2048)
        dn_v1 = over("dn_v1", [P, 4, P], "xb", 4096 * 5)
        dn_k0 = sq[:, :, :].rearrange("p a (b c) -> p (a b) c", b=2)
        dn_sq = over("dn_sq", [P, 8, T], "xb", 0)
        dn_rr = over("dn_rr", [P, 8, T], "xb", 8192)
        dn_s8 = at("dn_s8", [P, T], F32)
        gt, gc, eg, nbeg = small[:, 0:32], small[:, 32:48], small[:, 48:64], small[:, 64:80]
        ea, rw_mid, fac, omka = small[:, 80:81], small[:, 81:97], small[:, 97:105], small[:, 105:113]
        al = small[0:DN_H, 113:115]
        rw_c = over("rw_c", [P, 16, 132], "work", 0)
        rw_ep = over("rw_ep", [P, 16, 132], "work", 8448)
        rw_em = over("rw_em", [P, 16, 132], "work", 16896)
        rw_nm = over("rw_nm", [P, 8, P], "work", 25344)
        rw_rh = over("rw_rh", [P, 4, RW_D], "work", 29440)
        rw_sa = [over(f"rw_sa{c}", [P, 4, RW_D], "work", 30464 + 1024 * c) for c in range(2)]
        rw_st = over("rw_st", [P, 2, RW_D], "work", 32512)
        rw_bt = over("rw_bt", [P, 8, P], "work", 0)
        rw_kt = over("rw_kt", [P, 8, P], "work", 4096)
        rw_vt = over("rw_vt", [P, 8, 2, P], "work", 8192)
        rw_x = over("rw_x", [P, 8, P], "work", 16384)
        rw_xt = over("rw_xt", [P, 8, P], "work", 20480)
        rw_a = over("rw_a", [P, 8, T], "xa", 0)
        rw_kk = over("rw_kk", [P, 8, T], "xa", 8192)
        rw_mat = {n: over("rw_" + n, [P, 8, P], "xa", 16384 + 4096 * i) for i, n in enumerate(("ba", "ka", "br", "kr"))}
        rw_lw = over("rw_lw", [P, 1024], "xa", 16384)
        rw_g2 = over("rw_g2", [P, 1024], "xa", 20480)
        rw_bn = over("rw_bn", [P, 8, T], "xb", 16384)
        rw_d = over("rw_d", [P, 8, T], "xb", 16384 + 8192)
        rw_tt = over("rw_tt", [P, 8, P], "xb", 16384 + 8192)
        mem = over("mem", [P, DT, T], "work", 16 * COLS * 4)
        xs = over("xs", [P, 8, T], "work", 16 * COLS * 4)
        xp = over("xp", [P, 8, T], "work", 16 * COLS * 4 + 8192)
        xv = over("xv", [P, 4, 2, P], "work", 16 * COLS * 4 + 16384)
        xm = small[:, 120:136]

        inv_pe = [x for l in range(LEVELS) for x in ([f"t{l}", f"u{l}"] if l else ["t0"])]
        inv_dve = ["m0"] + [x for l in range(LEVELS) for x in ([f"m{l + 1}"] if l + 1 < LEVELS else []) + [f"u{l}"]]
        inv_act = [f"t{l}" for l in range(1, LEVELS)]

        def inverse_pe(pe, S, r, nm, x, xt, tt):
            for l in range(LEVELS):
                b = 1 << l
                S.dve.wait(pe, f"m{l}", r)
                if l:
                    S.dve.wait(pe, f"u{l - 1}", r)
                for n in range(8):
                    ins = nc.tensor.matmul(p4[:, n // 4, (n % 4) * P:(n % 4 + 1) * P], lhsT=nm[:, n],
                                           rhs=x[:, n] if l else const("ident"), start=True, stop=True)
                S.pe.done(ins, f"t{l}", r)
                if not l:
                    continue
                S.act.wait(pe, f"t{l}", r)
                for n in range(8):
                    if l + 1 < LEVELS:
                        first = tt[:, n].rearrange("p (g w b) -> p g w b", w=2, b=b)[:, :, 0]
                        nc.tensor.matmul(ps[2][:, n * 64:(n + 1) * 64], lhsT=xt[:, n], rhs=first, start=True, stop=True)
                    second = xt[:, n].rearrange("p (g w b) -> p g w b", w=2, b=b)[:, :, 1]
                    ins = nc.tensor.matmul(ps[3][:, n * 64:(n + 1) * 64], lhsT=tt[:, n], rhs=second, start=True, stop=True)
                S.pe.done(ins, f"u{l}", r)

        def inverse_act(act, S, r, tt):
            for l in range(1, LEVELS):
                S.pe.wait(act, f"t{l}", r)
                if l > 1:
                    S.pe.wait(act, f"u{l - 1}", r)
                S.act.done(nc.scalar.activation(tt[:, :, :], p4[:, 0:2, :].rearrange("p a (b c) -> p (a b) c", b=4),
                                                ACT.Copy), f"t{l}", r)

        def inverse_dve(dve, S, r, n_, nm, x, xt):
            mask = lambda l: masks[:, l, None, :].to_broadcast([P, 8, P])
            eye = const("ident")[:, None, :].to_broadcast([P, 8, P])
            S.dve.done(nc.vector.tensor_tensor(nm[:, :, :], n_[:, :, :], mask(0), ALU.mult), "m0", r)
            S.dve.wait(dve, "m0", r)
            dve_link(nc.vector.tensor_tensor(xt[:, :, :], eye, nm[:, :, :], ALU.subtract))
            for l in range(LEVELS):
                b = 1 << l
                S.pe.wait(dve, f"t{l}", r)
                if l + 1 < LEVELS:
                    S.dve.done(nc.vector.tensor_tensor(nm[:, :, :], n_[:, :, :], mask(l + 1), ALU.mult), f"m{l + 1}", r)
                if not l:
                    S.dve.done(nc.vector.tensor_tensor(x[:, :, :], eye,
                                                       p4[:, 0:2, :].rearrange("p a (b c) -> p (a b) c", b=4),
                                                       ALU.subtract), "u0", r)
                    continue
                S.dve.wait(dve, f"u{l - 1}", r)
                S.pe.wait(dve, f"u{l}", r)
                cut = lambda m, w: m[:, :, :].rearrange("p u (g w b) -> p u g w b", w=2, b=b)[:, :, :, w]
                part = lambda q: q.rearrange("p (u g b) -> p u g b", u=8, b=b)
                if l + 1 < LEVELS:
                    nc.vector.tensor_tensor(cut(x, 0), cut(x, 0), part(ps[2]), ALU.subtract)
                S.dve.done(nc.vector.tensor_tensor(cut(xt, 1), cut(xt, 1), part(ps[3]), ALU.subtract), f"u{l}", r)

        class Trio:

            def __init__(self, name, pe, dve, act):
                self.pe, self.dve, self.act = (Steps(sem(f"{name}_{e}"), x) for e, x in
                                               (("pe", pe), ("dve", dve), ("act", act)))

        dn_acc, dn_sig, dn_silu = sem("dn_acc"), sem("dn_sig"), sem("dn_silu")

        def dn_conv_dve(dve, m):
            if m >= 1:
                pair = slice(2 * (m - 1), 2 * m)
                dve.wait_ge(dn_sig, m)
                if m <= 12:
                    nc.vector.tensor_tensor(work[:, pair, PAD:COLS], work[:, pair, PAD:COLS], dnc[:, pair],
                                            ALU.mult).then_inc(dn_silu, 1)
                else:
                    nc.vector.tensor_tensor(work[:, pair, PAD:COLS], work[:, pair, PAD:COLS],
                                            dnc[:, 2 * (m - 13):2 * (m - 12)], ALU.mult).then_inc(dn_silu, 1)
            if m < 12:
                dve.wait_ge(evacuated, g_dn.b0 + m + 3)
                for j in range(4):
                    for c in (2 * m, 2 * m + 1):
                        x = work[:, c, PAD - 3 + j:PAD - 3 + j + T]
                        if j == 0:
                            ins = nc.vector.tensor_scalar(dnc[:, c], x, v2("dn_conv_w_2", c), None, ALU.mult)
                        else:
                            ins = nc.vector.scalar_tensor_tensor(out=dnc[:, c], in0=x, scalar=v2("dn_conv_w_2", 24 * j + c),
                                                                 in1=dnc[:, c], op0=ALU.mult, op1=ALU.add)
                        if j < 3:
                            seq["dve"] += 1
                            ins.then_inc(dve_seq, 1)
                    if j < 3:
                        dve.wait_ge(dve_seq, seq["dve"])
                ins.then_inc(dn_acc, 1)

        def dn_conv_act(act, m):
            if m < 12:
                act.wait_ge(dn_acc, m + 1)
                pair = slice(2 * m, 2 * m + 2)
                nc.scalar.activation(work[:, pair, PAD:COLS], dnc[:, pair], ACT.Sigmoid).then_inc(dn_sig, 1)
            else:
                act.wait_ge(evacuated, g_dn.b0 + m + 3)
                act.wait_ge(dn_silu, m - 11)
                pair = slice(2 * m, 2 * m + 2)
                nc.scalar.activation(dnc[:, 2 * (m - 12):2 * (m - 11)], work[:, pair, PAD:COLS],
                                     ACT.Sigmoid).then_inc(dn_sig, 1)

        L2 = Trio("l2", ["sum"], ["done"], ["sq", "root"])
        GT = Trio("gates2", ["t", "gc"], ["dt", "soft", "g", "t", "gc", "nbeg"], ["beta", "ln", "ea", "eg"])

        def l2_pe(pe):
            for h in range(DN_H):
                L2.act.wait(pe, "sq", h)
                if h >= 2:
                    L2.act.wait(pe, "root", h - 2)
                L2.pe.done(nc.tensor.matmul(ps[h % 2], lhsT=const("ones"), rhs=sq[:, :, :].rearrange("p a b -> p (a b)"),
                                            start=True, stop=True), "sum", h)

        def l2_act(act):
            act.wait_ge(dn_silu, 16)
            for h in range(DN_H):
                if h:
                    L2.pe.wait(act, "sum", h - 1)
                L2.act.done(nc.scalar.activation(sq[:, :, :], work[:, DQ + h:DQ + h + 9:8, PAD:COLS], ACT.Square), "sq", h)
                L2.pe.wait(act, "sum", h)
                if h >= 2:
                    L2.dve.wait(act, "done", h - 2)
                L2.act.done(nc.scalar.activation(dn_rn[:, h % 2], ps[h % 2], ACT.Sqrt, bias=EPS_C), "root", h)

        def l2_dve(dve):
            for h in range(DN_H):
                L2.act.wait(dve, "root", h)
                dve_link(nc.vector.reciprocal(dn_rn[:, h % 2], dn_rn[:, h % 2]))
                q, k = (work[:, t + h, PAD:COLS] for t in (DQ, DK))
                nc.vector.scalar_tensor_tensor(out=q, in0=q, scalar=128 ** -0.5, in1=dn_rn[:, h % 2, 0:T],
                                               op0=ALU.mult, op1=ALU.mult)
                L2.dve.done(nc.vector.tensor_tensor(k, k, dn_rn[:, h % 2, T:2 * T], ALU.mult), "done", h)

        ga, gb, s8 = work[0:DN_H, GA, PAD:COLS], work[0:DN_H, GB, PAD:COLS], dn_s8[0:DN_H, :]

        def gates_act(act):
            blocks_out(act, g_gab)
            GT.act.done(nc.scalar.activation(gb, gb, ACT.Sigmoid), "beta")
            GT.dve.wait(act, "dt")
            act_link(nc.scalar.activation(s8, ga, ACT.Abs))
            act_link(nc.scalar.activation(s8, s8, ACT.Exp, scale=-1.0))
            GT.act.done(nc.scalar.activation(s8, s8, ACT.Ln, bias=1.0), "ln")
            GT.act.done(nc.scalar.activation(ea[0:DN_H, :], al[:, 0:1], ACT.Exp), "ea")
            GT.pe.wait(act, "gc")
            GT.act.done(nc.scalar.activation(eg, ps[3][:, 0:16], ACT.Exp), "eg")

        def gates_dve(dve):
            blocks_out(dve, g_gab)
            GT.dve.done(nc.vector.tensor_scalar(ga, ga, al[:, 1:2], None, ALU.add), "dt")
            GT.act.wait(dve, "ln")
            GT.dve.done(nc.vector.scalar_tensor_tensor(out=s8, in0=ga, scalar=0.0, in1=s8, op0=ALU.max, op1=ALU.add), "soft")
            GT.dve.wait(dve, "soft")
            GT.act.wait(dve, "ea")
            GT.dve.done(nc.vector.tensor_scalar(s8, s8, ea[0:DN_H, :], -1.0, ALU.mult, ALU.mult), "g")
            GT.pe.wait(dve, "t")
            GT.dve.done(nc.vector.tensor_copy(gt, ps[2][:, 0:32]), "t")
            GT.pe.wait(dve, "gc")
            GT.act.wait(dve, "eg")
            GT.dve.done(nc.vector.tensor_copy(gc, ps[3][:, 0:16]), "gc")
            GT.dve.wait(dve, "gc")
            GT.dve.done(nc.vector.scalar_tensor_tensor(out=nbeg, in0=gt[:, 16:32], scalar=-1.0, in1=eg, op0=ALU.mult,
                                                       op1=ALU.mult), "nbeg")

        def gates_pe(pe):
            GT.dve.wait(pe, "g")
            GT.act.wait(pe, "beta")
            for c in range(2):
                for n, x in enumerate((s8, gb)):
                    ins = nc.tensor.transpose(ps[2][:, 16 * n + 8 * c:16 * n + 8 * c + 8], x[:, c * P:(c + 1) * P],
                                              const("ident")[0:DN_H, 0:DN_H])
            GT.pe.done(ins, "t")
            GT.dve.wait(pe, "t")
            GT.pe.done(nc.tensor.matmul(ps[3][:, 0:16], lhsT=const("incl"), rhs=gt[:, 0:16], start=True, stop=True), "gc")

        DN = Trio("dn",
                  ["row", "kk", "kq", "v", "k"] + inv_pe + ["v0", "s1", "m1", "v1", "o"],
                  ["min", "mask", "n", "n2", "attn", "qg"] + inv_dve + ["rhs1", "o"],
                  ["e", "eq", "v", "k"] + inv_act + ["v0", "s1", "v1"])
        quad = lambda n: p4[:, n:n + 2, :].rearrange("p a (b c) -> p (a b) c", b=4)
        units = [(hh, c) for hh in range(4) for c in range(2)]

        def chunk(tile, c):
            return work[:, tile, PAD + c * P:PAD + (c + 1) * P]

        def dn_pe(pe, r):
            H = 4 * r
            q2 = lambda base, n: p4[:, base + n // 4, (n % 4) * P:(n % 4 + 1) * P]
            if r:
                DN.dve.wait(pe, "o", r - 1)
            for n, (hh, c) in enumerate(units):
                col = gt[:, 8 * c + H + hh:8 * c + H + hh + 1]
                nc.tensor.matmul(q2(0, n), lhsT=col.to_broadcast([P, P]), rhs=const("incl"), start=True, stop=True)
            for n, (hh, c) in enumerate(units):
                col = gt[:, 16 + 8 * c + H + hh:16 + 8 * c + H + hh + 1]
                ins = nc.tensor.matmul(q2(2, n), lhsT=col.to_broadcast([P, P]), rhs=const("ident"), start=True, stop=True)
            DN.pe.done(ins, "row", r)
            DN.dve.wait(pe, "min", r)
            DN.act.wait(pe, "eq", r)
            for n, (hh, c) in enumerate(units):
                k = chunk(DK + H + hh, c)
                ins = nc.tensor.matmul(q2(0, n), lhsT=k, rhs=k, start=True, stop=True)
            DN.pe.done(ins, "kk", r)
            DN.dve.wait(pe, "n", r)
            for n, (hh, c) in enumerate(units):
                ins = nc.tensor.matmul(q2(0, n), lhsT=chunk(DK + H + hh, c), rhs=chunk(DQ + H + hh, c), start=True, stop=True)
            DN.pe.done(ins, "kq", r)
            DN.dve.wait(pe, "n2", r)
            for n, (hh, c) in enumerate(units):
                ins = nc.tensor.transpose(q2(2, n), chunk(DV + H + hh, c), const("ident"))
            DN.pe.done(ins, "v", r)
            DN.dve.wait(pe, "attn", r)
            for hh in range(4):
                ins = nc.tensor.transpose(q2(0, hh), chunk(DK + H + hh, 0), const("ident"))
            DN.pe.done(ins, "k", r)
            DN.act.wait(pe, "k", r)
            inverse_pe(pe, DN, r, dn_nm, dn_x, dn_xt, dn_tt)
            DN.dve.wait(pe, f"u{LEVELS - 1}", r)
            for hh in range(4):
                ins = nc.tensor.matmul(q2(0, hh), lhsT=dn_xt[:, 2 * hh], rhs=dn_v[:, 2 * hh], start=True, stop=True)
            DN.pe.done(ins, "v0", r)
            DN.act.wait(pe, "v0", r)
            for hh in range(4):
                ins = nc.tensor.matmul(q2(1, hh), lhsT=dn_k0[:, hh], rhs=dn_v0[:, hh], start=True, stop=True)
            DN.pe.done(ins, "s1", r)
            DN.act.wait(pe, "s1", r)
            for hh in range(4):
                ins = nc.tensor.matmul(q2(2, hh), lhsT=chunk(DK + H + hh, 1), rhs=dn_s1[:, hh], start=True, stop=True)
            DN.pe.done(ins, "m1", r)
            DN.dve.wait(pe, "rhs1", r)
            for hh in range(4):
                ins = nc.tensor.matmul(q2(3, hh), lhsT=dn_xt[:, 2 * hh + 1], rhs=dn_v[:, 2 * hh + 1], start=True, stop=True)
            DN.pe.done(ins, "v1", r)
            DN.act.wait(pe, "v1", r)
            for hh in range(4):
                o = lambda c: p4[:, hh // 2, (hh % 2) * T + c * P:(hh % 2) * T + (c + 1) * P]
                nc.tensor.matmul(o(0), lhsT=dn_v0[:, hh], rhs=dn_at_[:, 2 * hh], start=True, stop=True)
                nc.tensor.matmul(o(1), lhsT=dn_s1[:, hh], rhs=chunk(DQ + H + hh, 1), start=True, stop=False)
                ins = nc.tensor.matmul(o(1), lhsT=dn_v1[:, hh], rhs=dn_at_[:, 2 * hh + 1], start=False, stop=True)
            DN.pe.done(ins, "o", r)

        def dn_act(act, r):
            H = 4 * r
            DN.dve.wait(act, "min", r)
            DN.act.done(nc.scalar.activation(dn_e[:, :, :], dn_e[:, :, :], ACT.Exp), "e", r)
            DN.act.done(nc.scalar.activation(dn_eq[:, :, :], quad(0)[:, 1:8:2, :], ACT.Exp), "eq", r)
            DN.pe.wait(act, "v", r)
            for n, (hh, c) in enumerate(units):
                beta = gt[:, 16 + 8 * c + H + hh:16 + 8 * c + H + hh + 1]
                ins = nc.scalar.activation(dn_v[:, n], quad(2)[:, n], ACT.Copy, scale=beta)
            DN.act.done(ins, "v", r)
            DN.pe.wait(act, "k", r)
            for hh in range(4):
                ins = nc.scalar.activation(dn_k0[:, hh], quad(0)[:, hh], ACT.Copy, scale=dn_e[:, 2 * hh, P - 1:P])
            DN.act.done(ins, "k", r)
            inverse_act(act, DN, r, dn_tt)
            four = lambda n: ps[n].rearrange("p (b c) -> p b c", b=4)
            for name, bank, to in (("v0", 0, dn_v0), ("s1", 1, dn_s1), ("v1", 3, dn_v1)):
                DN.pe.wait(act, name, r)
                DN.act.done(nc.scalar.activation(to[:, :, :], four(bank), ACT.Copy), name, r)

        def dn_dve(dve, r):
            H = 4 * r
            DN.pe.wait(dve, "row", r)
            for n, (hh, c) in enumerate(units):
                col = gc[:, 8 * c + H + hh:8 * c + H + hh + 1]
                ins = nc.vector.tensor_scalar(dn_e[:, n], quad(0)[:, n], col, 0.0, ALU.subtract, ALU.min)
            DN.dve.done(ins, "min", r)
            DN.act.wait(dve, "e", r)
            DN.dve.done(nc.vector.tensor_tensor(dn_e[:, :, :], dn_e[:, :, :],
                                                const("incl")[:, None, :].to_broadcast([P, 8, P]), ALU.mult), "mask", r)
            DN.dve.wait(dve, "mask", r)
            DN.pe.wait(dve, "kk", r)
            DN.dve.done(nc.vector.tensor_tensor(dn_n[:, :, :], quad(0), dn_e[:, :, :], ALU.mult), "n", r)
            DN.dve.wait(dve, "n", r)
            DN.dve.done(nc.vector.tensor_tensor(dn_n[:, :, :], dn_n[:, :, :], quad(2), ALU.mult), "n2", r)
            DN.pe.wait(dve, "kq", r)
            DN.dve.done(nc.vector.tensor_tensor(dn_at_[:, :, :], quad(0), dn_e[:, :, :], ALU.mult), "attn", r)
            DN.act.wait(dve, "eq", r)
            q1 = work[:, DQ + H:DQ + H + 4, PAD + P:COLS]
            DN.dve.done(nc.vector.tensor_tensor(q1, q1, dn_eq[:, :, :], ALU.mult), "qg", r)
            DN.dve.wait(dve, "qg", r)
            inverse_dve(dve, DN, r, dn_n, dn_nm, dn_x, dn_xt)
            DN.pe.wait(dve, "m1", r)
            for hh in range(4):
                ins = nc.vector.scalar_tensor_tensor(out=dn_v[:, 2 * hh + 1], in0=quad(2)[:, hh],
                                                     scalar=nbeg[:, 8 + H + hh:8 + H + hh + 1], in1=dn_v[:, 2 * hh + 1],
                                                     op0=ALU.mult, op1=ALU.add)
            DN.dve.done(ins, "rhs1", r)
            DN.pe.wait(dve, "o", r)
            DN.dve.done(nc.vector.tensor_copy(work[:, DQ + H:DQ + H + 4, PAD:COLS],
                                              p4[:, 0:2, :].rearrange("p a (b c) -> p (a b) c", b=2)), "o", r)

        DF = Trio("dnf", ["sum"], ["rr", "o1", "o2", "lo"], ["sq", "root", "hi"])
        all4 = p4[:, :, :].rearrange("p a (b c) -> p (a b) c", b=2)
        dn_o = work[:, DQ:DQ + 8, PAD:COLS]

        def eight(ones, src):
            for j in range(8):
                ins = nc.tensor.matmul(all4[:, j], lhsT=const(ones), rhs=src[:, j], start=True, stop=True)
            return ins

        def dnf_pe(pe):
            DF.act.wait(pe, "sq")
            DF.pe.done(eight("ones", dn_sq), "sum")

        def dnf_act(act):
            DN.dve.wait(act, "o", 1)
            DF.act.done(nc.scalar.activation(dn_sq[:, :, :], dn_o, ACT.Square), "sq")
            DF.pe.wait(act, "sum")
            DF.act.done(nc.scalar.activation(dn_rr[:, :, :], all4, ACT.Sqrt, scale=1.0 / 128, bias=EPS_C), "root")
            DF.dve.wait(act, "o2")
            DF.act.done(nc.scalar.activation(xb[:, 0:8, 0:T], dn_o, ACT.Copy), "hi")

        def dnf_dve(dve):
            DF.act.wait(dve, "root")
            DF.dve.done(nc.vector.reciprocal(dn_rr[:, :, :], dn_rr[:, :, :]), "rr")
            DF.dve.wait(dve, "rr")
            DN.dve.wait(dve, "o", 1)
            DF.dve.done(nc.vector.scalar_tensor_tensor(out=dn_o, in0=dn_o, scalar=v2("dn_norm_w_2"), in1=dn_rr[:, :, :],
                                                       op0=ALU.mult, op1=ALU.mult), "o1")
            DF.dve.wait(dve, "o1")
            DF.dve.done(nc.vector.tensor_tensor(dn_o, dn_o, work[:, DZ:DZ + 8, PAD:COLS], ALU.mult), "o2")
            DF.act.wait(dve, "hi")
            DF.dve.done(nc.vector.tensor_tensor(xb[:, 0:8, T:2 * T], dn_o, xb[:, 0:8, 0:T].bitcast(F32), ALU.subtract), "lo")

        lots = [(RR, 8), (RK, 8), (RV, 8), (RL, 2)]
        rw_r, rw_k, rw_v = (work[:, t:t + 8, PAD:COLS] for t in (RR, RK, RV))
        RP = Trio("rwp", ["w", "a", "kk", "bonus", "t0", "t1", "t2", "t3"],
                  ["shift", "lora", "scan", "kkr", "kk", "k", "bonus", "bn", "sc", "rho", "alpha", "beta", "kappa", "t1", "t3"],
                  ["tanh", "w", "a", "sq", "root", "ep", "em", "t0", "t2"])
        lora_in = sem("lora_in")
        rw_big = [(0, 63)]
        C = lambda x, a_, b_: x[:, :, a_:b_]
        ctok = lambda x, a_: x[:, :, a_:a_ + P].rearrange("p (j c) t -> p j c t", c=2)
        jc = lambda x: x.rearrange("p j (c t) -> p j c t", c=2)

        def rwp_pe(pe):
            pe.wait_ge(lora_in, 16 * 2)
            RP.act.wait(pe, "tanh")
            for j in range(8):
                ins = nc.tensor.matmul(all4[:, j], lhsT=rw_lw[0:64, j * P:(j + 1) * P],
                                       rhs=work[0:64, RL, PAD:COLS], start=True, stop=True)
            RP.pe.done(ins, "w")
            RP.act.wait(pe, "w")
            for j in range(8):
                ins = nc.tensor.matmul(all4[:, j], lhsT=rw_lw[64:P, j * P:(j + 1) * P],
                                       rhs=work[64:P, RL, PAD:COLS], start=True, stop=True)
            RP.pe.done(ins, "a")
            RP.act.wait(pe, "sq")
            RP.pe.done(eight("ones_head", rw_d), "kk")
            RP.dve.wait(pe, "bonus")
            RP.act.wait(pe, "root")
            RP.pe.done(eight("ones_head", rw_d), "bonus")
            RP.dve.wait(pe, "beta")
            RP.dve.wait(pe, "kappa")
            for n, src in enumerate((rw_a, work[:, RK:RK + 8, PAD:COLS])):
                for j in range(8):
                    ins = nc.tensor.transpose(p4[:, 2 * n + j // 4, (j % 4) * P:(j % 4 + 1) * P], src[:, j, 0:P],
                                              const("ident"))
                RP.pe.done(ins, f"t{n}")
            for n in range(2):
                if n == 0:
                    RP.act.wait(pe, "t0")
                else:
                    RP.dve.wait(pe, "t1")
                for j in range(8):
                    ins = nc.tensor.transpose(p4[:, 2 * n + j // 4, (j % 4) * P:(j % 4 + 1) * P],
                                              chunk(RV + 4 * n + j // 2, j % 2), const("ident"))
                RP.pe.done(ins, f"t{2 + n}")

        def rwp_act(act):
            RP.dve.wait(act, "lora")
            act_link(nc.scalar.activation(work[0:64, RL, PAD:COLS], work[0:64, RL, PAD:COLS], ACT.Tanh))
            RP.act.done(nc.scalar.activation(work[:, RG, PAD:COLS], work[:, RG, PAD:COLS], ACT.Sigmoid), "tanh")
            RP.pe.wait(act, "w")
            for j in range(8):
                ins = nc.scalar.activation(rw_c[:, 2 * j:2 * j + 2, 4:132], all4[:, j].rearrange("p (c t) -> p c t", c=2),
                                           ACT.Sigmoid, bias=v2("rw_w0_2", j))
            RP.act.done(ins, "w")
            RP.pe.wait(act, "a")
            for j in range(8):
                ins = nc.scalar.activation(rw_a[:, j], all4[:, j], ACT.Sigmoid, bias=v2("rw_a0_2", j))
            RP.act.done(ins, "a")
            RP.dve.wait(act, "kkr")
            RP.act.done(nc.scalar.activation(rw_d[:, :, :], rw_kk[:, :, :], ACT.Square), "sq")
            RP.pe.wait(act, "kk")
            RP.act.done(nc.scalar.activation(rw_ep_flat, all4, ACT.Sqrt), "root")
            RP.dve.wait(act, "sc")
            RP.act.done(nc.scalar.activation(C(rw_ep, 3, 132), C(rw_c, 3, 132), ACT.Exp, scale=-RW_DECAY), "ep")
            RP.act.done(nc.scalar.activation(C(rw_em, 3, 132), C(rw_c, 3, 132), ACT.Exp, scale=RW_DECAY), "em")
            RP.pe.wait(act, "t0")
            RP.dve.wait(act, "kappa")
            RP.act.done(nc.scalar.activation(rw_bt[:, :, :], quad(0), ACT.Copy), "t0")
            RP.pe.wait(act, "t2")
            RP.act.done(nc.scalar.activation(rw_vt[:, 0:4].rearrange("p j c t -> p (j c) t"), quad(0), ACT.Copy), "t2")

        rw_ep_flat = over("rw_root", [P, 8, T], "work", 8448)[:, :, :]

        def rwp_dve(dve):
            blocks_out(dve, g_rw)
            for i, (t0, n) in enumerate(lots):
                if i:
                    dve.wait_ge(dve_seq, seq["dve"])
                now, before = work[:, t0:t0 + n, PAD:COLS], work[:, t0:t0 + n, PAD - 1:COLS - 1]
                dve_link(nc.vector.tensor_tensor(rw_d[:, 0:n], before, now, ALU.subtract))
                for j in range(n):
                    x = work[:, t0 + j, PAD:COLS]
                    ins = nc.vector.scalar_tensor_tensor(out=x, in0=rw_d[:, j], scalar=v2("rw_mu_2", t0 - RR + j), in1=x,
                                                         op0=ALU.mult, op1=ALU.add)
                if i < 3:
                    seq["dve"] += 1
                    ins.then_inc(dve_seq, 1)
            RP.dve.done(ins, "shift")
            RP.dve.done(nc.vector.memset(rw_c[:, :, 3:4], 0.0), "lora")
            RP.dve.wait(dve, "lora")
            RP.act.wait(dve, "w")
            for c in range(16):
                ins = nc.vector.tensor_tensor_scan(rw_c[:, c, 4:132], const("ones"), rw_c[:, c, 4:132], 0.0, ALU.mult,
                                                   ALU.add)
            RP.dve.done(ins, "scan")
            for j in range(8):
                ins = nc.vector.tensor_scalar(rw_kk[:, j], work[:, RK + j, PAD:COLS], v2("rw_k_k_2", j), None, ALU.mult)
            RP.dve.done(ins, "kkr")
            RP.act.wait(dve, "root")
            dve_link(nc.vector.tensor_scalar(rw_ep_flat, rw_ep_flat, 1e-12, None, ALU.max))
            dve_link(nc.vector.reciprocal(rw_ep_flat, rw_ep_flat))
            RP.dve.wait(dve, "kkr")
            RP.dve.done(nc.vector.tensor_tensor(rw_kk[:, :, :], rw_kk[:, :, :], rw_ep_flat, ALU.mult), "kk")
            RP.act.wait(dve, "a")
            dve_link(nc.vector.tensor_scalar(omka, vec[:, NV1 + V2["rw_k_a_2"]:NV1 + V2["rw_k_a_2"] + 8], -1.0, 1.0,
                                             ALU.mult, ALU.add))
            for j in range(8):
                ins = nc.vector.tensor_scalar(rw_d[:, j], rw_a[:, j], v2("rw_k_a_2", j), omka[:, j:j + 1], ALU.mult,
                                              ALU.add)
            dve_link(ins)
            RP.dve.done(nc.vector.tensor_tensor(rw_k, rw_k, rw_d[:, :, :], ALU.mult), "k")
            RP.dve.wait(dve, "k")
            for j in range(8):
                ins = nc.vector.scalar_tensor_tensor(out=rw_d[:, j], in0=work[:, RR + j, PAD:COLS],
                                                     scalar=v2("rw_r_k_2", j), in1=work[:, RK + j, PAD:COLS],
                                                     op0=ALU.mult, op1=ALU.mult)
            RP.dve.done(ins, "bonus")
            RP.pe.wait(dve, "bonus")
            RP.dve.done(nc.vector.tensor_tensor(rw_bn[:, :, :], all4, rw_v, ALU.mult), "bn")
            RP.dve.wait(dve, "scan")
            dve_link(nc.vector.tensor_copy(rw_mid, rw_c[:, :, 67]))
            RP.dve.wait(dve, "kk")
            RP.dve.done(nc.vector.tensor_tensor(C(rw_c, 3, 132), C(rw_c, 3, 132),
                                                rw_mid[:, :, None].to_broadcast([P, 16, 129]), ALU.subtract), "sc")
            RP.act.wait(dve, "ep")
            RP.dve.done(nc.vector.tensor_tensor(jc(rw_r), jc(rw_r), ctok(rw_ep, 4), ALU.mult), "rho")
            dve_link(nc.vector.tensor_tensor(rw_a[:, :, :], rw_a[:, :, :], rw_kk[:, :, :], ALU.mult))
            RP.dve.done(nc.vector.tensor_tensor(jc(rw_kk[:, :, :]), jc(rw_kk[:, :, :]), ctok(rw_ep, 3), ALU.mult), "alpha")
            RP.act.wait(dve, "em")
            RP.dve.done(nc.vector.tensor_tensor(jc(rw_a[:, :, :]), jc(rw_a[:, :, :]), ctok(rw_em, 4), ALU.mult), "beta")
            dve_link(nc.vector.tensor_tensor(fac, rw_ep[:, 0:16:2, 131], rw_em[:, 1:16:2, 3], ALU.mult))
            RP.dve.done(nc.vector.tensor_tensor(jc(rw_k), jc(rw_k), ctok(rw_em, 4), ALU.mult), "kappa")
            RP.dve.wait(dve, "kappa")
            RP.pe.wait(dve, "t1")
            RP.dve.done(nc.vector.tensor_copy(rw_kt[:, :, :], quad(2)), "t1")
            RP.pe.wait(dve, "t3")
            RP.dve.done(nc.vector.tensor_copy(rw_vt[:, 4:8].rearrange("p j c t -> p (j c) t"), quad(2)), "t3")

        MATS = [("ba", rw_a, rw_kk), ("ka", work[:, RK:RK + 8, PAD:COLS], rw_kk), ("br", rw_a, work[:, RR:RR + 8, PAD:COLS]),
                ("kr", work[:, RK:RK + 8, PAD:COLS], work[:, RR:RR + 8, PAD:COLS])]
        RW = Trio("rw", ["ba", "ka", "br", "kr"] + inv_pe + ["r0", "sa0", "st", "r1", "sa1", "y"],
                  ["ka", "kr"] + inv_dve + ["y"],
                  ["ba", "br"] + inv_act + ["r0", "sa0", "st", "r1", "sa1"])

        unit = lambda hh, c: 4 * (hh % 2) + 2 * (hh // 2) + c
        head = lambda hh: 2 * (hh % 2) + hh // 2

        def rw_pe(pe, r):
            if r:
                RW.dve.wait(pe, "y", r - 1)
            for i, (name, left, right) in enumerate(MATS):
                if name == "br":
                    RW.act.wait(pe, "ba", r)
                if name == "kr":
                    RW.dve.wait(pe, "ka", r)
                base = 2 * (i % 2)
                for hh, c in units:
                    n, j, hb = unit(hh, c), 2 * r + hh // 2, 64 * (hh % 2)
                    L, R = left[hb:hb + 64, j, c * P:(c + 1) * P], right[hb:hb + 64, j, c * P:(c + 1) * P]
                    bank, o = base + n // 4, (n % 4) * P
                    nc.tensor.matmul(p4[0:64, bank, o:o + P], lhsT=L[:, 0:64], rhs=R, start=True, stop=True)
                    ins = nc.tensor.matmul(p4[64:P, bank, o + 64:o + P], lhsT=L[:, 64:P], rhs=R[:, 64:P], start=True,
                                           stop=True)
                RW.pe.done(ins, name, r)
            RW.act.wait(pe, "br", r)
            inverse_pe(pe, RW, r, rw_nm, rw_x, rw_xt, rw_tt)
            RW.dve.wait(pe, f"u{LEVELS - 1}", r)
            ka, br, kr = rw_mat["ka"], rw_mat["br"], rw_mat["kr"]
            place = lambda hh: (2 * r + hh // 2, 64 * (hh % 2))
            vtok = lambda hh, c: rw_vt[:, 2 * r + hh // 2, c, 64 * (hh % 2):64 * (hh % 2) + 64]
            for hh in range(4):
                ins = nc.tensor.matmul(ps[2 * (hh % 2)][:, (hh // 2) * 64:(hh // 2 + 1) * 64], lhsT=ka[:, unit(hh, 0)], rhs=vtok(hh, 0), start=True,
                                       stop=True)
            RW.pe.done(ins, "r0", r)
            RW.act.wait(pe, "r0", r)
            for hh in range(4):
                ins = nc.tensor.matmul(ps[1][:, hh * 64:(hh + 1) * 64], lhsT=rw_xt[:, unit(hh, 0)], rhs=rw_rh[:, head(hh)], start=True,
                                       stop=True)
            RW.pe.done(ins, "sa0", r)
            RW.act.wait(pe, "sa0", r)
            for hh in range(4):
                j, hb = place(hh)
                o = ps[2][hb:hb + 64, (hh // 2) * 64:(hh // 2) * 64 + 64]
                nc.tensor.matmul(o, lhsT=rw_bt[:, j, hb:hb + 64], rhs=rw_sa[0][:, hh], start=True, stop=False)
                ins = nc.tensor.matmul(o, lhsT=rw_kt[:, j, hb:hb + 64], rhs=vtok(hh, 0), start=False, stop=True)
            RW.pe.done(ins, "st", r)
            RW.act.wait(pe, "st", r)
            for hh in range(4):
                j, hb = place(hh)
                o = ps[2 * (hh % 2)][:, (hh // 2) * 64:(hh // 2 + 1) * 64]
                nc.tensor.matmul(o, lhsT=rw_kk[hb:hb + 64, j, P:T], rhs=rw_st[hb:hb + 64, hh // 2], start=True, stop=False)
                ins = nc.tensor.matmul(o, lhsT=ka[:, unit(hh, 1)], rhs=vtok(hh, 1), start=False, stop=True)
            RW.pe.done(ins, "r1", r)
            RW.act.wait(pe, "r1", r)
            for hh in range(4):
                ins = nc.tensor.matmul(ps[1][:, hh * 64:(hh + 1) * 64], lhsT=rw_xt[:, unit(hh, 1)], rhs=rw_rh[:, head(hh)],
                                       start=True, stop=True)
            RW.pe.done(ins, "sa1", r)
            RW.act.wait(pe, "sa1", r)
            for hh in range(4):
                j, hb = place(hh)
                for c in range(2):
                    o = ps[3][hb:hb + 64, (hh // 2) * T + c * P:(hh // 2) * T + (c + 1) * P]
                    if c:
                        nc.tensor.matmul(o, lhsT=rw_st[hb:hb + 64, hh // 2],
                                         rhs=work[hb:hb + 64, RR + j, PAD + P:COLS], start=True, stop=False)
                    nc.tensor.matmul(o, lhsT=rw_sa[c][:, hh], rhs=br[:, unit(hh, c)], start=(c == 0), stop=False)
                    ins = nc.tensor.matmul(o, lhsT=vtok(hh, c), rhs=kr[:, unit(hh, c)], start=False, stop=True)
            RW.pe.done(ins, "y", r)

        def quarter(eng_op, name, base, mask):
            m, q = rw_mat[name], quad(base)
            a1 = eng_op(m[0:64, :, :], q[0:64], mask, slice(0, 64), slice(0, P))
            return eng_op(m[64:P, :, 64:P], q[64:P, :, 64:P], mask, slice(64, P), slice(64, P))

        def rw_act(act, r):
            copy = lambda o, i, *_: nc.scalar.activation(o, i, ACT.Copy)
            RW.pe.wait(act, "ba", r)
            RW.act.done(quarter(copy, "ba", 0, None), "ba", r)
            RW.pe.wait(act, "br", r)
            RW.act.done(quarter(copy, "br", 0, None), "br", r)
            inverse_act(act, RW, r, rw_tt)
            four = lambda n: ps[n][:, 0:T].rearrange("p (b c) -> p b c", b=4)
            for name, bank, to, scale in (("r0", 0, rw_rh, -1.0), ("sa0", 1, rw_sa[0], 1.0), ("st", 2, rw_st, None),
                                          ("r1", 0, rw_rh, -1.0), ("sa1", 1, rw_sa[1], 1.0)):
                RW.pe.wait(act, name, r)
                if name == "st":
                    for j in range(2):
                        ins = nc.scalar.activation(rw_st[:, j], ps[2][:, 64 * j:64 * j + 64], ACT.Copy,
                                                   scale=fac[:, 2 * r + j:2 * r + j + 1])
                elif scale < 0:
                    ins = nc.scalar.activation(to[:, :, :].rearrange("p (a b) c -> p a b c", a=2),
                                               p4[:, 0:4:2, 0:P].rearrange("p a (b c) -> p a b c", b=2), ACT.Copy, scale=scale)
                else:
                    ins = nc.scalar.activation(to[:, :, :], four(bank), ACT.Copy)
                RW.act.done(ins, name, r)

        def rw_dve(dve, r):
            if not r:
                for m in rw_mat.values():
                    ins = nc.vector.memset(m[64:P, :, 0:64], 0.0)
                dve_link(ins)
            masked = lambda name: (lambda o, i, mask, p_, c_: nc.vector.tensor_tensor(
                o, i, const(name)[p_, None, c_].to_broadcast([64, 8, c_.stop - c_.start]), ALU.mult))
            RW.pe.wait(dve, "ka", r)
            RW.dve.done(quarter(masked("before"), "ka", 2, None), "ka", r)
            RW.pe.wait(dve, "kr", r)
            RW.dve.done(quarter(masked("incl"), "kr", 2, None), "kr", r)
            RW.act.wait(dve, "br", r)
            br = rw_mat["br"]
            dve_link(nc.vector.tensor_tensor(br[:, :, :], br[:, :, :], const("incl")[:, None, :].to_broadcast([P, 8, P]),
                                             ALU.mult))
            inverse_dve(dve, RW, r, rw_mat["ba"], rw_nm, rw_x, rw_xt)
            RW.pe.wait(dve, "y", r)
            RW.dve.done(nc.vector.tensor_copy(work[:, RR + 2 * r:RR + 2 * r + 2, PAD:COLS],
                                              ps[3].rearrange("p (j t) -> p j t", j=2)), "y", r)

        RN = Trio("rwn", ["mean", "var", "gate"], ["mid", "rr", "y1", "y2", "y3", "y4", "lo"], ["sq", "root", "hi"])

        def rwn_pe(pe):
            RW.dve.wait(pe, "y", 3)
            RN.pe.done(eight("ones_head", rw_r), "mean")
            RN.act.wait(pe, "sq")
            RN.pe.done(eight("ones_head", rw_d), "var")
            RN.act.wait(pe, "root")
            pe.wait_ge(lora_in, 16 * 3)
            for j in range(8):
                ins = nc.tensor.matmul(all4[:, j], lhsT=rw_g2[:, j * P:(j + 1) * P], rhs=work[:, RG, PAD:COLS], start=True,
                                       stop=True)
            RN.pe.done(ins, "gate")

        def rwn_act(act):
            RN.dve.wait(act, "mid")
            RN.act.done(nc.scalar.activation(rw_d[:, :, :], rw_r, ACT.Square), "sq")
            RN.pe.wait(act, "var")
            RN.act.done(nc.scalar.activation(rw_a[:, :, :], all4, ACT.Sqrt, scale=1.0 / RW_D, bias=const_eps(64e-5)), "root")
            RN.dve.wait(act, "y4")
            RN.act.done(nc.scalar.activation(xb[:, 8:16, 0:T], rw_r, ACT.Copy), "hi")

        def rwn_dve(dve):
            RN.pe.wait(dve, "mean")
            RN.dve.done(nc.vector.scalar_tensor_tensor(out=rw_r, in0=all4, scalar=-1.0 / RW_D, in1=rw_r, op0=ALU.mult,
                                                       op1=ALU.add), "mid")
            RN.act.wait(dve, "root")
            RN.dve.done(nc.vector.reciprocal(rw_a[:, :, :], rw_a[:, :, :]), "rr")
            RN.dve.wait(dve, "rr")
            RN.dve.done(nc.vector.tensor_tensor(rw_r, rw_r, rw_a[:, :, :], ALU.mult), "y1")
            RN.dve.wait(dve, "y1")
            for j in range(8):
                y = work[:, RR + j, PAD:COLS]
                ins = nc.vector.tensor_scalar(y, y, v2("rw_ln_w_2", j), v2("rw_ln_b_2", j), ALU.mult, ALU.add)
            RN.dve.done(ins, "y2")
            RN.dve.wait(dve, "y2")
            RN.dve.done(nc.vector.tensor_tensor(rw_r, rw_r, rw_bn[:, :, :], ALU.add), "y3")
            RN.dve.wait(dve, "y3")
            RN.pe.wait(dve, "gate")
            RN.dve.done(nc.vector.tensor_tensor(rw_r, rw_r, all4, ALU.mult), "y4")
            RN.act.wait(dve, "hi")
            RN.dve.done(nc.vector.tensor_tensor(xb[:, 8:16, T:2 * T], rw_r, xb[:, 8:16, 0:T].bitcast(F32), ALU.subtract),
                        "lo")

        XA_ = Trio("xat", ["s", "p", "v", "o"], ["max", "sub", "sum", "div", "p", "lo"], ["exp", "v", "hi"])
        xs4 = xs[:, :, :].rearrange("p (h m) k -> p h m k", m=2)

        def xat_pe(pe):
            blocks_out(pe, g_xq)
            for h in range(XA_H):
                for m in range(2):
                    ins = nc.tensor.matmul(all4[:, 2 * h + m], lhsT=chunk(8 + h, m), rhs=work[:, h, PAD:COLS], start=True,
                                           stop=True)
            XA_.pe.done(ins, "s")
            XA_.dve.wait(pe, "div")
            for kh in range(2):
                for h in range(XA_H):
                    for m in range(2):
                        ins = nc.tensor.transpose(all4[:, 4 * kh + h, m * P:(m + 1) * P], xs[:, 2 * h + m, kh * P:(kh + 1) * P],
                                                  const("ident"))
            XA_.pe.done(ins, "p")
            XA_.dve.wait(pe, "p")
            for n in range(8):
                ins = nc.tensor.transpose(quad(0)[:, n], chunk(4 + n // 2, n % 2), const("ident"))
            XA_.pe.done(ins, "v")
            XA_.act.wait(pe, "v")
            for h in range(XA_H):
                for kh in range(2):
                    ins = nc.tensor.matmul(all4[:, 4 + h], lhsT=xv[:, h, kh], rhs=xp[:, 4 * kh + h], start=(kh == 0),
                                           stop=(kh == 1))
            XA_.pe.done(ins, "o")

        def xat_act(act):
            XA_.dve.wait(act, "sub")
            XA_.act.done(nc.scalar.activation(xs[:, :, :], xs[:, :, :], ACT.Exp, scale=XA_D ** -0.5), "exp")
            XA_.pe.wait(act, "v")
            XA_.act.done(nc.scalar.activation(xv[:, :, :, :].rearrange("p h m d -> p (h m) d"), quad(0), ACT.Copy), "v")
            XA_.pe.wait(act, "o")
            XA_.act.done(nc.scalar.activation(xb[:, 0:4, 0:T], all4[:, 4:8], ACT.Copy), "hi")

        def xat_dve(dve):
            XA_.pe.wait(dve, "s")
            XA_.dve.done(nc.vector.tensor_reduce(xm[:, 0:8], all4, AX.X, ALU.max), "max")
            XA_.dve.wait(dve, "max")
            XA_.dve.done(nc.vector.tensor_tensor(xs[:, :, :], all4, xm[:, 0:8, None].to_broadcast([P, 8, T]), ALU.subtract),
                         "sub")
            XA_.act.wait(dve, "exp")
            XA_.dve.done(nc.vector.tensor_reduce(xm[:, 8:16], xs[:, :, :], AX.X, ALU.add), "sum")
            XA_.dve.wait(dve, "sum")
            dve_link(nc.vector.reciprocal(xm[:, 8:16], xm[:, 8:16]))
            XA_.dve.done(nc.vector.tensor_tensor(xs[:, :, :], xs[:, :, :], xm[:, 8:16, None].to_broadcast([P, 8, T]),
                                                 ALU.mult), "div")
            XA_.pe.wait(dve, "p")
            XA_.dve.done(nc.vector.tensor_copy(xp[:, :, :], all4), "p")
            XA_.act.wait(dve, "hi")
            XA_.dve.done(nc.vector.tensor_tensor(xb[:, 0:4, T:2 * T], all4[:, 4:8], xb[:, 0:4, 0:T].bitcast(F32),
                                                 ALU.subtract), "lo")

        block = ctx.enter_context(nc.Block())

        @block.sync
        def _(sp):
            sp.dma_start(resid[:, :, :], a["x"]).then_inc(resid_in, 16)
            sp.dma_start(cst[:, :, :], a["consts"]).then_inc(consts_in, 16)
            sp.dma_start(vec[:, :], a["vecs"]).then_inc(consts_in, 16)
            for g in plan.stages:
                load_weights(sp, g)
            for n in range(4):
                sp.wait_ge(out_ready, 4 * n + 4)
                sp.dma_start(out.rearrange("(k p) t -> p k t", p=P)[:, 4 * n:4 * n + 4],
                             work[:, 4 * n:4 * n + 4, PAD:COLS]).then_inc(out_done, 16)
            sp.wait_ge(out_done, 64)

        @block.gpsimd
        def _(pool):
            pool.wait_ge(x_ready, 48)
            pool.dma_start(masks[:, :, :], a["masks"]).then_inc(masks_in, 16)
            pool.dma_start(al, a["dn_ab"]).then_inc(masks_in, 16)
            blocks_out(pool, g_rw)
            DF.dve.wait(pool, "lo")
            pool.dma_start(rw_lw[0:64, :], a["rw_w2_2"]).then_inc(lora_in, 16)
            pool.dma_start(rw_lw[64:P, :], a["rw_a2_2"]).then_inc(lora_in, 16)
            RW.dve.wait(pool, "y", 3)
            pool.dma_start(rw_g2[:, :], a["rw_g2_2"]).then_inc(lora_in, 16)
            pool.dma_start(mem[:, :, :], a["mem"]).then_inc(mem_in, 16)

        @block.scalar
        def _(act):
            norm_act(act, 0, resid, 0, 0, lambda e: e.wait_ge(resid_in, 16))
            split_hi(act, g_glu, 0, 0)
            norm_split_act(act, 0, xa)
            gemm_act(act, g_glu, follows=g_qkv)
            blocks_out(act, g_glu)
            nc.scalar.activation(glu(TB_), glu(TB_), ACT.Sigmoid).then_inc(glu_sig, 1)
            gemm_act(act, g_qkv, follows=g_gsb)
            gemm_act(act, g_gsb, lambda m: att_act(act, m), follows=g_gcv)
            gemm_act(act, g_gcv, lambda m: att_act(act, m + 8), follows=g_sbo)
            att_act(act, 16)
            blocks_out(act, g_gcv)
            nc.scalar.activation(gates(TGS), gates(TGS), ACT.Sigmoid).then_inc(gates_done, 1)
            nc.scalar.activation(gates(TGC), gates(TGC), ACT.Sigmoid).then_inc(gates_done, 1)
            gemm_act(act, g_sbo, lambda m: ln_act(act, m), follows=g_cvo)
            gemm_act(act, g_cvo, follows=g_wo)
            act.wait_ge(merged, 1)
            nc.scalar.activation(xa[:, :, 0:T], gates(TGS), ACT.Copy).then_inc(merged_hi, 1)
            gemm_act(act, g_wo, follows=ff1[0])
            norm_act(act, 1, work, PAD, 16, lambda e: blocks_out(e, g_wo))
            norm_act(act, 2, resid, 0, 0, lambda e: e.wait_ge(norm_res, DT))
            norm_split_act(act, 1, xa)
            for g, n in zip(ff1, ff1[1:] + [g_dn]):
                gemm_act(act, g, follows=n)
            norm_act(act, 3, work, PAD, 16, lambda e: blocks_out(e, ff1[-1]))
            norm_act(act, 4, resid, 0, 0, lambda e: e.wait_ge(norm_res, 2 * DT))
            norm_split_act(act, 2, xa)
            gemm_act(act, g_dn, lambda m: dn_conv_act(act, m), follows=g_gab)
            act.wait_ge(masks_in, 32)
            gemm_act(act, g_gab, follows=g_rw)
            gemm_act(act, g_rw, follows=g_mk)
            gates_act(act)
            l2_act(act)
            L2.dve.wait(act, "done", DN_H - 1)
            for r in range(2):
                dn_act(act, r)
            dnf_act(act)
            rwp_act(act)
            for r in range(4):
                rw_act(act, r)
            rwn_act(act)
            norm_act(act, 5, mem, 0, 0, lambda e: e.wait_ge(mem_in, 16))
            norm_split_act(act, 3, xa)
            gemm_act(act, g_mk, follows=g_mv)
            gemm_act(act, g_mv, follows=g_out)
            gemm_act(act, g_out, follows=g_xq)
            norm_act(act, 6, resid, 0, 0, lambda e: blocks_out(e, g_out))
            norm_split_act(act, 4, xa)
            gemm_act(act, g_xq, follows=g_xo)
            xat_act(act)
            gemm_act(act, g_xo, follows=ff2[0])
            norm_act(act, 7, resid, 0, 0, lambda e: blocks_out(e, g_xo))
            norm_split_act(act, 5, xa)
            for g, n in zip(ff2, ff2[1:] + [None]):
                gemm_act(act, g, follows=n)
            norm_act(act, 8, resid, 0, 0, lambda e: blocks_out(e, ff2[-1]))

        @block.vector
        def _(dve):
            dve.sem_inc(lo_ready, RING)
            dve.sem_inc(slab_used, RING)
            dve.sem_inc(evacuated, 2)
            dve_link(nc.vector.memset(u[:, :, 0:UPAD], 0.0))
            dve_link(nc.vector.memset(work[:, :, 0:PAD], 0.0))
            dve.wait_ge(consts_in, 32)
            split_lo(dve, g_glu, 0, 0)
            norm_rs_dve(dve, 0)
            norm_split_dve(dve, 0, xa, resid, 0, 0, lambda k: v1("g_pre_mix", k), 0)
            gemm_dve(dve, g_glu, follows=g_qkv)
            dve.wait_ge(glu_sig, 1)
            dve_link(nc.vector.tensor_tensor(u[:, :, UPAD:UCOLS], glu(TA), glu(TB_), ALU.mult))
            gemm_dve(dve, g_qkv, lambda m: conv(dve, share(m)), follows=g_gsb)

            def beside(m):
                att_dve(dve, m)
                conv(dve, share(12 + m))
            gemm_dve(dve, g_gsb, beside, follows=g_gcv)
            gemm_dve(dve, g_gcv, lambda m: beside(m + 8), follows=g_sbo)
            att_dve(dve, 16)
            dve.wait_ge(gates_done, 2)
            gemm_dve(dve, g_sbo, lambda m: ln_dve(dve, m), follows=g_cvo)
            gemm_dve(dve, g_cvo, follows=g_wo)
            blocks_out(dve, g_cvo)
            nc.vector.tensor_tensor(gates(TGS), gates(TGS), gates(TGC), ALU.add).then_inc(merged, 1)
            dve.wait_ge(merged_hi, 1)
            nc.vector.tensor_tensor(xa[:, :, T:2 * T], gates(TGS), xa[:, :, 0:T].bitcast(F32),
                                    ALU.subtract).then_inc(x_ready, 16)
            gemm_dve(dve, g_wo, follows=ff1[0])
            norm_add_dve(dve, 1, 0, 16, lambda k: v1("g_post_mix", k))
            norm_rs_dve(dve, 2)
            norm_split_dve(dve, 1, xa, resid, 0, 0, lambda k: v1("g_pre_mlp", k), 48)
            for g, n in zip(ff1, ff1[1:] + [g_dn]):
                gemm_dve(dve, g, follows=n)
            norm_add_dve(dve, 3, 1, 16, lambda k: v1("g_post_mlp", k))
            norm_rs_dve(dve, 4)
            norm_split_dve(dve, 2, xa, resid, 0, 0, lambda k: v2("mix_norm_w_2", k), 64)
            gemm_dve(dve, g_dn, lambda m: dn_conv_dve(dve, m), follows=g_gab)
            dn_conv_dve(dve, 16)
            dve.wait_ge(masks_in, 32)
            gemm_dve(dve, g_gab, follows=g_rw)
            gemm_dve(dve, g_rw, follows=g_mk)
            gates_dve(dve)
            l2_dve(dve)
            for r in range(2):
                dn_dve(dve, r)
            dnf_dve(dve)
            rwp_dve(dve)
            for r in range(4):
                rw_dve(dve, r)
            rwn_dve(dve)
            norm_rs_dve(dve, 5)
            norm_split_dve(dve, 3, xa, mem, 0, 0, lambda k: v2("mem_norm_w_2", k), 80)
            gemm_dve(dve, g_mk, follows=g_mv)
            gemm_dve(dve, g_mv, follows=g_out)
            gemm_dve(dve, g_out, follows=g_xq)
            norm_rs_dve(dve, 6)
            norm_split_dve(dve, 4, xa, resid, 0, 0, lambda k: v2("xa_norm_w_2", k), 96)
            gemm_dve(dve, g_xq, follows=g_xo)
            xat_dve(dve)
            gemm_dve(dve, g_xo, follows=ff2[0])
            norm_rs_dve(dve, 7)
            norm_split_dve(dve, 5, xa, resid, 0, 0, lambda k: v2("ffn_norm_w_2", k), 112)
            for g, n in zip(ff2, ff2[1:] + [None]):
                gemm_dve(dve, g, follows=n)
            norm_rs_dve(dve, 8)
            for k in range(DT):
                nc.vector.scalar_tensor_tensor(out=work[:, k, PAD:COLS], in0=resid[:, k], scalar=v2("final_norm_w_2", k),
                                               in1=rs[:, :], op0=ALU.mult, op1=ALU.mult).then_inc(out_ready, 1)

        @block.tensor
        def _(pe):
            pe.wait_ge(consts_in, 32)
            norm_pe(pe, 0)
            gemm_pe(pe, g_glu, x_tiles=0)
            gemm_pe(pe, g_qkv)
            blocks_out(pe, g_qkv)
            gemm_pe(pe, g_gsb, lambda m: att_pe(pe, m))
            gemm_pe(pe, g_gcv, lambda m: att_pe(pe, m + 8))
            att_pe(pe, 16)
            pe.wait_ge(att_lo, SB_H)
            gemm_pe(pe, g_sbo, lambda m: ln_pe(pe, m))
            pe.wait_ge(x_ready, 32)
            gemm_pe(pe, g_cvo)
            pe.wait_ge(x_ready, 48)
            gemm_pe(pe, g_wo)
            norm_pe(pe, 1)
            norm_pe(pe, 2)
            gemm_pe(pe, ff1[0], x_tiles=48)
            for g in ff1[1:]:
                blocks_out(pe, plan.stages[plan.stages.index(g) - 1])
                gemm_pe(pe, g)
            norm_pe(pe, 3)
            norm_pe(pe, 4)
            gemm_pe(pe, g_dn, x_tiles=64)
            gemm_pe(pe, g_gab)
            gemm_pe(pe, g_rw)
            gates_pe(pe)
            l2_pe(pe)
            L2.dve.wait(pe, "done", DN_H - 1)
            for r in range(2):
                dn_pe(pe, r)
            dnf_pe(pe)
            rwp_pe(pe)
            RP.dve.wait(pe, "t3")
            RP.act.wait(pe, "t2")
            for r in range(4):
                rw_pe(pe, r)
            rwn_pe(pe)
            RN.dve.wait(pe, "y4")
            norm_pe(pe, 5)
            gemm_pe(pe, g_mk, x_tiles=80)
            gemm_pe(pe, g_mv)
            DF.dve.wait(pe, "lo")
            RN.dve.wait(pe, "lo")
            gemm_pe(pe, g_out)
            norm_pe(pe, 6)
            gemm_pe(pe, g_xq, x_tiles=96)
            blocks_out(pe, g_mv)
            xat_pe(pe)
            XA_.dve.wait(pe, "lo")
            gemm_pe(pe, g_xo)
            norm_pe(pe, 7)
            gemm_pe(pe, ff2[0], x_tiles=112)
            for g in ff2[1:]:
                blocks_out(pe, plan.stages[plan.stages.index(g) - 1])
                gemm_pe(pe, g)
            norm_pe(pe, 8)


def kernel(**inputs):
    import numpy as _np
    import concourse.bacc as _bacc
    from concourse import mybir as _mybir
    from concourse.bass_utils import run_bass_kernel_spmd as _run

    def tiles(x):
        x = _np.asarray(x)
        return x.reshape(-1, P).T

    nc = _bacc.Bacc("TRN2", target_bir_lowering=False, num_devices=1)
    arrays = {
        "x": _np.ascontiguousarray(_np.asarray(inputs["x"])[0].T.reshape(DT, P, T).transpose(1, 0, 2)),
        "consts": constants().reshape(P, len(CONSTS), P),
        "masks": level_masks(),
        "vecs": _np.concatenate([tiles(inputs[n]) for n, _ in VEC1 + VEC2], axis=1),
        "mem": _np.asarray(inputs["mem_2"])[0].T.reshape(DT, P, T).transpose(1, 0, 2),
        "dn_ab": _np.stack([_np.asarray(inputs[n])[0] for n in ("dn_a_log_2", "dn_dt_bias_2")], axis=1),
    }
    for name in ("w_in", "w_sb_out", "w_conv_out", "w_o", "w_up", "w_down", "w_in_2", "w_out_2", "xa_wq_2", "xa_wk_2",
                 "xa_wv_2", "xa_wo_2", "ffn_w1_2", "ffn_w2_2", "rw_w2_2", "rw_a2_2", "rw_g2_2"):
        arrays[name] = _np.asarray(inputs[name])[0]
    arrays = {k: _np.ascontiguousarray(v) for k, v in arrays.items()}
    aps = {k: nc.dram_tensor(k, v.shape, _mybir.dt.from_np(v.dtype), kind="ExternalInput").ap() for k, v in arrays.items()}
    out = nc.dram_tensor("out", (D, T), F32, kind="ExternalOutput").ap()
    build_program(nc, aps, out)
    r = _run(nc, [arrays], core_ids=[0])
    return _np.ascontiguousarray(r.results[0]["out"].T).reshape(1, T, D)
```

```python
from contextlib import ExitStack

import numpy as np

import concourse.bass as bass
from concourse import mybir

F32 = mybir.dt.float32
F32R = mybir.dt.float32r
ALU = mybir.AluOpType
ACT = mybir.ActivationFunctionType
AX = mybir.AxisListType

P = 128
T = 256
D = 2048
DT = D // P
EPS = 1e-6
PAD = 4
COLS = T + PAD
BW = 256
KG = 4
RING = 4
SB_H, SB_D = 8, 128
CONV = 31
UPAD = CONV - 1
UCOLS = T + UPAD
D_FF = 4 * D
FF_PIECES = 4

VEC1 = [("g_pre_mix", 16), ("b_in", 72), ("w_dw", CONV * 8), ("b_dw", 8), ("g_conv_ln", 8), ("b_conv_ln", 8),
        ("g_post_mix", 16), ("g_pre_mlp", 16), ("g_post_mlp", 16)]


def columns(spec):
    at, out = 0, {}
    for name, n in spec:
        out[name] = at
        at += n
    return out, at


VEC2 = [("mix_norm_w_2", 16), ("dn_conv_w_2", 96), ("dn_norm_w_2", 1), ("rw_mu_2", 26), ("rw_w0_2", 8), ("rw_a0_2", 8),
        ("rw_k_k_2", 8), ("rw_k_a_2", 8), ("rw_r_k_2", 8), ("rw_ln_w_2", 8), ("rw_ln_b_2", 8), ("xa_norm_w_2", 16),
        ("mem_norm_w_2", 16), ("ffn_norm_w_2", 16), ("final_norm_w_2", 16)]
V1, NV1 = columns(VEC1)
V2, NV2 = columns(VEC2)

CONSTS = ["ident", "ones", "upto", "before", "before_big", "incl", "ones_head"]
LEVELS = 7
DN_H, RW_H, RW_D = 8, 16, 64
RW_DECAY = float(np.exp(-0.5))
XA_H, XA_D = 4, 128


def constants():
    i = np.arange(P)
    later = (i[:, None] >= i[None, :]).astype(np.float32)
    before = (i[:, None] < i[None, :]).astype(np.float32)
    big = np.where(before > 0, 0.0, -1e30).astype(np.float32)
    incl = (i[:, None] <= i[None, :]).astype(np.float32)
    head = (i[:, None] // RW_D == i[None, :] // RW_D).astype(np.float32)
    return np.concatenate([np.eye(P, dtype=np.float32), np.ones((P, P), np.float32), later, before, big, incl, head],
                          axis=1)


def level_masks():
    i = np.arange(P)
    out = []
    for l in range(LEVELS):
        n = i >> l
        out.append(((n[:, None] % 2 == 0) & (n[None, :] == n[:, None] + 1)).astype(np.float32))
    return np.stack(out, axis=1)


class Gemm:

    def __init__(self, plan, name, w, k, n0, n, x, kind, dst, x_from=0, bias=None, k0=0, apart=P):
        self.name, self.w, self.n0, self.x, self.kind, self.dst = name, w, n0, x, kind, dst
        self.k0, self.x_from, self.bias, self.apart = k0, x_from, bias, apart
        self.groups = k // (P * KG)
        self.blocks = n // BW
        self.b0, self.s0, self.sum0, self.sq0 = plan.blocks, plan.slabs, plan.sums, plan.squares
        self.unroll = 4 if self.groups == 1 else 2
        self.turn = self.unroll * self.groups
        plan.blocks += self.blocks
        plan.slabs += self.blocks * self.groups
        plan.sums += self.blocks if kind != "store" else 0
        plan.squares += self.blocks if kind == "relu2" else 0
        plan.stages.append(self)
        assert self.s0 % RING == 0 and self.turn % RING == 0

    def slab(self, i, block, j):
        o = block * self.groups + j
        return o % RING, self.s0 // RING + i * (self.turn // RING) + o // RING, self.s0 + i * self.turn + o


class Steps:

    def __init__(self, sem, names):
        self.sem, self.names, self.n = sem, names, 0

    def at(self, name, r=0):
        return r * len(self.names) + self.names.index(name) + 1

    def done(self, ins, name, r=0):
        self.n += 1
        assert self.at(name, r) == self.n, (name, r, self.names[(self.n - 1) % len(self.names)])
        ins.then_inc(self.sem, 1)

    def wait(self, eng, name, r=0):
        eng.wait_ge(self.sem, self.at(name, r))


class Plan:
    def __init__(self):
        self.blocks = self.slabs = self.sums = self.squares = 0
        self.stages = []


def build_program(nc, a, out):
    plan = Plan()
    ctx = ExitStack()
    with ctx:
        base = 16640
        top = [base]

        def at(name, shape, dt, offset=None):
            size = 4 * int(np.prod(shape[1:]))
            if offset is None:
                offset = top[0]
                top[0] += (size + 31) // 32 * 32
            return nc.alloc_sbuf_tensor_at(name, shape, dt, offset=offset)

        def sem(name):
            return ctx.enter_context(nc.semaphore(name))

        raw = at("raw", [P, RING, KG, BW], F32)
        hi = at("hi", [P, RING, KG, BW], F32R)
        lo = at("lo", [P, RING, KG, BW], F32R)
        half = at("half", [P, 2, T], F32)
        sq = at("sq", [P, 2, T], F32)
        rs = at("rs", [P, T], F32)
        resid = at("resid", [P, DT, T], F32)
        xa_at = top[0]
        xa = at("xa", [P, DT, 2 * T], F32R)
        xb_at = top[0]
        xb = at("xb", [P, DT, 2 * T], F32R)
        work_at = top[0]
        work = at("work", [P, 64, COLS], F32)
        cst = at("cst", [P, len(CONSTS), P], F32)
        vec = at("vec", [P, NV1 + NV2], F32)
        small = at("small", [P, 160], F32)
        u = at("u", [P, 8, UCOLS], F32, xb_at + 16384)
        zs = at("zs", [P, 3 * P], F32, xb_at + 16384 + 8 * UCOLS * 4)
        la = at("la", [P, 3 * P], F32, xb_at + 16384 + 8 * UCOLS * 4 + 1536)
        vt = at("vt", [P, 2, P], F32, xb_at + 16384 + 8 * UCOLS * 4 + 3072)

        def const(name):
            return cst[:, CONSTS.index(name), :]

        def v1(name, i=0):
            return vec[:, V1[name] + i:V1[name] + i + 1]

        pg = ctx.enter_context(nc.psum_tensor("pg", [P, 2, 2, 2 * T], F32))
        p4 = ctx.enter_context(nc.psum_tensor("p4", [P, 4, 512], F32))
        ps = [p4[:, n] for n in range(4)]

        w_in = a["w_in"]
        TA, TB_, TQ, TK, TV, TGS, TGC, TY = 0, 8, 16, 24, 32, 0, 40, 56
        g_glu = Gemm(plan, "glu", w_in, D, 3072, 2048, xa, "store", (work, TA, PAD), bias=V1["b_in"] + 24)
        g_qkv = Gemm(plan, "qkv", w_in, D, 0, 3072, xa, "store", (work, TQ, PAD), bias=V1["b_in"])
        g_gsb = Gemm(plan, "gate_sb", w_in, D, 5120, 2048, xa, "store", (work, TGS, PAD), bias=V1["b_in"] + 40)
        g_gcv = Gemm(plan, "gate_cv", w_in, D, 7168, 2048, xa, "store", (work, TGC, PAD), bias=V1["b_in"] + 56)
        g_sbo = Gemm(plan, "sb_out", a["w_sb_out"], D // 2, 0, D, xb, "mult", (work, TGS, PAD))
        g_cvo = Gemm(plan, "conv_out", a["w_conv_out"], D // 2, 0, D, xb, "mult", (work, TGC, PAD), x_from=8)
        g_wo = Gemm(plan, "w_o", a["w_o"], D, 0, D, xa, "store", (work, 16, PAD))
        ff1 = []
        for p in range(FF_PIECES):
            up = Gemm(plan, f"up{p}", a["w_up"], D, p * D, D, xa, "relu2", (xb, 0, 0))
            down = Gemm(plan, f"down{p}", a["w_down"], D, 0, D, xb, "add" if p else "store", (work, 16, PAD), k0=p * D)
            ff1 += [up, down]

        consts_in, resid_in = sem("consts_in"), sem("resid_in")
        raw_in = [sem(f"raw_in{n}") for n in range(RING)]
        hi_ready = sem("hi_ready")
        lo_ready = sem("lo_ready")
        slab_used = sem("slab_used")
        half_out = sem("half_out")
        evacuated = sem("evacuated")
        summed = sem("summed")
        squared, rounded = sem("squared"), sem("rounded")
        x_ready = sem("x_ready")
        norm_sq, norm_used = sem("norm_sq"), sem("norm_used")
        norm_rs, norm_nx, norm_hi = sem("norm_rs"), sem("norm_nx"), sem("norm_hi")
        norm_res = sem("norm_res")
        dve_seq, act_seq = sem("dve_seq"), sem("act_seq")
        glu_sig, glu_u = sem("glu_sig"), sem("glu_u")
        att_z, att_zs, att_ln, att_sp, att_s, att_t = [sem("att_" + n) for n in ("z", "zs", "ln", "sp", "s", "t")]
        att_a, att_vt, att_o, att_hi, att_lo, att_vp = [sem("att_" + n) for n in ("a", "vt", "o", "hi", "lo", "vp")]
        conv_done, gates_done, merged_hi, merged = sem("conv_done"), sem("gates_done"), sem("merged_hi"), sem("merged")
        ln_sum, ln_mid, ln_sq, ln_var, ln_std = [sem("ln_" + n) for n in ("sum", "mid", "sq", "var", "std")]
        ln_y, ln_sig, ln_f, ln_hi = [sem("ln_" + n) for n in ("y", "sig", "f", "hi")]
        out_ready, out_done = sem("out_ready"), sem("out_done")
        masks_in, mem_in = sem("masks_in"), sem("mem_in")
        seq = {"dve": 0, "act": 0}

        def dve_link(ins):
            seq["dve"] += 1
            ins.then_inc(dve_seq, 1)
            nc.vector.wait_ge(dve_seq, seq["dve"])

        def act_link(ins):
            seq["act"] += 1
            ins.then_inc(act_seq, 1)
            nc.scalar.wait_ge(act_seq, seq["act"])

        def run_blocks(eng, n, unroll, body, after=None, each=None):
            whole = n // unroll
            if after is None and each is None and whole > 1:
                with eng.Fori(0, whole) as i:
                    for v in range(unroll):
                        body(i, v)
            else:
                for t in range(whole * unroll):
                    body(t // unroll, t % unroll)
                    if after:
                        after(t)
            for v in range(n - whole * unroll):
                body(whole, v)
                if after:
                    after(whole * unroll + v)

        def load_weights(sp, g):
            w = g.w.rearrange("(k p) n -> p k n", p=P)

            def block(i, v):
                first = sp.snap(g.n0 + (i * g.unroll + v) * BW) if not isinstance(i, int) else g.n0 + (i * g.unroll + v) * BW
                for j in range(g.groups):
                    slot, turn, s = g.slab(i, v, j)
                    k = g.k0 // P + j * KG
                    sp.wait_ge(lo_ready, s + 1)
                    sp.dma_start(raw[:, slot], w[:, k:k + KG, bass.ds(first, BW)]).then_inc(raw_in[slot], 16)

            run_blocks(sp, g.blocks, g.unroll, block)

        def split_hi(act, g, i, v, each=None):
            for j in range(g.groups):
                slot, turn, s = g.slab(i, v, j)
                act.wait_ge(raw_in[slot], turn * 16 + 16)
                act.wait_ge(slab_used, s + 1)
                nc.scalar.activation(hi[:, slot], raw[:, slot], ACT.Copy).then_inc(hi_ready, 1)
                if each:
                    each()

        def take_half(act, g, i, v):
            b = g.b0 + i * g.unroll + v
            par = (g.b0 + v) % 2
            act.wait_ge(slab_used, g.slab(i, v, g.groups - 1)[2] + 1 + RING)
            act.wait_ge(evacuated, b + 2)
            if g.bias is None:
                nc.scalar.activation(half[:, :, :], pg[:, par, :, T:2 * T], ACT.Copy).then_inc(half_out, 1)
            else:
                for t in range(2):
                    c = g.bias + 2 * (i * g.unroll + v) + t
                    ins = nc.scalar.activation(half[:, t], pg[:, par, t, T:2 * T], ACT.Identity,
                                               bias=vec[:, bass.ds(c, 1)])
                ins.then_inc(half_out, 1)

        def gemm_act(act, g, after=None, follows=None, each=None):
            def block(i, v):
                split_hi(act, g, i, v + 1, each)
                take_half(act, g, i, v)
            run_blocks(act, g.blocks - 1, g.unroll, block, after, each)
            if follows:
                split_hi(act, follows, 0, 0, each)
            n = g.blocks - 1
            take_half(act, g, n // g.unroll, n % g.unroll)
            if after:
                after(n)

        def split_lo(dve, g, i, v, each=None):
            for j in range(g.groups):
                slot, turn, s = g.slab(i, v, j)
                dve.wait_ge(hi_ready, s + 1)
                nc.vector.tensor_tensor(lo[:, slot], raw[:, slot], hi[:, slot].bitcast(F32),
                                        ALU.subtract).then_inc(lo_ready, 1)
                if each:
                    each()

        def evacuate(dve, g, i, v):
            t = i * g.unroll + v
            par = (g.b0 + v) % 2
            into, tile, off = g.dst
            dve.wait_ge(half_out, g.b0 + t + 1)
            psum = pg[:, par, :, 0:T]
            place = into[:, bass.ds(tile + 2 * t, 2), off:off + T]
            if g.kind == "store":
                nc.vector.tensor_tensor(place, psum, half[:, :, :], ALU.add).then_inc(evacuated, 1)
                return
            own = g.sum0 + t + 1
            if g.kind in ("add", "mult"):
                nc.vector.tensor_tensor(half[:, :, :], psum, half[:, :, :], ALU.add).then_inc(summed, 1)
                dve.wait_ge(summed, own)
                nc.vector.tensor_tensor(place, place, half[:, :, :],
                                        ALU.add if g.kind == "add" else ALU.mult).then_inc(evacuated, 1)
                return
            own_sq = g.sq0 + t + 1
            nc.vector.tensor_tensor(sq[:, :, :], psum, half[:, :, :], ALU.add).then_inc(summed, 1)
            dve.wait_ge(summed, own)
            nc.vector.scalar_tensor_tensor(out=sq[:, :, :], in0=sq[:, :, :], scalar=0.0, in1=sq[:, :, :],
                                           op0=ALU.max, op1=ALU.mult).then_inc(squared, 1)
            dve.wait_ge(squared, own_sq)
            nc.vector.tensor_copy(place, sq[:, :, :]).then_inc(rounded, 1)
            dve.wait_ge(rounded, own_sq)
            rest = into[:, bass.ds(tile + 2 * t, 2), T:2 * T]
            nc.vector.tensor_tensor(rest, sq[:, :, :], place.bitcast(F32), ALU.subtract).then_inc(evacuated, 1)

        def gemm_dve(dve, g, after=None, follows=None, each=None):
            def block(i, v):
                split_lo(dve, g, i, v + 1, each)
                evacuate(dve, g, i, v)
            run_blocks(dve, g.blocks - 1, g.unroll, block, after, each)
            if follows:
                split_lo(dve, follows, 0, 0, each)
            n = g.blocks - 1
            evacuate(dve, g, n // g.unroll, n % g.unroll)
            if after:
                after(n)

        def gemm_pe(pe, g, after=None, x_tiles=None, of=None, each=None):
            def block(i, v, waits=False):
                par = (g.b0 + v) % 2
                pe.wait_ge(evacuated, g.b0 + i * g.unroll + v + 1)
                for j in range(g.groups):
                    slot, turn, s = g.slab(i, v, j)
                    pe.wait_ge(lo_ready, s + 1 + RING)
                    if waits and of:
                        pe.wait_ge(evacuated, of.b0 + KG // 2 * (j + 1) + 2)
                    elif waits:
                        pe.wait_ge(x_ready, x_tiles + KG * (j + 1))
                    for t in range(2):
                        c = t * g.apart
                        for k in range(KG):
                            kk = g.x_from + j * KG + k
                            nc.tensor.matmul(pg[:, par, t, :], lhsT=hi[:, slot, k, c:c + P], rhs=g.x[:, kk, :],
                                             start=(j == 0 and k == 0), stop=False)
                            ins = nc.tensor.matmul(pg[:, par, t, 0:T], lhsT=lo[:, slot, k, c:c + P],
                                                   rhs=g.x[:, kk, 0:T], start=False,
                                                   stop=(j == g.groups - 1 and k == KG - 1))
                    ins.then_inc(slab_used, 1)
                    if each:
                        each()

            if x_tiles is not None or of:
                for v in range(g.unroll):
                    block(0, v, waits=(v == 0))
                    if after:
                        after(v)
                rest = g.blocks - g.unroll
                run_blocks(pe, rest, g.unroll, lambda i, v: block(i + 1, v),
                           (lambda t: after(t + g.unroll)) if after else None)
            else:
                run_blocks(pe, g.blocks, g.unroll, block, after, each)

        def square_tile(act, n, k, src, off, tile0):
            if n or k >= 2:
                act.wait_ge(norm_used, DT * n + k - 1)
            nc.scalar.activation(sq[:, k % 2], src[:, tile0 + k, off:off + T], ACT.Square).then_inc(norm_sq, 1)

        def norm_act(act, n, src, off, tile0, ready, k0=0):
            for k in range(k0, DT):
                ready(act, k)
                square_tile(act, n, k, src, off, tile0)
            act.wait_ge(norm_used, DT * (n + 1))
            act_link(nc.scalar.activation(rs[:, :], ps[0][:, 0:T], ACT.Ln, scale=1.0 / D, bias=EPS))
            nc.scalar.activation(rs[:, :], rs[:, :], ACT.Exp, scale=-0.5).then_inc(norm_rs, 1)

        def squares_beside(act, g, n, src, off, tile0):
            def after(m):
                if m:
                    act.wait_ge(evacuated, g.b0 + m + 2)
                    for k in (2 * m - 2, 2 * m - 1):
                        square_tile(act, n, k, src, off, tile0)
            return after

        def sums_beside(pe, n):
            def after(m):
                if m >= 2:
                    norm_pe(pe, n, 2 * m - 4, 2 * m - 2)
            return after

        LATE = DT - 4

        def norm_split_act(act, m, x):
            for k in range(DT):
                act.wait_ge(norm_nx, DT * m + k + 1)
                nc.scalar.activation(x[:, k, 0:T], half[:, k % 2], ACT.Copy).then_inc(norm_hi, 1)

        def norm_pe(pe, n, k0=0, k1=DT):
            for k in range(k0, k1):
                pe.wait_ge(norm_sq, DT * n + k + 1)
                ins = nc.tensor.matmul(ps[0][:, 0:T], lhsT=const("ones"), rhs=sq[:, k % 2],
                                       start=(k == 0), stop=(k == DT - 1))
                ins.then_inc(norm_used, 1)

        def norm_rs_dve(dve, n):
            dve.wait_ge(norm_rs, n + 1)

        def norm_split_dve(dve, m, x, src, off, tile0, gain, x_tiles):
            for k in range(DT + 1):
                if k < DT:
                    if k >= 2:
                        dve.wait_ge(x_ready, x_tiles + k - 1)
                    nc.vector.scalar_tensor_tensor(out=half[:, k % 2], in0=src[:, tile0 + k, off:off + T],
                                                   scalar=gain(k), in1=rs[:, :], op0=ALU.mult,
                                                   op1=ALU.mult).then_inc(norm_nx, 1)
                if k:
                    dve.wait_ge(norm_hi, DT * m + k)
                    nc.vector.tensor_tensor(x[:, k - 1, T:2 * T], half[:, (k - 1) % 2],
                                            x[:, k - 1, 0:T].bitcast(F32), ALU.subtract).then_inc(x_ready, 1)

        def norm_add_dve(dve, n, added, tile0, gain):
            norm_rs_dve(dve, n)
            for k in range(DT + 1):
                if k < DT:
                    if k >= 2:
                        dve.wait_ge(norm_res, DT * added + k - 1)
                    seq["dve"] += 1
                    nc.vector.scalar_tensor_tensor(out=half[:, k % 2], in0=work[:, tile0 + k, PAD:COLS],
                                                   scalar=gain(k), in1=rs[:, :], op0=ALU.mult,
                                                   op1=ALU.mult).then_inc(dve_seq, 1)
                if k:
                    dve.wait_ge(dve_seq, seq["dve"] - (1 if k < DT else 0))
                    nc.vector.tensor_tensor(resid[:, k - 1], resid[:, k - 1], half[:, (k - 1) % 2],
                                            ALU.add).then_inc(norm_res, 1)

        glu = lambda t: work[:, t:t + 8, PAD:COLS]
        conv_steps = [(c, j) for c in range(8) for j in range(CONV)]

        def conv(dve, lot):
            for c, j in lot:
                acc, x = work[:, TY + c, PAD:COLS], u[:, c, j:j + T]
                if j == 0:
                    ins = nc.vector.tensor_scalar(acc, x, v1("w_dw", c), v1("b_dw", c), ALU.mult, ALU.add)
                else:
                    ins = nc.vector.scalar_tensor_tensor(out=acc, in0=x, scalar=v1("w_dw", 8 * j + c), in1=acc,
                                                         op0=ALU.mult, op1=ALU.add)
                if (c, j) == conv_steps[-1]:
                    ins.then_inc(conv_done, 1)
                else:
                    dve_link(ins)

        def share(m):
            a0 = 12 * m if m < 12 else 144 + 7 * (m - 12)
            return conv_steps[a0:a0 + (12 if m < 12 else 7)]

        diag = lambda x: x[:, 0:3 * P].rearrange("p (b c) -> p b c", c=P)[:, 0:3:2, :]
        both = lambda name: const(name)[:, None, :].to_broadcast([P, 2, P])

        def att_pe(pe, m):
            h = m // 2
            if m % 2 == 0 and h > 0:
                pe.wait_ge(att_a, h)
                if h >= 2:
                    pe.wait_ge(att_lo, h - 1)
                nc.tensor.matmul(ps[3][:, 0:P], lhsT=vt[:, 0], rhs=la[:, 0:P], start=True, stop=True)
                nc.tensor.matmul(ps[3][:, P:T], lhsT=vt[:, 0], rhs=la[:, P:T], start=True, stop=False)
                nc.tensor.matmul(ps[3][:, P:T], lhsT=vt[:, 1], rhs=la[:, T:3 * P], start=False,
                                 stop=True).then_inc(att_o, 1)
            if h >= SB_H:
                return
            if m % 2 == 0:
                q, k, v = (work[:, t + h, PAD:COLS] for t in (TQ, TK, TV))
                if h:
                    pe.wait_ge(att_zs, h)
                    pe.wait_ge(att_vt, h)
                nc.tensor.matmul(ps[0][:, 0:T], lhsT=k[:, 0:P], rhs=q, start=True, stop=True)
                nc.tensor.matmul(ps[0][:, T:3 * P], lhsT=k[:, P:T], rhs=q[:, P:T], start=True,
                                 stop=True).then_inc(att_z, 1)
                nc.tensor.transpose(ps[2][:, 0:P], v[:, 0:P], const("ident"))
                nc.tensor.transpose(ps[2][:, P:T], v[:, P:T], const("ident")).then_inc(att_vp, 1)
            else:
                pe.wait_ge(att_sp, h + 1)
                nc.tensor.matmul(diag(ps[1][:, 0:3 * P]), lhsT=const("upto"), rhs=diag(la), start=True, stop=True)
                nc.tensor.matmul(ps[1][:, P:T], lhsT=const("upto"), rhs=la[:, P:T], start=True, stop=False)
                nc.tensor.matmul(ps[1][:, P:T], lhsT=const("ones"), rhs=la[:, T:3 * P], start=False,
                                 stop=True).then_inc(att_s, 1)

        def att_act(act, m):
            h = m // 2
            if m % 2 == 0 and h > 0:
                act.wait_ge(att_o, h)
                nc.scalar.activation(xb[:, h - 1, 0:T], ps[3][:, 0:T], ACT.Copy).then_inc(att_hi, 1)
            if h >= SB_H:
                return
            if m % 2 == 0:
                act.wait_ge(att_vp, h + 1)
                if h:
                    act.wait_ge(att_o, h)
                nc.scalar.activation(vt[:, :, :], ps[2][:, 0:T].rearrange("p (a b) -> p a b", a=2),
                                     ACT.Copy).then_inc(att_vt, 1)
                act.wait_ge(att_zs, h + 1)
                act_link(nc.scalar.activation(la[:, :], zs[:, :], ACT.Abs))
                act_link(nc.scalar.activation(la[:, :], la[:, :], ACT.Exp, scale=-1.0))
                nc.scalar.activation(la[:, :], la[:, :], ACT.Ln, bias=1.0).then_inc(att_ln, 1)
            else:
                act.wait_ge(att_t, h + 1)
                nc.scalar.activation(la[:, :], zs[:, :], ACT.Exp).then_inc(att_a, 1)

        def att_dve(dve, m):
            h = m // 2
            if m % 2 == 0 and h > 0:
                dve.wait_ge(att_hi, h)
                nc.vector.tensor_tensor(xb[:, h - 1, T:2 * T], ps[3][:, 0:T], xb[:, h - 1, 0:T].bitcast(F32),
                                        ALU.subtract).then_inc(att_lo, 1)
            if h >= SB_H:
                return
            if m % 2 == 0:
                dve.wait_ge(att_z, h + 1)
                if h:
                    dve.wait_ge(att_a, h)
                nc.vector.tensor_scalar(zs[:, :], ps[0][:, 0:3 * P], SB_D ** -0.5, None, ALU.mult).then_inc(att_zs, 1)
                dve.wait_ge(att_ln, h + 1)
                dve_link(nc.vector.scalar_tensor_tensor(out=la[:, :], in0=zs[:, :], scalar=0.0, in1=la[:, :],
                                                        op0=ALU.max, op1=ALU.add))
                nc.vector.tensor_tensor(diag(la), diag(la), both("before"), ALU.mult).then_inc(att_sp, 1)
            else:
                dve.wait_ge(att_s, h + 1)
                dve_link(nc.vector.tensor_tensor(zs[:, :], zs[:, :], ps[1][:, 0:3 * P], ALU.subtract))
                nc.vector.tensor_tensor(diag(zs), diag(zs), both("before_big"), ALU.add).then_inc(att_t, 1)

        CV = D // 2
        conv_y = work[:, TY:TY + 8, PAD:COLS]
        ln_tmp = work[:, 16:24, PAD:COLS]

        def ln_pe(pe, m):
            if m == 0:
                pe.wait_ge(conv_done, 1)
                for c in range(8):
                    ins = nc.tensor.matmul(ps[0][:, 0:T], lhsT=const("ones"), rhs=work[:, TY + c, PAD:COLS],
                                           start=(c == 0), stop=(c == 7))
                ins.then_inc(ln_sum, 1)
            if m == 2:
                pe.wait_ge(ln_sq, 1)
                for c in range(8):
                    ins = nc.tensor.matmul(ps[1][:, 0:T], lhsT=const("ones"), rhs=work[:, 16 + c, PAD:COLS],
                                           start=(c == 0), stop=(c == 7))
                ins.then_inc(ln_var, 1)

        def ln_act(act, m):
            if m == 0:
                act.wait_ge(ln_mid, 1)
                nc.scalar.activation(ln_tmp, conv_y, ACT.Square).then_inc(ln_sq, 1)
            if m == 2:
                act.wait_ge(ln_var, 1)
                act_link(nc.scalar.activation(rs[:, :], ps[1][:, 0:T], ACT.Ln, scale=1.0 / CV, bias=EPS))
                nc.scalar.activation(rs[:, :], rs[:, :], ACT.Exp, scale=-0.5).then_inc(ln_std, 1)
            if m == 3:
                act.wait_ge(ln_y, 1)
                for c in range(8):
                    ins = nc.scalar.activation(work[:, 16 + c, PAD:COLS], work[:, TY + c, PAD:COLS], ACT.Sigmoid,
                                               scale=v1("g_conv_ln", c), bias=v1("b_conv_ln", c))
                ins.then_inc(ln_sig, 1)
            if m == 5:
                act.wait_ge(ln_f, 1)
                nc.scalar.activation(xb[:, 8:16, 0:T], conv_y, ACT.Copy).then_inc(ln_hi, 1)

        def ln_dve(dve, m):
            if m == 0:
                dve.wait_ge(ln_sum, 1)
                nc.vector.scalar_tensor_tensor(out=conv_y, in0=ps[0][:, None, 0:T].to_broadcast([P, 8, T]),
                                               scalar=-1.0 / CV, in1=conv_y, op0=ALU.mult,
                                               op1=ALU.add).then_inc(ln_mid, 1)
            if m == 2:
                dve.wait_ge(ln_std, 1)
                nc.vector.tensor_tensor(conv_y, conv_y, rs[:, None, :].to_broadcast([P, 8, T]),
                                        ALU.mult).then_inc(ln_y, 1)
            if m == 4:
                dve.wait_ge(ln_sig, 1)
                for c in range(8):
                    ins = nc.vector.tensor_scalar(work[:, TY + c, PAD:COLS], work[:, TY + c, PAD:COLS],
                                                  v1("g_conv_ln", c), v1("b_conv_ln", c), ALU.mult, ALU.add)
                dve_link(ins)
                nc.vector.tensor_tensor(conv_y, conv_y, ln_tmp, ALU.mult).then_inc(ln_f, 1)
            if m == 6:
                dve.wait_ge(ln_hi, 1)
                nc.vector.tensor_tensor(xb[:, 8:16, T:2 * T], conv_y, xb[:, 8:16, 0:T].bitcast(F32),
                                        ALU.subtract).then_inc(x_ready, 16)

        EPS_C = EPS
        const_eps = lambda x: x
        gates = lambda t0: work[:, t0:t0 + DT, PAD:COLS]
        last = lambda g: g.slab((g.blocks - 1) // g.unroll, (g.blocks - 1) % g.unroll, g.groups - 1)[2] + 1 + RING

        def blocks_out(eng, g):
            eng.wait_ge(evacuated, g.b0 + g.blocks + 2)

        def v2(name, i=0):
            c = NV1 + V2[name] + i
            return vec[:, c:c + 1]

        w2in = a["w_in_2"]
        DQ, DK, DV, DZ, RR, RK, RV, RL, RG, GA, GB = 0, 8, 16, 24, 32, 40, 48, 56, 57, 58, 59
        g_dn = Gemm(plan, "dn", w2in, D, 0, 4096, xa, "store", (work, DQ, PAD))
        g_gab = Gemm(plan, "gab", w2in, D, 4096, BW, xa, "store", (work, GA, PAD), apart=DN_H)
        g_rw = Gemm(plan, "rw", w2in, D, 4112, 3328, xa, "store", (work, RR, PAD))
        g_mk = Gemm(plan, "mem_k", a["xa_wk_2"], D, 0, 512, xa, "store", (work, 0, PAD))
        g_mv = Gemm(plan, "mem_v", a["xa_wv_2"], D, 0, 512, xa, "store", (work, 4, PAD))
        g_out = Gemm(plan, "w_out", a["w_out_2"], D, 0, D, xb, "add", (resid, 0, 0))
        g_xq = Gemm(plan, "xa_q", a["xa_wq_2"], D, 0, 512, xa, "store", (work, 8, PAD))
        g_xo = Gemm(plan, "xa_o", a["xa_wo_2"], 512, 0, D, xb, "add", (resid, 0, 0))
        ff2 = []
        for p in range(FF_PIECES):
            ff2 += [Gemm(plan, f"w1_{p}", a["ffn_w1_2"], D, p * D, D, xa, "relu2", (xb, 0, 0)),
                    Gemm(plan, f"w2_{p}", a["ffn_w2_2"], D, 0, D, xb, "add", (resid, 0, 0), k0=p * D)]

        def over(name, shape, region, byte):
            start = {"xa": xa_at, "xb": xb_at, "work": work_at}[region]
            return at(name, shape, F32, start + byte)

        masks = over("masks", [P, LEVELS, P], "work", 60 * COLS * 4)
        dnc = over("dnc", [P, 24, T], "xb", 0)
        dn_rn = over("dn_rn", [P, 2, 2 * T], "xb", 24576)
        slot = lambda name, n: over(name, [P, 8, P], "xb", 4096 * n)
        dn_at_, dn_n, dn_x, dn_xt, dn_nm, dn_tt, dn_e, dn_v = (
            slot(f"dn_{x}", n) for n, x in enumerate(("attn", "n", "x", "xt", "nm", "tt", "e", "v")))
        dn_eq = over("dn_eq", [P, 4, P], "xb", 4096 * 2)
        dn_v0 = over("dn_v0", [P, 4, P], "xb", 4096 * 6)
        dn_s1 = over("dn_s1", [P, 4, P], "xb", 4096 * 6 + 2048)
        dn_v1 = over("dn_v1", [P, 4, P], "xb", 4096 * 5)
        dn_k0 = sq[:, :, :].rearrange("p a (b c) -> p (a b) c", b=2)
        dn_sq = over("dn_sq", [P, 8, T], "xb", 0)
        dn_rr = over("dn_rr", [P, 8, T], "xb", 8192)
        dn_s8 = at("dn_s8", [P, T], F32)
        gt, gc, eg, nbeg = small[:, 0:32], small[:, 32:48], small[:, 48:64], small[:, 64:80]
        ea, rw_mid, fac, omka = small[:, 80:81], small[:, 81:97], small[:, 97:105], small[:, 105:113]
        al = small[0:DN_H, 113:115]
        rw_c = over("rw_c", [P, 16, 132], "work", 0)
        rw_ep = over("rw_ep", [P, 16, 132], "work", 8448)
        rw_em = over("rw_em", [P, 16, 132], "work", 16896)
        rw_nm = over("rw_nm", [P, 8, P], "work", 25344)
        rw_rh = over("rw_rh", [P, 4, RW_D], "work", 29440)
        rw_sa = [over(f"rw_sa{c}", [P, 4, RW_D], "work", 30464 + 1024 * c) for c in range(2)]
        rw_st = over("rw_st", [P, 2, RW_D], "work", 32512)
        rw_bt = over("rw_bt", [P, 8, P], "work", 0)
        rw_kt = over("rw_kt", [P, 8, P], "work", 4096)
        rw_vt = over("rw_vt", [P, 8, 2, P], "work", 8192)
        rw_x = over("rw_x", [P, 8, P], "work", 16384)
        rw_xt = over("rw_xt", [P, 8, P], "work", 20480)
        rw_a = over("rw_a", [P, 8, T], "xa", 0)
        rw_kk = over("rw_kk", [P, 8, T], "xa", 8192)
        rw_mat = {n: over("rw_" + n, [P, 8, P], "xa", 16384 + 4096 * i) for i, n in enumerate(("ba", "ka", "br", "kr"))}
        rw_lw = over("rw_lw", [P, 1024], "xa", 16384)
        rw_g2 = over("rw_g2", [P, 1024], "xa", 20480)
        rw_bn = over("rw_bn", [P, 8, T], "xb", 16384)
        rw_d = over("rw_d", [P, 8, T], "xb", 16384 + 8192)
        rw_tt = over("rw_tt", [P, 8, P], "xb", 16384 + 8192)
        mem = over("mem", [P, DT, T], "work", 16 * COLS * 4)
        xs = over("xs", [P, 8, T], "work", 16 * COLS * 4)
        xp = over("xp", [P, 8, T], "work", 16 * COLS * 4 + 8192)
        xv = over("xv", [P, 4, 2, P], "work", 16 * COLS * 4 + 16384)
        xm = small[:, 120:136]

        inv_pe = [x + s_ for l in range(LEVELS) for x in ([f"t{l}", f"u{l}"] if l else ["t0"]) for s_ in "ab"]
        inv_dve = ["m0a", "m0b", "m1a", "u0a", "m1b", "u0b"]
        for l in range(1, LEVELS):
            inv_dve += ([f"m{l + 1}a", f"m{l + 1}b"] if l + 1 < LEVELS else []) + [f"u{l}a", f"u{l}b"]
        inv_act = [f"t{l}{s_}" for l in range(1, LEVELS) for s_ in "ab"]
        FOUR = {"a": (0, slice(0, 4)), "b": (1, slice(4, 8))}
        bank4 = lambda n: ps[n].rearrange("p (b c) -> p b c", b=4)

        def inverse_pe(pe, S, r, nm, x, xt, tt):
            for l in range(LEVELS):
                for s_, (n, four) in FOUR.items():
                    S.dve.wait(pe, f"m{l}{s_}", r)
                    if l:
                        S.dve.wait(pe, f"u{l - 1}{s_}", r)
                    for m in range(4):
                        ins = nc.tensor.matmul(bank4(n)[:, m], lhsT=nm[:, 4 * n + m],
                                               rhs=x[:, 4 * n + m] if l else const("ident"), start=True, stop=True)
                    S.pe.done(ins, f"t{l}{s_}", r)
                yield
                if not l:
                    continue
                for s_, (n, four) in FOUR.items():
                    S.act.wait(pe, f"t{l}{s_}", r)
                    for m in range(4 * n, 4 * n + 4):
                        if l + 1 < LEVELS:
                            nc.tensor.matmul(bank4(n)[:, m % 4], lhsT=xt[:, m], rhs=tt[:, m], start=True, stop=True)
                        ins = nc.tensor.matmul(bank4(2 + n)[:, m % 4], lhsT=tt[:, m], rhs=xt[:, m], start=True, stop=True)
                    S.pe.done(ins, f"u{l}{s_}", r)
                yield

        def inverse_act(act, S, r, tt):
            yield
            for l in range(1, LEVELS):
                for s_, (n, four) in FOUR.items():
                    S.pe.wait(act, f"t{l}{s_}", r)
                    if l > 1:
                        S.pe.wait(act, f"u{l - 1}{s_}", r)
                    S.act.done(nc.scalar.activation(tt[:, four], bank4(n), ACT.Copy), f"t{l}{s_}", r)
                yield
                yield

        def inverse_dve(dve, S, r, n_, nm, x, xt):
            mask = lambda l: masks[:, l, None, :].to_broadcast([P, 4, P])
            eye = const("ident")[:, None, :].to_broadcast([P, 4, P])
            for s_, (n, four) in FOUR.items():
                S.dve.done(nc.vector.tensor_tensor(nm[:, four], n_[:, four], mask(0), ALU.mult), f"m0{s_}", r)
            for l in range(LEVELS):
                for s_, (n, four) in FOUR.items():
                    if not l:
                        S.dve.wait(dve, f"m0{s_}", r)
                        dve_link(nc.vector.tensor_tensor(xt[:, four], eye, nm[:, four], ALU.subtract))
                    S.pe.wait(dve, f"t{l}{s_}", r)
                    if l + 1 < LEVELS:
                        S.dve.done(nc.vector.tensor_tensor(nm[:, four], n_[:, four], mask(l + 1), ALU.mult),
                                   f"m{l + 1}{s_}", r)
                    if not l:
                        S.dve.done(nc.vector.tensor_tensor(x[:, four], eye, bank4(n), ALU.subtract), f"u0{s_}", r)
                yield
                if not l:
                    continue
                for s_, (n, four) in FOUR.items():
                    S.dve.wait(dve, f"u{l - 1}{s_}", r)
                    S.pe.wait(dve, f"u{l}{s_}", r)
                    if l + 1 < LEVELS:
                        nc.vector.tensor_tensor(x[:, four], x[:, four], bank4(n), ALU.subtract)
                    S.dve.done(nc.vector.tensor_tensor(xt[:, four], xt[:, four], bank4(2 + n), ALU.subtract),
                               f"u{l}{s_}", r)
                yield

        class Trio:

            def __init__(self, name, pe, dve, act):
                self.pe, self.dve, self.act = (Steps(sem(f"{name}_{e}"), x) for e, x in
                                               (("pe", pe), ("dve", dve), ("act", act)))

        dn_acc, dn_sig, dn_silu = sem("dn_acc"), sem("dn_sig"), sem("dn_silu")

        def dn_conv_dve(dve, m):
            if m >= 1:
                pair = slice(2 * (m - 1), 2 * m)
                dve.wait_ge(dn_sig, m)
                if m <= 12:
                    nc.vector.tensor_tensor(work[:, pair, PAD:COLS], work[:, pair, PAD:COLS], dnc[:, pair],
                                            ALU.mult).then_inc(dn_silu, 1)
                else:
                    nc.vector.tensor_tensor(work[:, pair, PAD:COLS], work[:, pair, PAD:COLS],
                                            dnc[:, 2 * (m - 13):2 * (m - 12)], ALU.mult).then_inc(dn_silu, 1)
            if m < 12:
                dve.wait_ge(evacuated, g_dn.b0 + m + 3)
                for j in range(4):
                    for c in (2 * m, 2 * m + 1):
                        x = work[:, c, PAD - 3 + j:PAD - 3 + j + T]
                        if j == 0:
                            ins = nc.vector.tensor_scalar(dnc[:, c], x, v2("dn_conv_w_2", c), None, ALU.mult)
                        else:
                            ins = nc.vector.scalar_tensor_tensor(out=dnc[:, c], in0=x, scalar=v2("dn_conv_w_2", 24 * j + c),
                                                                 in1=dnc[:, c], op0=ALU.mult, op1=ALU.add)
                        if j < 3:
                            seq["dve"] += 1
                            ins.then_inc(dve_seq, 1)
                    if j < 3:
                        dve.wait_ge(dve_seq, seq["dve"])
                ins.then_inc(dn_acc, 1)

        def dn_conv_act(act, m):
            if m < 12:
                act.wait_ge(dn_acc, m + 1)
                pair = slice(2 * m, 2 * m + 2)
                nc.scalar.activation(work[:, pair, PAD:COLS], dnc[:, pair], ACT.Sigmoid).then_inc(dn_sig, 1)
            else:
                act.wait_ge(evacuated, g_dn.b0 + m + 3)
                act.wait_ge(dn_silu, m - 11)
                pair = slice(2 * m, 2 * m + 2)
                nc.scalar.activation(dnc[:, 2 * (m - 12):2 * (m - 11)], work[:, pair, PAD:COLS],
                                     ACT.Sigmoid).then_inc(dn_sig, 1)

        L2 = Trio("l2", ["sum"], ["done"], ["sq", "root"])
        GT = Trio("gates2", ["t", "gc"], ["dt", "soft", "g", "t", "gc", "nbeg"], ["beta", "ln", "ea", "eg"])

        def l2_pe(pe, m):
            h = m - 9
            if 0 <= h < DN_H:
                L2.act.wait(pe, "sq", h)
                if h >= 2:
                    L2.act.wait(pe, "root", h - 2)
                L2.pe.done(nc.tensor.matmul(ps[h % 2], lhsT=const("ones"), rhs=sq[:, :, :].rearrange("p a b -> p (a b)"),
                                            start=True, stop=True), "sum", h)

        def l2_act(act, m):
            h = m - 9
            if 0 <= h < DN_H:
                L2.pe.wait(act, "sum", h)
                if h >= 2:
                    L2.dve.wait(act, "done", h - 2)
                act_link(nc.scalar.activation(dn_rn[:, h % 2], ps[h % 2], ACT.Ln, bias=EPS))
                L2.act.done(nc.scalar.activation(dn_rn[:, h % 2], dn_rn[:, h % 2], ACT.Exp, scale=-0.5), "root", h)
            h = m - 8
            if 0 <= h < DN_H:
                act.wait_ge(dn_silu, 8)
                L2.act.done(nc.scalar.activation(sq[:, :, :], work[:, DQ + h:DQ + h + 9:8, PAD:COLS], ACT.Square), "sq", h)

        def l2_dve(dve, m):
            h = m - 9
            if 0 <= h < DN_H:
                L2.act.wait(dve, "root", h)
                dve.wait_ge(dn_silu, 8)
                q, k = (work[:, t + h, PAD:COLS] for t in (DQ, DK))
                nc.vector.scalar_tensor_tensor(out=q, in0=q, scalar=128 ** -0.5, in1=dn_rn[:, h % 2, 0:T],
                                               op0=ALU.mult, op1=ALU.mult)
                L2.dve.done(nc.vector.tensor_tensor(k, k, dn_rn[:, h % 2, T:2 * T], ALU.mult), "done", h)

        ga, gb, s8 = work[0:DN_H, GA, PAD:COLS], work[0:DN_H, GB, PAD:COLS], dn_s8[0:DN_H, :]

        def gates_act(act):
            blocks_out(act, g_gab)
            act.wait_ge(masks_in, 32)
            GT.act.done(nc.scalar.activation(gb, gb, ACT.Sigmoid), "beta")
            GT.dve.wait(act, "dt")
            act_link(nc.scalar.activation(s8, ga, ACT.Abs))
            act_link(nc.scalar.activation(s8, s8, ACT.Exp, scale=-1.0))
            GT.act.done(nc.scalar.activation(s8, s8, ACT.Ln, bias=1.0), "ln")
            GT.act.done(nc.scalar.activation(ea[0:DN_H, :], al[:, 0:1], ACT.Exp), "ea")
            yield
            yield
            GT.pe.wait(act, "gc")
            GT.act.done(nc.scalar.activation(eg, ps[3][:, 0:16], ACT.Exp), "eg")
            yield

        def gates_dve(dve):
            blocks_out(dve, g_gab)
            dve.wait_ge(masks_in, 32)
            GT.dve.done(nc.vector.tensor_scalar(ga, ga, al[:, 1:2], None, ALU.add), "dt")
            GT.act.wait(dve, "ln")
            GT.dve.done(nc.vector.scalar_tensor_tensor(out=s8, in0=ga, scalar=0.0, in1=s8, op0=ALU.max, op1=ALU.add), "soft")
            GT.dve.wait(dve, "soft")
            GT.act.wait(dve, "ea")
            GT.dve.done(nc.vector.tensor_scalar(s8, s8, ea[0:DN_H, :], -1.0, ALU.mult, ALU.mult), "g")
            yield
            GT.pe.wait(dve, "t")
            GT.dve.done(nc.vector.tensor_copy(gt, ps[2][:, 0:32]), "t")
            yield
            GT.pe.wait(dve, "gc")
            GT.act.wait(dve, "eg")
            GT.dve.done(nc.vector.tensor_copy(gc, ps[3][:, 0:16]), "gc")
            GT.dve.wait(dve, "gc")
            GT.dve.done(nc.vector.scalar_tensor_tensor(out=nbeg, in0=gt[:, 16:32], scalar=-1.0, in1=eg, op0=ALU.mult,
                                                       op1=ALU.mult), "nbeg")
            yield

        def gates_pe(pe):
            yield
            GT.dve.wait(pe, "g")
            GT.act.wait(pe, "beta")
            for c in range(2):
                for n, x in enumerate((s8, gb)):
                    ins = nc.tensor.transpose(ps[2][:, 16 * n + 8 * c:16 * n + 8 * c + 8], x[:, c * P:(c + 1) * P],
                                              const("ident")[0:DN_H, 0:DN_H])
            GT.pe.done(ins, "t")
            yield
            GT.dve.wait(pe, "t")
            GT.pe.done(nc.tensor.matmul(ps[3][:, 0:16], lhsT=const("incl"), rhs=gt[:, 0:16], start=True, stop=True), "gc")
            yield

        DN = Trio("dn",
                  ["row", "kk", "kq", "v", "k"] + inv_pe + ["v0", "s1", "m1", "v1", "o"],
                  ["min", "mask", "n", "n2", "attn", "qg"] + inv_dve + ["rhs1", "o"],
                  ["e", "eq", "v", "k"] + inv_act + ["v0", "s1", "v1"])
        quad = lambda n: p4[:, n:n + 2, :].rearrange("p a (b c) -> p (a b) c", b=4)
        units = [(hh, c) for hh in range(4) for c in range(2)]

        def chunk(tile, c):
            return work[:, tile, PAD + c * P:PAD + (c + 1) * P]

        def dn_pe(pe, r):
            H = 4 * r
            q2 = lambda base, n: p4[:, base + n // 4, (n % 4) * P:(n % 4 + 1) * P]
            if r:
                DN.dve.wait(pe, "o", r - 1)
            else:
                GT.dve.wait(pe, "nbeg")
            for n, (hh, c) in enumerate(units):
                col = gt[:, 8 * c + H + hh:8 * c + H + hh + 1]
                nc.tensor.matmul(q2(0, n), lhsT=col.to_broadcast([P, P]), rhs=const("incl"), start=True, stop=True)
            for n, (hh, c) in enumerate(units):
                col = gt[:, 16 + 8 * c + H + hh:16 + 8 * c + H + hh + 1]
                ins = nc.tensor.matmul(q2(2, n), lhsT=col.to_broadcast([P, P]), rhs=const("ident"), start=True, stop=True)
            DN.pe.done(ins, "row", r)
            yield
            DN.dve.wait(pe, "min", r)
            DN.act.wait(pe, "eq", r)
            for n, (hh, c) in enumerate(units):
                k = chunk(DK + H + hh, c)
                ins = nc.tensor.matmul(q2(0, n), lhsT=k, rhs=k, start=True, stop=True)
            DN.pe.done(ins, "kk", r)
            yield
            DN.dve.wait(pe, "n", r)
            for n, (hh, c) in enumerate(units):
                ins = nc.tensor.matmul(q2(0, n), lhsT=chunk(DK + H + hh, c), rhs=chunk(DQ + H + hh, c), start=True, stop=True)
            DN.pe.done(ins, "kq", r)
            yield
            DN.dve.wait(pe, "n2", r)
            for n, (hh, c) in enumerate(units):
                ins = nc.tensor.transpose(q2(2, n), chunk(DV + H + hh, c), const("ident"))
            DN.pe.done(ins, "v", r)
            DN.dve.wait(pe, "attn", r)
            for hh in range(4):
                ins = nc.tensor.transpose(q2(0, hh), chunk(DK + H + hh, 0), const("ident"))
            DN.pe.done(ins, "k", r)
            yield
            DN.act.wait(pe, "k", r)
            yield from inverse_pe(pe, DN, r, dn_nm, dn_x, dn_xt, dn_tt)
            DN.dve.wait(pe, f"u{LEVELS - 1}b", r)
            for hh in range(4):
                ins = nc.tensor.matmul(q2(0, hh), lhsT=dn_xt[:, 2 * hh], rhs=dn_v[:, 2 * hh], start=True, stop=True)
            DN.pe.done(ins, "v0", r)
            yield
            DN.act.wait(pe, "v0", r)
            for hh in range(4):
                ins = nc.tensor.matmul(q2(1, hh), lhsT=dn_k0[:, hh], rhs=dn_v0[:, hh], start=True, stop=True)
            DN.pe.done(ins, "s1", r)
            yield
            DN.act.wait(pe, "s1", r)
            for hh in range(4):
                ins = nc.tensor.matmul(q2(2, hh), lhsT=chunk(DK + H + hh, 1), rhs=dn_s1[:, hh], start=True, stop=True)
            DN.pe.done(ins, "m1", r)
            yield
            DN.dve.wait(pe, "rhs1", r)
            for hh in range(4):
                ins = nc.tensor.matmul(q2(3, hh), lhsT=dn_xt[:, 2 * hh + 1], rhs=dn_v[:, 2 * hh + 1], start=True, stop=True)
            DN.pe.done(ins, "v1", r)
            yield
            DN.act.wait(pe, "v1", r)
            for hh in range(4):
                o = lambda c: p4[:, hh // 2, (hh % 2) * T + c * P:(hh % 2) * T + (c + 1) * P]
                nc.tensor.matmul(o(0), lhsT=dn_v0[:, hh], rhs=dn_at_[:, 2 * hh], start=True, stop=True)
                nc.tensor.matmul(o(1), lhsT=dn_s1[:, hh], rhs=chunk(DQ + H + hh, 1), start=True, stop=False)
                ins = nc.tensor.matmul(o(1), lhsT=dn_v1[:, hh], rhs=dn_at_[:, 2 * hh + 1], start=False, stop=True)
            DN.pe.done(ins, "o", r)
            yield

        def dn_act(act, r):
            H = 4 * r
            DN.dve.wait(act, "min", r)
            DN.act.done(nc.scalar.activation(dn_e[:, :, :], dn_e[:, :, :], ACT.Exp), "e", r)
            DN.act.done(nc.scalar.activation(dn_eq[:, :, :], quad(0)[:, 1:8:2, :], ACT.Exp), "eq", r)
            yield
            yield
            yield
            DN.pe.wait(act, "v", r)
            for n, (hh, c) in enumerate(units):
                beta = gt[:, 16 + 8 * c + H + hh:16 + 8 * c + H + hh + 1]
                ins = nc.scalar.activation(dn_v[:, n], quad(2)[:, n], ACT.Copy, scale=beta)
            DN.act.done(ins, "v", r)
            DN.pe.wait(act, "k", r)
            for hh in range(4):
                ins = nc.scalar.activation(dn_k0[:, hh], quad(0)[:, hh], ACT.Copy, scale=dn_e[:, 2 * hh, P - 1:P])
            DN.act.done(ins, "k", r)
            yield
            yield from inverse_act(act, DN, r, dn_tt)
            four = lambda n: ps[n].rearrange("p (b c) -> p b c", b=4)
            for name, bank, to in (("v0", 0, dn_v0), ("s1", 1, dn_s1), ("v1", 3, dn_v1)):
                DN.pe.wait(act, name, r)
                DN.act.done(nc.scalar.activation(to[:, :, :], four(bank), ACT.Copy), name, r)
                yield
                if name == "s1":
                    yield
            yield

        def dn_dve(dve, r):
            H = 4 * r
            DN.pe.wait(dve, "row", r)
            for n, (hh, c) in enumerate(units):
                col = gc[:, 8 * c + H + hh:8 * c + H + hh + 1]
                ins = nc.vector.tensor_scalar(dn_e[:, n], quad(0)[:, n], col, 0.0, ALU.subtract, ALU.min)
            DN.dve.done(ins, "min", r)
            DN.act.wait(dve, "e", r)
            DN.dve.done(nc.vector.tensor_tensor(dn_e[:, :, :], dn_e[:, :, :],
                                                const("incl")[:, None, :].to_broadcast([P, 8, P]), ALU.mult), "mask", r)
            yield
            DN.dve.wait(dve, "mask", r)
            DN.pe.wait(dve, "kk", r)
            DN.dve.done(nc.vector.tensor_tensor(dn_n[:, :, :], quad(0), dn_e[:, :, :], ALU.mult), "n", r)
            DN.dve.wait(dve, "n", r)
            DN.dve.done(nc.vector.tensor_tensor(dn_n[:, :, :], dn_n[:, :, :], quad(2), ALU.mult), "n2", r)
            yield
            DN.pe.wait(dve, "kq", r)
            DN.dve.done(nc.vector.tensor_tensor(dn_at_[:, :, :], quad(0), dn_e[:, :, :], ALU.mult), "attn", r)
            DN.act.wait(dve, "eq", r)
            q1 = work[:, DQ + H:DQ + H + 4, PAD + P:COLS]
            DN.dve.done(nc.vector.tensor_tensor(q1, q1, dn_eq[:, :, :], ALU.mult), "qg", r)
            DN.dve.wait(dve, "qg", r)
            yield
            yield from inverse_dve(dve, DN, r, dn_n, dn_nm, dn_x, dn_xt)
            yield
            yield
            DN.pe.wait(dve, "m1", r)
            for hh in range(4):
                ins = nc.vector.scalar_tensor_tensor(out=dn_v[:, 2 * hh + 1], in0=quad(2)[:, hh],
                                                     scalar=nbeg[:, 8 + H + hh:8 + H + hh + 1], in1=dn_v[:, 2 * hh + 1],
                                                     op0=ALU.mult, op1=ALU.add)
            DN.dve.done(ins, "rhs1", r)
            yield
            yield
            DN.pe.wait(dve, "o", r)
            DN.dve.done(nc.vector.tensor_copy(work[:, DQ + H:DQ + H + 4, PAD:COLS],
                                              p4[:, 0:2, :].rearrange("p a (b c) -> p (a b) c", b=2)), "o", r)
            yield

        DF = Trio("dnf", ["sum"], ["o1", "o2", "lo"], ["sq", "ln", "root", "hi"])
        all4 = p4[:, :, :].rearrange("p a (b c) -> p (a b) c", b=2)
        dn_o = work[:, DQ:DQ + 8, PAD:COLS]

        def eight(ones, src):
            for j in range(8):
                ins = nc.tensor.matmul(all4[:, j], lhsT=const(ones), rhs=src[:, j], start=True, stop=True)
            return ins

        def dnf_pe(pe):
            yield
            DF.act.wait(pe, "sq")
            DF.pe.done(eight("ones", dn_sq), "sum")
            yield

        def dnf_act(act):
            DN.dve.wait(act, "o", 1)
            DF.act.done(nc.scalar.activation(dn_sq[:, :, :], dn_o, ACT.Square), "sq")
            yield
            DF.pe.wait(act, "sum")
            DF.act.done(nc.scalar.activation(dn_rr[:, :, :], all4, ACT.Ln, scale=1.0 / 128, bias=EPS), "ln")
            DF.act.wait(act, "ln")
            DF.act.done(nc.scalar.activation(dn_rr[:, :, :], dn_rr[:, :, :], ACT.Exp, scale=-0.5), "root")
            yield
            DF.dve.wait(act, "o2")
            DF.act.done(nc.scalar.activation(xb[:, 0:8, 0:T], dn_o, ACT.Copy), "hi")

        def dnf_dve(dve):
            yield
            DF.act.wait(dve, "root")
            DN.dve.wait(dve, "o", 1)
            DF.dve.done(nc.vector.scalar_tensor_tensor(out=dn_o, in0=dn_o, scalar=v2("dn_norm_w_2"), in1=dn_rr[:, :, :],
                                                       op0=ALU.mult, op1=ALU.mult), "o1")
            yield
            DF.dve.wait(dve, "o1")
            DF.dve.done(nc.vector.tensor_tensor(dn_o, dn_o, work[:, DZ:DZ + 8, PAD:COLS], ALU.mult), "o2")
            DF.act.wait(dve, "hi")
            DF.dve.done(nc.vector.tensor_tensor(xb[:, 0:8, T:2 * T], dn_o, xb[:, 0:8, 0:T].bitcast(F32), ALU.subtract), "lo")

        def dn_core(eng, gates, rounds, final):
            yield from gates(eng)
            for r in range(2):
                yield from rounds(eng, r)
            yield from final(eng)

        def step_of(gen):
            return lambda: next(gen, None)

        def rest_of(gen):
            for _ in gen:
                pass

        lots = [(RR, 8), (RK, 8), (RV, 8), (RL, 2)]
        rw_r, rw_k, rw_v = (work[:, t:t + 8, PAD:COLS] for t in (RR, RK, RV))
        RP = Trio("rwp", ["w", "a", "kk", "bonus", "t0", "t1", "t2", "t3"],
                  ["shift", "lora", "scan", "kkr", "kk", "k", "bonus", "bn", "sc", "rho", "alpha", "beta", "kappa", "t1", "t3"],
                  ["tanh", "w", "a", "sq", "root", "ep", "em", "t0", "t2"])
        lora_in = sem("lora_in")
        rw_big = [(0, 63)]
        C = lambda x, a_, b_: x[:, :, a_:b_]
        ctok = lambda x, a_: x[:, :, a_:a_ + P].rearrange("p (j c) t -> p j c t", c=2)
        jc = lambda x: x.rearrange("p j (c t) -> p j c t", c=2)

        def rwp_pe(pe):
            pe.wait_ge(lora_in, 16 * 2)
            RP.act.wait(pe, "tanh")
            for j in range(8):
                ins = nc.tensor.matmul(all4[:, j], lhsT=rw_lw[0:64, j * P:(j + 1) * P],
                                       rhs=work[0:64, RL, PAD:COLS], start=True, stop=True)
            RP.pe.done(ins, "w")
            RP.act.wait(pe, "w")
            for j in range(8):
                ins = nc.tensor.matmul(all4[:, j], lhsT=rw_lw[64:P, j * P:(j + 1) * P],
                                       rhs=work[64:P, RL, PAD:COLS], start=True, stop=True)
            RP.pe.done(ins, "a")
            RP.act.wait(pe, "sq")
            RP.pe.done(eight("ones_head", rw_d), "kk")
            RP.dve.wait(pe, "bonus")
            RP.act.wait(pe, "root")
            RP.pe.done(eight("ones_head", rw_d), "bonus")
            RP.dve.wait(pe, "beta")
            RP.dve.wait(pe, "kappa")
            for n, src in enumerate((rw_a, work[:, RK:RK + 8, PAD:COLS])):
                for j in range(8):
                    ins = nc.tensor.transpose(p4[:, 2 * n + j // 4, (j % 4) * P:(j % 4 + 1) * P], src[:, j, 0:P],
                                              const("ident"))
                RP.pe.done(ins, f"t{n}")
            for n in range(2):
                if n == 0:
                    RP.act.wait(pe, "t0")
                else:
                    RP.dve.wait(pe, "t1")
                for j in range(8):
                    ins = nc.tensor.transpose(p4[:, 2 * n + j // 4, (j % 4) * P:(j % 4 + 1) * P],
                                              chunk(RV + 4 * n + j // 2, j % 2), const("ident"))
                RP.pe.done(ins, f"t{2 + n}")

        def rwp_act(act):
            RP.dve.wait(act, "lora")
            act_link(nc.scalar.activation(work[0:64, RL, PAD:COLS], work[0:64, RL, PAD:COLS], ACT.Tanh))
            RP.act.done(nc.scalar.activation(work[:, RG, PAD:COLS], work[:, RG, PAD:COLS], ACT.Sigmoid), "tanh")
            RP.pe.wait(act, "w")
            for j in range(8):
                ins = nc.scalar.activation(rw_c[:, 2 * j:2 * j + 2, 4:132], all4[:, j].rearrange("p (c t) -> p c t", c=2),
                                           ACT.Sigmoid, bias=v2("rw_w0_2", j))
            RP.act.done(ins, "w")
            RP.pe.wait(act, "a")
            for j in range(8):
                ins = nc.scalar.activation(rw_a[:, j], all4[:, j], ACT.Sigmoid, bias=v2("rw_a0_2", j))
            RP.act.done(ins, "a")
            RP.dve.wait(act, "kkr")
            RP.act.done(nc.scalar.activation(rw_d[:, :, :], rw_kk[:, :, :], ACT.Square), "sq")
            RP.pe.wait(act, "kk")
            RP.act.done(nc.scalar.activation(rw_ep_flat, all4, ACT.Sqrt), "root")
            RP.dve.wait(act, "sc")
            RP.act.done(nc.scalar.activation(C(rw_ep, 3, 132), C(rw_c, 3, 132), ACT.Exp, scale=-RW_DECAY), "ep")
            RP.act.done(nc.scalar.activation(C(rw_em, 3, 132), C(rw_c, 3, 132), ACT.Exp, scale=RW_DECAY), "em")
            RP.pe.wait(act, "t0")
            RP.dve.wait(act, "kappa")
            RP.act.done(nc.scalar.activation(rw_bt[:, :, :], quad(0), ACT.Copy), "t0")
            RP.pe.wait(act, "t2")
            RP.act.done(nc.scalar.activation(rw_vt[:, 0:4].rearrange("p j c t -> p (j c) t"), quad(0), ACT.Copy), "t2")

        rw_ep_flat = over("rw_root", [P, 8, T], "work", 8448)[:, :, :]

        def rwp_dve(dve):
            blocks_out(dve, g_rw)
            for i, (t0, n) in enumerate(lots):
                if i:
                    dve.wait_ge(dve_seq, seq["dve"])
                now, before = work[:, t0:t0 + n, PAD:COLS], work[:, t0:t0 + n, PAD - 1:COLS - 1]
                dve_link(nc.vector.tensor_tensor(rw_d[:, 0:n], before, now, ALU.subtract))
                for j in range(n):
                    x = work[:, t0 + j, PAD:COLS]
                    ins = nc.vector.scalar_tensor_tensor(out=x, in0=rw_d[:, j], scalar=v2("rw_mu_2", t0 - RR + j), in1=x,
                                                         op0=ALU.mult, op1=ALU.add)
                if i < 3:
                    seq["dve"] += 1
                    ins.then_inc(dve_seq, 1)
            RP.dve.done(ins, "shift")
            RP.dve.done(nc.vector.memset(rw_c[:, :, 3:4], 0.0), "lora")
            RP.dve.wait(dve, "lora")
            RP.act.wait(dve, "w")
            for c in range(16):
                ins = nc.vector.tensor_tensor_scan(rw_c[:, c, 4:132], const("ones"), rw_c[:, c, 4:132], 0.0, ALU.mult,
                                                   ALU.add)
            RP.dve.done(ins, "scan")
            for j in range(8):
                ins = nc.vector.tensor_scalar(rw_kk[:, j], work[:, RK + j, PAD:COLS], v2("rw_k_k_2", j), None, ALU.mult)
            RP.dve.done(ins, "kkr")
            RP.act.wait(dve, "root")
            dve_link(nc.vector.tensor_scalar(rw_ep_flat, rw_ep_flat, 1e-12, None, ALU.max))
            dve_link(nc.vector.reciprocal(rw_ep_flat, rw_ep_flat))
            RP.dve.wait(dve, "kkr")
            RP.dve.done(nc.vector.tensor_tensor(rw_kk[:, :, :], rw_kk[:, :, :], rw_ep_flat, ALU.mult), "kk")
            RP.act.wait(dve, "a")
            dve_link(nc.vector.tensor_scalar(omka, vec[:, NV1 + V2["rw_k_a_2"]:NV1 + V2["rw_k_a_2"] + 8], -1.0, 1.0,
                                             ALU.mult, ALU.add))
            for j in range(8):
                ins = nc.vector.tensor_scalar(rw_d[:, j], rw_a[:, j], v2("rw_k_a_2", j), omka[:, j:j + 1], ALU.mult,
                                              ALU.add)
            dve_link(ins)
            RP.dve.done(nc.vector.tensor_tensor(rw_k, rw_k, rw_d[:, :, :], ALU.mult), "k")
            RP.dve.wait(dve, "k")
            for j in range(8):
                ins = nc.vector.scalar_tensor_tensor(out=rw_d[:, j], in0=work[:, RR + j, PAD:COLS],
                                                     scalar=v2("rw_r_k_2", j), in1=work[:, RK + j, PAD:COLS],
                                                     op0=ALU.mult, op1=ALU.mult)
            RP.dve.done(ins, "bonus")
            RP.pe.wait(dve, "bonus")
            RP.dve.done(nc.vector.tensor_tensor(rw_bn[:, :, :], all4, rw_v, ALU.mult), "bn")
            RP.dve.wait(dve, "scan")
            dve_link(nc.vector.tensor_copy(rw_mid, rw_c[:, :, 67]))
            RP.dve.wait(dve, "kk")
            RP.dve.done(nc.vector.tensor_tensor(C(rw_c, 3, 132), C(rw_c, 3, 132),
                                                rw_mid[:, :, None].to_broadcast([P, 16, 129]), ALU.subtract), "sc")
            RP.act.wait(dve, "ep")
            RP.dve.done(nc.vector.tensor_tensor(jc(rw_r), jc(rw_r), ctok(rw_ep, 4), ALU.mult), "rho")
            dve_link(nc.vector.tensor_tensor(rw_a[:, :, :], rw_a[:, :, :], rw_kk[:, :, :], ALU.mult))
            RP.dve.done(nc.vector.tensor_tensor(jc(rw_kk[:, :, :]), jc(rw_kk[:, :, :]), ctok(rw_ep, 3), ALU.mult), "alpha")
            RP.act.wait(dve, "em")
            RP.dve.done(nc.vector.tensor_tensor(jc(rw_a[:, :, :]), jc(rw_a[:, :, :]), ctok(rw_em, 4), ALU.mult), "beta")
            dve_link(nc.vector.tensor_tensor(fac, rw_ep[:, 0:16:2, 131], rw_em[:, 1:16:2, 3], ALU.mult))
            RP.dve.done(nc.vector.tensor_tensor(jc(rw_k), jc(rw_k), ctok(rw_em, 4), ALU.mult), "kappa")
            RP.dve.wait(dve, "kappa")
            RP.pe.wait(dve, "t1")
            RP.dve.done(nc.vector.tensor_copy(rw_kt[:, :, :], quad(2)), "t1")
            RP.pe.wait(dve, "t3")
            RP.dve.done(nc.vector.tensor_copy(rw_vt[:, 4:8].rearrange("p j c t -> p (j c) t"), quad(2)), "t3")

        MATS = [("ba", rw_a, rw_kk), ("ka", work[:, RK:RK + 8, PAD:COLS], rw_kk), ("br", rw_a, work[:, RR:RR + 8, PAD:COLS]),
                ("kr", work[:, RK:RK + 8, PAD:COLS], work[:, RR:RR + 8, PAD:COLS])]
        RW = Trio("rw", ["ba", "ka", "br", "kr"] + inv_pe + ["r0", "sa0", "st", "r1", "sa1", "y"],
                  ["ka", "kr"] + inv_dve + ["y"],
                  ["ba", "br"] + inv_act + ["r0", "sa0", "st", "r1", "sa1"])

        unit = lambda hh, c: 4 * (hh % 2) + 2 * (hh // 2) + c
        head = lambda hh: 2 * (hh % 2) + hh // 2

        def rw_pe(pe, r):
            if r:
                RW.dve.wait(pe, "y", r - 1)
            for i, (name, left, right) in enumerate(MATS):
                if name == "br":
                    RW.act.wait(pe, "ba", r)
                if name == "kr":
                    RW.dve.wait(pe, "ka", r)
                base = 2 * (i % 2)
                for hh, c in units:
                    n, j, hb = unit(hh, c), 2 * r + hh // 2, 64 * (hh % 2)
                    L, R = left[hb:hb + 64, j, c * P:(c + 1) * P], right[hb:hb + 64, j, c * P:(c + 1) * P]
                    bank, o = base + n // 4, (n % 4) * P
                    nc.tensor.matmul(p4[0:64, bank, o:o + P], lhsT=L[:, 0:64], rhs=R, start=True, stop=True)
                    ins = nc.tensor.matmul(p4[64:P, bank, o + 64:o + P], lhsT=L[:, 64:P], rhs=R[:, 64:P], start=True,
                                           stop=True)
                RW.pe.done(ins, name, r)
            RW.act.wait(pe, "br", r)
            rest_of(inverse_pe(pe, RW, r, rw_nm, rw_x, rw_xt, rw_tt))
            RW.dve.wait(pe, f"u{LEVELS - 1}b", r)
            ka, br, kr = rw_mat["ka"], rw_mat["br"], rw_mat["kr"]
            place = lambda hh: (2 * r + hh // 2, 64 * (hh % 2))
            vtok = lambda hh, c: rw_vt[:, 2 * r + hh // 2, c, 64 * (hh % 2):64 * (hh % 2) + 64]
            for hh in range(4):
                ins = nc.tensor.matmul(ps[2 * (hh % 2)][:, (hh // 2) * 64:(hh // 2 + 1) * 64], lhsT=ka[:, unit(hh, 0)], rhs=vtok(hh, 0), start=True,
                                       stop=True)
            RW.pe.done(ins, "r0", r)
            RW.act.wait(pe, "r0", r)
            for hh in range(4):
                ins = nc.tensor.matmul(ps[1][:, hh * 64:(hh + 1) * 64], lhsT=rw_xt[:, unit(hh, 0)], rhs=rw_rh[:, head(hh)], start=True,
                                       stop=True)
            RW.pe.done(ins, "sa0", r)
            RW.act.wait(pe, "sa0", r)
            for hh in range(4):
                j, hb = place(hh)
                o = ps[2][hb:hb + 64, (hh // 2) * 64:(hh // 2) * 64 + 64]
                nc.tensor.matmul(o, lhsT=rw_bt[:, j, hb:hb + 64], rhs=rw_sa[0][:, hh], start=True, stop=False)
                ins = nc.tensor.matmul(o, lhsT=rw_kt[:, j, hb:hb + 64], rhs=vtok(hh, 0), start=False, stop=True)
            RW.pe.done(ins, "st", r)
            RW.act.wait(pe, "st", r)
            for hh in range(4):
                j, hb = place(hh)
                o = ps[2 * (hh % 2)][:, (hh // 2) * 64:(hh // 2 + 1) * 64]
                nc.tensor.matmul(o, lhsT=rw_kk[hb:hb + 64, j, P:T], rhs=rw_st[hb:hb + 64, hh // 2], start=True, stop=False)
                ins = nc.tensor.matmul(o, lhsT=ka[:, unit(hh, 1)], rhs=vtok(hh, 1), start=False, stop=True)
            RW.pe.done(ins, "r1", r)
            RW.act.wait(pe, "r1", r)
            for hh in range(4):
                ins = nc.tensor.matmul(ps[1][:, hh * 64:(hh + 1) * 64], lhsT=rw_xt[:, unit(hh, 1)], rhs=rw_rh[:, head(hh)],
                                       start=True, stop=True)
            RW.pe.done(ins, "sa1", r)
            RW.act.wait(pe, "sa1", r)
            for hh in range(4):
                j, hb = place(hh)
                for c in range(2):
                    o = ps[3][hb:hb + 64, (hh // 2) * T + c * P:(hh // 2) * T + (c + 1) * P]
                    if c:
                        nc.tensor.matmul(o, lhsT=rw_st[hb:hb + 64, hh // 2],
                                         rhs=work[hb:hb + 64, RR + j, PAD + P:COLS], start=True, stop=False)
                    nc.tensor.matmul(o, lhsT=rw_sa[c][:, hh], rhs=br[:, unit(hh, c)], start=(c == 0), stop=False)
                    ins = nc.tensor.matmul(o, lhsT=vtok(hh, c), rhs=kr[:, unit(hh, c)], start=False, stop=True)
            RW.pe.done(ins, "y", r)

        def quarter(eng_op, name, base, mask):
            m, q = rw_mat[name], quad(base)
            a1 = eng_op(m[0:64, :, :], q[0:64], mask, slice(0, 64), slice(0, P))
            return eng_op(m[64:P, :, 64:P], q[64:P, :, 64:P], mask, slice(64, P), slice(64, P))

        def rw_act(act, r):
            copy = lambda o, i, *_: nc.scalar.activation(o, i, ACT.Copy)
            RW.pe.wait(act, "ba", r)
            RW.act.done(quarter(copy, "ba", 0, None), "ba", r)
            RW.pe.wait(act, "br", r)
            RW.act.done(quarter(copy, "br", 0, None), "br", r)
            rest_of(inverse_act(act, RW, r, rw_tt))
            four = lambda n: ps[n][:, 0:T].rearrange("p (b c) -> p b c", b=4)
            for name, bank, to, scale in (("r0", 0, rw_rh, -1.0), ("sa0", 1, rw_sa[0], 1.0), ("st", 2, rw_st, None),
                                          ("r1", 0, rw_rh, -1.0), ("sa1", 1, rw_sa[1], 1.0)):
                RW.pe.wait(act, name, r)
                if name == "st":
                    for j in range(2):
                        ins = nc.scalar.activation(rw_st[:, j], ps[2][:, 64 * j:64 * j + 64], ACT.Copy,
                                                   scale=fac[:, 2 * r + j:2 * r + j + 1])
                elif scale < 0:
                    ins = nc.scalar.activation(to[:, :, :].rearrange("p (a b) c -> p a b c", a=2),
                                               p4[:, 0:4:2, 0:P].rearrange("p a (b c) -> p a b c", b=2), ACT.Copy, scale=scale)
                else:
                    ins = nc.scalar.activation(to[:, :, :], four(bank), ACT.Copy)
                RW.act.done(ins, name, r)

        def rw_dve(dve, r):
            if not r:
                for m in rw_mat.values():
                    ins = nc.vector.memset(m[64:P, :, 0:64], 0.0)
                dve_link(ins)
            masked = lambda name: (lambda o, i, mask, p_, c_: nc.vector.tensor_tensor(
                o, i, const(name)[p_, None, c_].to_broadcast([64, 8, c_.stop - c_.start]), ALU.mult))
            RW.pe.wait(dve, "ka", r)
            RW.dve.done(quarter(masked("before"), "ka", 2, None), "ka", r)
            RW.pe.wait(dve, "kr", r)
            RW.dve.done(quarter(masked("incl"), "kr", 2, None), "kr", r)
            RW.act.wait(dve, "br", r)
            br = rw_mat["br"]
            dve_link(nc.vector.tensor_tensor(br[:, :, :], br[:, :, :], const("incl")[:, None, :].to_broadcast([P, 8, P]),
                                             ALU.mult))
            rest_of(inverse_dve(dve, RW, r, rw_mat["ba"], rw_nm, rw_x, rw_xt))
            RW.pe.wait(dve, "y", r)
            RW.dve.done(nc.vector.tensor_copy(work[:, RR + 2 * r:RR + 2 * r + 2, PAD:COLS],
                                              ps[3].rearrange("p (j t) -> p j t", j=2)), "y", r)

        RN = Trio("rwn", ["mean", "var", "gate"], ["mid", "rr", "y1", "y2", "y3", "y4", "lo"], ["sq", "root", "hi"])

        def rwn_pe(pe):
            RW.dve.wait(pe, "y", 3)
            RN.pe.done(eight("ones_head", rw_r), "mean")
            RN.act.wait(pe, "sq")
            RN.pe.done(eight("ones_head", rw_d), "var")
            RN.act.wait(pe, "root")
            pe.wait_ge(lora_in, 16 * 3)
            for j in range(8):
                ins = nc.tensor.matmul(all4[:, j], lhsT=rw_g2[:, j * P:(j + 1) * P], rhs=work[:, RG, PAD:COLS], start=True,
                                       stop=True)
            RN.pe.done(ins, "gate")

        def rwn_act(act):
            RN.dve.wait(act, "mid")
            RN.act.done(nc.scalar.activation(rw_d[:, :, :], rw_r, ACT.Square), "sq")
            RN.pe.wait(act, "var")
            RN.act.done(nc.scalar.activation(rw_a[:, :, :], all4, ACT.Sqrt, scale=1.0 / RW_D, bias=const_eps(64e-5)), "root")
            RN.dve.wait(act, "y4")
            RN.act.done(nc.scalar.activation(xb[:, 8:16, 0:T], rw_r, ACT.Copy), "hi")

        def rwn_dve(dve):
            RN.pe.wait(dve, "mean")
            RN.dve.done(nc.vector.scalar_tensor_tensor(out=rw_r, in0=all4, scalar=-1.0 / RW_D, in1=rw_r, op0=ALU.mult,
                                                       op1=ALU.add), "mid")
            RN.act.wait(dve, "root")
            RN.dve.done(nc.vector.reciprocal(rw_a[:, :, :], rw_a[:, :, :]), "rr")
            RN.dve.wait(dve, "rr")
            RN.dve.done(nc.vector.tensor_tensor(rw_r, rw_r, rw_a[:, :, :], ALU.mult), "y1")
            RN.dve.wait(dve, "y1")
            for j in range(8):
                y = work[:, RR + j, PAD:COLS]
                ins = nc.vector.tensor_scalar(y, y, v2("rw_ln_w_2", j), v2("rw_ln_b_2", j), ALU.mult, ALU.add)
            RN.dve.done(ins, "y2")
            RN.dve.wait(dve, "y2")
            RN.dve.done(nc.vector.tensor_tensor(rw_r, rw_r, rw_bn[:, :, :], ALU.add), "y3")
            RN.dve.wait(dve, "y3")
            RN.pe.wait(dve, "gate")
            RN.dve.done(nc.vector.tensor_tensor(rw_r, rw_r, all4, ALU.mult), "y4")
            RN.act.wait(dve, "hi")
            RN.dve.done(nc.vector.tensor_tensor(xb[:, 8:16, T:2 * T], rw_r, xb[:, 8:16, 0:T].bitcast(F32), ALU.subtract),
                        "lo")

        XA_ = Trio("xat", ["s", "p", "v", "o"], ["max", "sub", "sum", "div", "p", "lo"], ["exp", "v", "hi"])
        xs4 = xs[:, :, :].rearrange("p (h m) k -> p h m k", m=2)

        def xat_pe(pe):
            blocks_out(pe, g_xq)
            for h in range(XA_H):
                for m in range(2):
                    ins = nc.tensor.matmul(all4[:, 2 * h + m], lhsT=chunk(8 + h, m), rhs=work[:, h, PAD:COLS], start=True,
                                           stop=True)
            XA_.pe.done(ins, "s")
            XA_.dve.wait(pe, "div")
            for kh in range(2):
                for h in range(XA_H):
                    for m in range(2):
                        ins = nc.tensor.transpose(all4[:, 4 * kh + h, m * P:(m + 1) * P], xs[:, 2 * h + m, kh * P:(kh + 1) * P],
                                                  const("ident"))
            XA_.pe.done(ins, "p")
            XA_.dve.wait(pe, "p")
            for n in range(8):
                ins = nc.tensor.transpose(quad(0)[:, n], chunk(4 + n // 2, n % 2), const("ident"))
            XA_.pe.done(ins, "v")
            XA_.act.wait(pe, "v")
            for h in range(XA_H):
                for kh in range(2):
                    ins = nc.tensor.matmul(all4[:, 4 + h], lhsT=xv[:, h, kh], rhs=xp[:, 4 * kh + h], start=(kh == 0),
                                           stop=(kh == 1))
            XA_.pe.done(ins, "o")

        def xat_act(act):
            XA_.dve.wait(act, "sub")
            XA_.act.done(nc.scalar.activation(xs[:, :, :], xs[:, :, :], ACT.Exp, scale=XA_D ** -0.5), "exp")
            XA_.pe.wait(act, "v")
            XA_.act.done(nc.scalar.activation(xv[:, :, :, :].rearrange("p h m d -> p (h m) d"), quad(0), ACT.Copy), "v")
            XA_.pe.wait(act, "o")
            XA_.act.done(nc.scalar.activation(xb[:, 0:4, 0:T], all4[:, 4:8], ACT.Copy), "hi")

        def xat_dve(dve):
            XA_.pe.wait(dve, "s")
            XA_.dve.done(nc.vector.tensor_reduce(xm[:, 0:8], all4, AX.X, ALU.max), "max")
            XA_.dve.wait(dve, "max")
            XA_.dve.done(nc.vector.tensor_tensor(xs[:, :, :], all4, xm[:, 0:8, None].to_broadcast([P, 8, T]), ALU.subtract),
                         "sub")
            XA_.act.wait(dve, "exp")
            XA_.dve.done(nc.vector.tensor_reduce(xm[:, 8:16], xs[:, :, :], AX.X, ALU.add), "sum")
            XA_.dve.wait(dve, "sum")
            dve_link(nc.vector.reciprocal(xm[:, 8:16], xm[:, 8:16]))
            XA_.dve.done(nc.vector.tensor_tensor(xs[:, :, :], xs[:, :, :], xm[:, 8:16, None].to_broadcast([P, 8, T]),
                                                 ALU.mult), "div")
            XA_.pe.wait(dve, "p")
            XA_.dve.done(nc.vector.tensor_copy(xp[:, :, :], all4), "p")
            XA_.act.wait(dve, "hi")
            XA_.dve.done(nc.vector.tensor_tensor(xb[:, 0:4, T:2 * T], all4[:, 4:8], xb[:, 0:4, 0:T].bitcast(F32),
                                                 ALU.subtract), "lo")

        block = ctx.enter_context(nc.Block())

        @block.sync
        def _(sp):
            sp.dma_start(resid[:, :, :], a["x"]).then_inc(resid_in, 16)
            sp.dma_start(cst[:, :, :], a["consts"]).then_inc(consts_in, 16)
            sp.dma_start(vec[:, :], a["vecs"]).then_inc(consts_in, 16)
            for g in plan.stages:
                load_weights(sp, g)
            for n in range(4):
                sp.wait_ge(out_ready, 4 * n + 4)
                sp.dma_start(out.rearrange("(k p) t -> p k t", p=P)[:, 4 * n:4 * n + 4],
                             work[:, 4 * n:4 * n + 4, PAD:COLS]).then_inc(out_done, 16)
            sp.wait_ge(out_done, 64)

        @block.gpsimd
        def _(pool):
            pool.wait_ge(x_ready, 48)
            pool.dma_start(masks[:, :, :], a["masks"]).then_inc(masks_in, 16)
            pool.dma_start(al, a["dn_ab"]).then_inc(masks_in, 16)
            blocks_out(pool, g_rw)
            DF.dve.wait(pool, "lo")
            pool.dma_start(rw_lw[0:64, :], a["rw_w2_2"]).then_inc(lora_in, 16)
            pool.dma_start(rw_lw[64:P, :], a["rw_a2_2"]).then_inc(lora_in, 16)
            RW.dve.wait(pool, "y", 3)
            pool.dma_start(rw_g2[:, :], a["rw_g2_2"]).then_inc(lora_in, 16)
            pool.dma_start(mem[:, :, :], a["mem"]).then_inc(mem_in, 16)

        @block.scalar
        def _(act):
            norm_act(act, 0, resid, 0, 0, lambda e, k: e.wait_ge(resid_in, 16))
            split_hi(act, g_glu, 0, 0)
            norm_split_act(act, 0, xa)
            gemm_act(act, g_glu, follows=g_qkv)
            blocks_out(act, g_glu)
            nc.scalar.activation(glu(TB_), glu(TB_), ACT.Sigmoid).then_inc(glu_sig, 1)
            gemm_act(act, g_qkv, follows=g_gsb)
            gemm_act(act, g_gsb, lambda m: att_act(act, m), follows=g_gcv)
            gemm_act(act, g_gcv, lambda m: att_act(act, m + 8), follows=g_sbo)
            att_act(act, 16)
            blocks_out(act, g_gcv)
            nc.scalar.activation(gates(TGS), gates(TGS), ACT.Sigmoid).then_inc(gates_done, 1)
            nc.scalar.activation(gates(TGC), gates(TGC), ACT.Sigmoid).then_inc(gates_done, 1)
            gemm_act(act, g_sbo, lambda m: ln_act(act, m), follows=g_cvo)
            gemm_act(act, g_cvo, follows=g_wo)
            act.wait_ge(merged, 1)
            nc.scalar.activation(xa[:, :, 0:T], gates(TGS), ACT.Copy).then_inc(merged_hi, 1)
            gemm_act(act, g_wo, squares_beside(act, g_wo, 1, work, PAD, 16), follows=ff1[0])
            norm_act(act, 1, work, PAD, 16, lambda e, k: blocks_out(e, g_wo), DT - 2)
            norm_act(act, 2, resid, 0, 0, lambda e, k: e.wait_ge(norm_res, k + 1))
            norm_split_act(act, 1, xa)
            for g, n in zip(ff1, ff1[1:] + [g_dn]):
                gemm_act(act, g, squares_beside(act, g, 3, work, PAD, 16) if g is ff1[-1] else None, follows=n)
            norm_act(act, 3, work, PAD, 16, lambda e, k: blocks_out(e, ff1[-1]), DT - 2)
            norm_act(act, 4, resid, 0, 0, lambda e, k: e.wait_ge(norm_res, DT + k + 1))
            norm_split_act(act, 2, xa)

            def conv_l2(m):
                dn_conv_act(act, m)
                l2_act(act, m)
            gemm_act(act, g_dn, conv_l2, follows=g_gab)
            gemm_act(act, g_gab, lambda m: l2_act(act, 16), follows=g_rw)
            core = dn_core(act, gates_act, dn_act, dnf_act)
            gemm_act(act, g_rw, follows=g_mk, each=step_of(core))
            rest_of(core)
            rwp_act(act)
            for r in range(4):
                rw_act(act, r)
            rwn_act(act)
            norm_act(act, 5, mem, 0, 0, lambda e, k: e.wait_ge(mem_in, 16))
            norm_split_act(act, 3, xa)
            gemm_act(act, g_mk, follows=g_mv)
            gemm_act(act, g_mv, follows=g_out)
            gemm_act(act, g_out, squares_beside(act, g_out, 6, resid, 0, 0), follows=g_xq)
            norm_act(act, 6, resid, 0, 0, lambda e, k: blocks_out(e, g_out), DT - 2)
            norm_split_act(act, 4, xa)
            gemm_act(act, g_xq, follows=g_xo)
            xat_act(act)
            gemm_act(act, g_xo, squares_beside(act, g_xo, 7, resid, 0, 0), follows=ff2[0])
            norm_act(act, 7, resid, 0, 0, lambda e, k: blocks_out(e, g_xo), DT - 2)
            norm_split_act(act, 5, xa)
            for g, n in zip(ff2, ff2[1:] + [None]):
                gemm_act(act, g, squares_beside(act, g, 8, resid, 0, 0) if g is ff2[-1] else None, follows=n)
            norm_act(act, 8, resid, 0, 0, lambda e, k: blocks_out(e, ff2[-1]), DT - 2)

        @block.vector
        def _(dve):
            dve.sem_inc(lo_ready, RING)
            dve.sem_inc(slab_used, RING)
            dve.sem_inc(evacuated, 2)
            dve_link(nc.vector.memset(u[:, :, 0:UPAD], 0.0))
            dve_link(nc.vector.memset(work[:, :, 0:PAD], 0.0))
            dve.wait_ge(consts_in, 32)
            split_lo(dve, g_glu, 0, 0)
            norm_rs_dve(dve, 0)
            norm_split_dve(dve, 0, xa, resid, 0, 0, lambda k: v1("g_pre_mix", k), 0)
            gemm_dve(dve, g_glu, follows=g_qkv)
            dve.wait_ge(glu_sig, 1)
            dve_link(nc.vector.tensor_tensor(u[:, :, UPAD:UCOLS], glu(TA), glu(TB_), ALU.mult))
            gemm_dve(dve, g_qkv, lambda m: conv(dve, share(m)), follows=g_gsb)

            def beside(m):
                att_dve(dve, m)
                conv(dve, share(12 + m))
            gemm_dve(dve, g_gsb, beside, follows=g_gcv)
            gemm_dve(dve, g_gcv, lambda m: beside(m + 8), follows=g_sbo)
            att_dve(dve, 16)
            dve.wait_ge(gates_done, 2)
            gemm_dve(dve, g_sbo, lambda m: ln_dve(dve, m), follows=g_cvo)
            gemm_dve(dve, g_cvo, follows=g_wo)
            blocks_out(dve, g_cvo)
            nc.vector.tensor_tensor(gates(TGS), gates(TGS), gates(TGC), ALU.add).then_inc(merged, 1)
            dve.wait_ge(merged_hi, 1)
            nc.vector.tensor_tensor(xa[:, :, T:2 * T], gates(TGS), xa[:, :, 0:T].bitcast(F32),
                                    ALU.subtract).then_inc(x_ready, 16)
            gemm_dve(dve, g_wo, follows=ff1[0])
            norm_add_dve(dve, 1, 0, 16, lambda k: v1("g_post_mix", k))
            norm_rs_dve(dve, 2)
            norm_split_dve(dve, 1, xa, resid, 0, 0, lambda k: v1("g_pre_mlp", k), 48)
            for g, n in zip(ff1, ff1[1:] + [g_dn]):
                gemm_dve(dve, g, follows=n)
            norm_add_dve(dve, 3, 1, 16, lambda k: v1("g_post_mlp", k))
            norm_rs_dve(dve, 4)
            norm_split_dve(dve, 2, xa, resid, 0, 0, lambda k: v2("mix_norm_w_2", k), 64)

            def conv_l2(m):
                dn_conv_dve(dve, m)
                l2_dve(dve, m)
            gemm_dve(dve, g_dn, conv_l2, follows=g_gab)
            gemm_dve(dve, g_gab, lambda m: conv_l2(16), follows=g_rw)
            core = dn_core(dve, gates_dve, dn_dve, dnf_dve)
            gemm_dve(dve, g_rw, follows=g_mk, each=step_of(core))
            rest_of(core)
            rwp_dve(dve)
            for r in range(4):
                rw_dve(dve, r)
            rwn_dve(dve)
            norm_rs_dve(dve, 5)
            norm_split_dve(dve, 3, xa, mem, 0, 0, lambda k: v2("mem_norm_w_2", k), 80)
            gemm_dve(dve, g_mk, follows=g_mv)
            gemm_dve(dve, g_mv, follows=g_out)
            gemm_dve(dve, g_out, follows=g_xq)
            norm_rs_dve(dve, 6)
            norm_split_dve(dve, 4, xa, resid, 0, 0, lambda k: v2("xa_norm_w_2", k), 96)
            gemm_dve(dve, g_xq, follows=g_xo)
            xat_dve(dve)
            gemm_dve(dve, g_xo, follows=ff2[0])
            norm_rs_dve(dve, 7)
            norm_split_dve(dve, 5, xa, resid, 0, 0, lambda k: v2("ffn_norm_w_2", k), 112)
            for g, n in zip(ff2, ff2[1:] + [None]):
                gemm_dve(dve, g, follows=n)
            norm_rs_dve(dve, 8)
            for k in range(DT):
                nc.vector.scalar_tensor_tensor(out=work[:, k, PAD:COLS], in0=resid[:, k], scalar=v2("final_norm_w_2", k),
                                               in1=rs[:, :], op0=ALU.mult, op1=ALU.mult).then_inc(out_ready, 1)

        @block.tensor
        def _(pe):
            pe.wait_ge(consts_in, 32)
            norm_pe(pe, 0)
            gemm_pe(pe, g_glu, x_tiles=0)
            gemm_pe(pe, g_qkv)
            blocks_out(pe, g_qkv)
            gemm_pe(pe, g_gsb, lambda m: att_pe(pe, m))
            gemm_pe(pe, g_gcv, lambda m: att_pe(pe, m + 8))
            att_pe(pe, 16)
            pe.wait_ge(att_lo, SB_H)
            gemm_pe(pe, g_sbo, lambda m: ln_pe(pe, m))
            pe.wait_ge(x_ready, 32)
            gemm_pe(pe, g_cvo)
            pe.wait_ge(x_ready, 48)
            gemm_pe(pe, g_wo, sums_beside(pe, 1))
            norm_pe(pe, 1, LATE)
            norm_pe(pe, 2)
            gemm_pe(pe, ff1[0], x_tiles=48)
            for n, g in enumerate(ff1[1:]):
                gemm_pe(pe, g, sums_beside(pe, 3) if g is ff1[-1] else None, of=None if n % 2 else ff1[n])
            norm_pe(pe, 3, LATE)
            norm_pe(pe, 4)
            gemm_pe(pe, g_dn, lambda m: l2_pe(pe, m), x_tiles=64)
            gemm_pe(pe, g_gab, lambda m: l2_pe(pe, 16))
            L2.dve.wait(pe, "done", DN_H - 1)
            core = dn_core(pe, gates_pe, dn_pe, dnf_pe)
            gemm_pe(pe, g_rw, each=step_of(core))
            rest_of(core)
            rwp_pe(pe)
            RP.dve.wait(pe, "t3")
            RP.act.wait(pe, "t2")
            for r in range(4):
                rw_pe(pe, r)
            rwn_pe(pe)
            RN.dve.wait(pe, "y4")
            norm_pe(pe, 5)
            gemm_pe(pe, g_mk, x_tiles=80)
            gemm_pe(pe, g_mv)
            DF.dve.wait(pe, "lo")
            RN.dve.wait(pe, "lo")
            gemm_pe(pe, g_out, sums_beside(pe, 6))
            norm_pe(pe, 6, LATE)
            gemm_pe(pe, g_xq, x_tiles=96)
            blocks_out(pe, g_mv)
            xat_pe(pe)
            XA_.dve.wait(pe, "lo")
            gemm_pe(pe, g_xo, sums_beside(pe, 7))
            norm_pe(pe, 7, LATE)
            gemm_pe(pe, ff2[0], x_tiles=112)
            for n, g in enumerate(ff2[1:]):
                gemm_pe(pe, g, sums_beside(pe, 8) if g is ff2[-1] else None, of=None if n % 2 else ff2[n])
            norm_pe(pe, 8, LATE)


def kernel(**inputs):
    import numpy as _np
    import concourse.bacc as _bacc
    from concourse import mybir as _mybir
    from concourse.bass_utils import run_bass_kernel_spmd as _run

    def tiles(x):
        x = _np.asarray(x)
        return x.reshape(-1, P).T

    nc = _bacc.Bacc("TRN2", target_bir_lowering=False, num_devices=1)
    arrays = {
        "x": _np.ascontiguousarray(_np.asarray(inputs["x"])[0].T.reshape(DT, P, T).transpose(1, 0, 2)),
        "consts": constants().reshape(P, len(CONSTS), P),
        "masks": level_masks(),
        "vecs": _np.concatenate([tiles(inputs[n]) for n, _ in VEC1 + VEC2], axis=1),
        "mem": _np.asarray(inputs["mem_2"])[0].T.reshape(DT, P, T).transpose(1, 0, 2),
        "dn_ab": _np.stack([_np.asarray(inputs[n])[0] for n in ("dn_a_log_2", "dn_dt_bias_2")], axis=1),
    }
    for name in ("w_in", "w_sb_out", "w_conv_out", "w_o", "w_up", "w_down", "w_in_2", "w_out_2", "xa_wq_2", "xa_wk_2",
                 "xa_wv_2", "xa_wo_2", "ffn_w1_2", "ffn_w2_2", "rw_w2_2", "rw_a2_2", "rw_g2_2"):
        arrays[name] = _np.asarray(inputs[name])[0]
    arrays = {k: _np.ascontiguousarray(v) for k, v in arrays.items()}
    aps = {k: nc.dram_tensor(k, v.shape, _mybir.dt.from_np(v.dtype), kind="ExternalInput").ap() for k, v in arrays.items()}
    out = nc.dram_tensor("out", (D, T), F32, kind="ExternalOutput").ap()
    build_program(nc, aps, out)
    r = _run(nc, [arrays], core_ids=[0])
    return _np.ascontiguousarray(r.results[0]["out"].T).reshape(1, T, D)
```

```python
from contextlib import ExitStack

import numpy as np

import concourse.bass as bass
from concourse import mybir

F32 = mybir.dt.float32
F32R = mybir.dt.float32r
ALU = mybir.AluOpType
ACT = mybir.ActivationFunctionType
AX = mybir.AxisListType

P = 128
T = 256
D = 2048
DT = D // P
EPS = 1e-6
PAD = 4
COLS = T + PAD
BW = 256
KG = 4
RING = 4
SB_H, SB_D = 8, 128
CONV = 31
UPAD = CONV - 1
UCOLS = T + UPAD
D_FF = 4 * D
FF_PIECES = 4

VEC1 = [("g_pre_mix", 16), ("b_in", 72), ("w_dw", CONV * 8), ("b_dw", 8), ("g_conv_ln", 8), ("b_conv_ln", 8),
        ("g_post_mix", 16), ("g_pre_mlp", 16), ("g_post_mlp", 16)]


def columns(spec):
    at, out = 0, {}
    for name, n in spec:
        out[name] = at
        at += n
    return out, at


VEC2 = [("mix_norm_w_2", 16), ("dn_conv_w_2", 96), ("dn_norm_w_2", 1), ("rw_mu_2", 26), ("rw_w0_2", 8), ("rw_a0_2", 8),
        ("rw_k_k_2", 8), ("rw_k_a_2", 8), ("rw_r_k_2", 8), ("rw_ln_w_2", 8), ("rw_ln_b_2", 8), ("xa_norm_w_2", 16),
        ("mem_norm_w_2", 16), ("ffn_norm_w_2", 16), ("final_norm_w_2", 16)]
V1, NV1 = columns(VEC1)
V2, NV2 = columns(VEC2)

CONSTS = ["ident", "ones", "upto", "before", "before_big", "incl", "ones_head"]
LEVELS = 7
DN_H, RW_H, RW_D = 8, 16, 64
RW_DECAY = float(np.exp(-0.5))
XA_H, XA_D = 4, 128


def constants():
    i = np.arange(P)
    later = (i[:, None] >= i[None, :]).astype(np.float32)
    before = (i[:, None] < i[None, :]).astype(np.float32)
    big = np.where(before > 0, 0.0, -1e30).astype(np.float32)
    incl = (i[:, None] <= i[None, :]).astype(np.float32)
    head = (i[:, None] // RW_D == i[None, :] // RW_D).astype(np.float32)
    return np.concatenate([np.eye(P, dtype=np.float32), np.ones((P, P), np.float32), later, before, big, incl, head],
                          axis=1)


def level_masks():
    i = np.arange(P)
    out = []
    for l in range(LEVELS):
        n = i >> l
        out.append(((n[:, None] % 2 == 0) & (n[None, :] == n[:, None] + 1)).astype(np.float32))
    return np.stack(out, axis=1)


class Gemm:

    def __init__(self, plan, name, w, k, n0, n, x, kind, dst, x_from=0, bias=None, k0=0, apart=P):
        self.name, self.w, self.n0, self.x, self.kind, self.dst = name, w, n0, x, kind, dst
        self.k0, self.x_from, self.bias, self.apart = k0, x_from, bias, apart
        self.groups = k // (P * KG)
        self.blocks = n // BW
        self.b0, self.s0, self.sum0, self.sq0 = plan.blocks, plan.slabs, plan.sums, plan.squares
        self.unroll = 4 if self.groups == 1 else 2
        self.turn = self.unroll * self.groups
        plan.blocks += self.blocks
        plan.slabs += self.blocks * self.groups
        plan.sums += self.blocks if kind != "store" else 0
        plan.squares += self.blocks if kind == "relu2" else 0
        plan.stages.append(self)
        assert self.s0 % RING == 0 and self.turn % RING == 0

    def slab(self, i, block, j):
        o = block * self.groups + j
        return o % RING, self.s0 // RING + i * (self.turn // RING) + o // RING, self.s0 + i * self.turn + o


class Steps:

    def __init__(self, sem, names):
        self.sem, self.names, self.n = sem, names, 0

    def at(self, name, r=0):
        return r * len(self.names) + self.names.index(name) + 1

    def done(self, ins, name, r=0):
        self.n += 1
        assert self.at(name, r) == self.n, (name, r, self.names[(self.n - 1) % len(self.names)])
        ins.then_inc(self.sem, 1)

    def wait(self, eng, name, r=0):
        eng.wait_ge(self.sem, self.at(name, r))


class Plan:
    def __init__(self):
        self.blocks = self.slabs = self.sums = self.squares = 0
        self.stages = []


def build_program(nc, a, out):
    plan = Plan()
    ctx = ExitStack()
    with ctx:
        base = 16640
        top = [base]

        def at(name, shape, dt, offset=None):
            size = 4 * int(np.prod(shape[1:]))
            if offset is None:
                offset = top[0]
                top[0] += (size + 31) // 32 * 32
            return nc.alloc_sbuf_tensor_at(name, shape, dt, offset=offset)

        def sem(name):
            return ctx.enter_context(nc.semaphore(name))

        raw = at("raw", [P, RING, KG, BW], F32)
        hi = at("hi", [P, RING, KG, BW], F32R)
        lo = at("lo", [P, RING, KG, BW], F32R)
        half = at("half", [P, 2, T], F32)
        sq = at("sq", [P, 2, T], F32)
        rs = at("rs", [P, T], F32)
        resid = at("resid", [P, DT, T], F32)
        xa_at = top[0]
        xa = at("xa", [P, DT, 2 * T], F32R)
        xb_at = top[0]
        xb = at("xb", [P, DT, 2 * T], F32R)
        work_at = top[0]
        work = at("work", [P, 64, COLS], F32)
        cst = at("cst", [P, len(CONSTS), P], F32)
        vec = at("vec", [P, NV1 + NV2], F32)
        small = at("small", [P, 144], F32)
        u = at("u", [P, 8, UCOLS], F32, xb_at + 16384)
        zs = at("zs", [P, 3 * P], F32, xb_at + 16384 + 8 * UCOLS * 4)
        la = at("la", [P, 3 * P], F32, xb_at + 16384 + 8 * UCOLS * 4 + 1536)
        vt = at("vt", [P, 2, P], F32, xb_at + 16384 + 8 * UCOLS * 4 + 3072)

        def const(name):
            return cst[:, CONSTS.index(name), :]

        def v1(name, i=0):
            return vec[:, V1[name] + i:V1[name] + i + 1]

        pg = ctx.enter_context(nc.psum_tensor("pg", [P, 2, 2, 2 * T], F32))
        p4 = ctx.enter_context(nc.psum_tensor("p4", [P, 4, 512], F32))
        ps = [p4[:, n] for n in range(4)]

        w_in = a["w_in"]
        TA, TB, TQ, TK, TV, TGS, TGC, TY = 0, 8, 16, 24, 32, 0, 40, 56
        g_glu = Gemm(plan, "glu", w_in, D, 3072, 2048, xa, "store", (work, TA, PAD), bias=V1["b_in"] + 24)
        g_qkv = Gemm(plan, "qkv", w_in, D, 0, 3072, xa, "store", (work, TQ, PAD), bias=V1["b_in"])
        g_gsb = Gemm(plan, "gate_sb", w_in, D, 5120, 2048, xa, "store", (work, TGS, PAD), bias=V1["b_in"] + 40)
        g_gcv = Gemm(plan, "gate_cv", w_in, D, 7168, 2048, xa, "store", (work, TGC, PAD), bias=V1["b_in"] + 56)
        g_sbo = Gemm(plan, "sb_out", a["w_sb_out"], D // 2, 0, D, xb, "mult", (work, TGS, PAD))
        g_cvo = Gemm(plan, "conv_out", a["w_conv_out"], D // 2, 0, D, xb, "mult", (work, TGC, PAD), x_from=8)
        g_wo = Gemm(plan, "w_o", a["w_o"], D, 0, D, xa, "store", (work, 16, PAD))
        ff1 = []
        for p in range(FF_PIECES):
            up = Gemm(plan, f"up{p}", a["w_up"], D, p * D, D, xa, "relu2", (xb, 0, 0))
            down = Gemm(plan, f"down{p}", a["w_down"], D, 0, D, xb, "add" if p else "store", (work, 16, PAD), k0=p * D)
            ff1 += [up, down]

        consts_in = sem("consts_in")
        resid_in = [sem(f"resid_in{n}") for n in range(4)]
        raw_in = [sem(f"raw_in{n}") for n in range(RING)]
        hi_ready = sem("hi_ready")
        lo_ready = sem("lo_ready")
        slab_used = sem("slab_used")
        half_out = sem("half_out")
        evacuated = sem("evacuated")
        summed = sem("summed")
        squared, rounded = sem("squared"), sem("rounded")
        x_ready = sem("x_ready")
        norm_sq, norm_used = sem("norm_sq"), sem("norm_used")
        norm_rs, norm_nx, norm_hi = sem("norm_rs"), sem("norm_nx"), sem("norm_hi")
        norm_res = sem("norm_res")
        dve_seq, act_seq = sem("dve_seq"), sem("act_seq")
        glu_sig, glu_u = sem("glu_sig"), sem("glu_u")
        att_z, att_zs, att_ln, att_sp, att_s, att_t = [sem("att_" + n) for n in ("z", "zs", "ln", "sp", "s", "t")]
        att_a, att_vt, att_o, att_hi, att_lo, att_vp = [sem("att_" + n) for n in ("a", "vt", "o", "hi", "lo", "vp")]
        conv_done, gates_done, merged_hi, merged = sem("conv_done"), sem("gates_done"), sem("merged_hi"), sem("merged")
        ln_sum, ln_mid, ln_sq, ln_var, ln_std = [sem("ln_" + n) for n in ("sum", "mid", "sq", "var", "std")]
        ln_y, ln_sig, ln_f, ln_hi = [sem("ln_" + n) for n in ("y", "sig", "f", "hi")]
        out_ready, out_done = sem("out_ready"), sem("out_done")
        masks_in, mem_in = sem("masks_in"), sem("mem_in")
        seq = {"dve": 0, "act": 0}

        def dve_link(ins):
            seq["dve"] += 1
            ins.then_inc(dve_seq, 1)
            nc.vector.wait_ge(dve_seq, seq["dve"])

        def act_link(ins):
            seq["act"] += 1
            ins.then_inc(act_seq, 1)
            nc.scalar.wait_ge(act_seq, seq["act"])

        def run_blocks(eng, n, unroll, body, after=None, each=None):
            whole = n // unroll
            if after is None and each is None and whole > 1:
                with eng.Fori(0, whole) as i:
                    for v in range(unroll):
                        body(i, v)
            else:
                for t in range(whole * unroll):
                    body(t // unroll, t % unroll)
                    if after:
                        after(t)
            for v in range(n - whole * unroll):
                body(whole, v)
                if after:
                    after(whole * unroll + v)

        def load_weights(sp, g):
            w = g.w.rearrange("(k p) n -> p k n", p=P)

            def block(i, v):
                first = sp.snap(g.n0 + (i * g.unroll + v) * BW) if not isinstance(i, int) else g.n0 + (i * g.unroll + v) * BW
                for j in range(g.groups):
                    slot, turn, s = g.slab(i, v, j)
                    k = g.k0 // P + j * KG
                    sp.wait_ge(lo_ready, s + 1)
                    sp.dma_start(raw[:, slot], w[:, k:k + KG, bass.ds(first, BW)]).then_inc(raw_in[slot], 16)

            run_blocks(sp, g.blocks, g.unroll, block)

        def split_hi(act, g, i, v, each=None):
            for j in range(g.groups):
                slot, turn, s = g.slab(i, v, j)
                act.wait_ge(raw_in[slot], turn * 16 + 16)
                act.wait_ge(slab_used, s + 1)
                nc.scalar.activation(hi[:, slot], raw[:, slot], ACT.Copy).then_inc(hi_ready, 1)
                if each:
                    each()

        def take_half(act, g, i, v):
            b = g.b0 + i * g.unroll + v
            par = (g.b0 + v) % 2
            act.wait_ge(slab_used, g.slab(i, v, g.groups - 1)[2] + 1 + RING)
            act.wait_ge(evacuated, b + 2)
            if g.bias is None:
                nc.scalar.activation(half[:, :, :], pg[:, par, :, T:2 * T], ACT.Copy).then_inc(half_out, 1)
            else:
                for t in range(2):
                    c = g.bias + 2 * (i * g.unroll + v) + t
                    ins = nc.scalar.activation(half[:, t], pg[:, par, t, T:2 * T], ACT.Identity,
                                               bias=vec[:, bass.ds(c, 1)])
                ins.then_inc(half_out, 1)

        def gemm_act(act, g, after=None, follows=None, each=None):
            def block(i, v):
                split_hi(act, g, i, v + 1, each)
                take_half(act, g, i, v)
            run_blocks(act, g.blocks - 1, g.unroll, block, after, each)
            if follows:
                split_hi(act, follows, 0, 0, each)
            n = g.blocks - 1
            take_half(act, g, n // g.unroll, n % g.unroll)
            if after:
                after(n)

        def split_lo(dve, g, i, v, each=None):
            for j in range(g.groups):
                slot, turn, s = g.slab(i, v, j)
                dve.wait_ge(hi_ready, s + 1)
                nc.vector.tensor_tensor(lo[:, slot], raw[:, slot], hi[:, slot].bitcast(F32),
                                        ALU.subtract).then_inc(lo_ready, 1)
                if each:
                    each()

        def evacuate(dve, g, i, v):
            t = i * g.unroll + v
            par = (g.b0 + v) % 2
            into, tile, off = g.dst
            dve.wait_ge(half_out, g.b0 + t + 1)
            psum = pg[:, par, :, 0:T]
            place = into[:, bass.ds(tile + 2 * t, 2), off:off + T]
            if g.kind == "store":
                nc.vector.tensor_tensor(place, psum, half[:, :, :], ALU.add).then_inc(evacuated, 1)
                return
            own = g.sum0 + t + 1
            if g.kind in ("add", "mult"):
                nc.vector.tensor_tensor(half[:, :, :], psum, half[:, :, :], ALU.add).then_inc(summed, 1)
                dve.wait_ge(summed, own)
                nc.vector.tensor_tensor(place, place, half[:, :, :],
                                        ALU.add if g.kind == "add" else ALU.mult).then_inc(evacuated, 1)
                return
            own_sq = g.sq0 + t + 1
            nc.vector.tensor_tensor(sq[:, :, :], psum, half[:, :, :], ALU.add).then_inc(summed, 1)
            dve.wait_ge(summed, own)
            nc.vector.scalar_tensor_tensor(out=sq[:, :, :], in0=sq[:, :, :], scalar=0.0, in1=sq[:, :, :],
                                           op0=ALU.max, op1=ALU.mult).then_inc(squared, 1)
            dve.wait_ge(squared, own_sq)
            nc.vector.tensor_copy(place, sq[:, :, :]).then_inc(rounded, 1)
            dve.wait_ge(rounded, own_sq)
            rest = into[:, bass.ds(tile + 2 * t, 2), T:2 * T]
            nc.vector.tensor_tensor(rest, sq[:, :, :], place.bitcast(F32), ALU.subtract).then_inc(evacuated, 1)

        def gemm_dve(dve, g, after=None, follows=None, each=None):
            def block(i, v):
                split_lo(dve, g, i, v + 1, each)
                evacuate(dve, g, i, v)
            run_blocks(dve, g.blocks - 1, g.unroll, block, after, each)
            if follows:
                split_lo(dve, follows, 0, 0, each)
            n = g.blocks - 1
            evacuate(dve, g, n // g.unroll, n % g.unroll)
            if after:
                after(n)

        def gemm_pe(pe, g, after=None, x_tiles=None, of=None, each=None):
            def block(i, v, waits=False):
                par = (g.b0 + v) % 2
                pe.wait_ge(evacuated, g.b0 + i * g.unroll + v + 1)
                for j in range(g.groups):
                    slot, turn, s = g.slab(i, v, j)
                    pe.wait_ge(lo_ready, s + 1 + RING)
                    if waits and of:
                        pe.wait_ge(evacuated, of.b0 + KG // 2 * (j + 1) + 2)
                    elif waits:
                        pe.wait_ge(x_ready, x_tiles + KG * (j + 1))
                    for t in range(2):
                        c = t * g.apart
                        for k in range(KG):
                            kk = g.x_from + j * KG + k
                            nc.tensor.matmul(pg[:, par, t, :], lhsT=hi[:, slot, k, c:c + P], rhs=g.x[:, kk, :],
                                             start=(j == 0 and k == 0), stop=False)
                            ins = nc.tensor.matmul(pg[:, par, t, 0:T], lhsT=lo[:, slot, k, c:c + P],
                                                   rhs=g.x[:, kk, 0:T], start=False,
                                                   stop=(j == g.groups - 1 and k == KG - 1))
                    ins.then_inc(slab_used, 1)
                    if each:
                        each()

            if x_tiles is not None or of:
                for v in range(g.unroll):
                    block(0, v, waits=(v == 0))
                    if after:
                        after(v)
                rest = g.blocks - g.unroll
                run_blocks(pe, rest, g.unroll, lambda i, v: block(i + 1, v),
                           (lambda t: after(t + g.unroll)) if after else None)
            else:
                run_blocks(pe, g.blocks, g.unroll, block, after, each)

        def square_tile(act, n, k, src, off, tile0):
            if n or k >= 2:
                act.wait_ge(norm_used, DT * n + k - 1)
            nc.scalar.activation(sq[:, k % 2], src[:, tile0 + k, off:off + T], ACT.Square).then_inc(norm_sq, 1)

        def norm_act(act, n, src, off, tile0, ready, k0=0):
            act_link(nc.scalar.activation(small[:, 140:141], const("ones")[:, 0:1], ACT.Ln))
            for k in range(k0, DT):
                ready(act, k)
                square_tile(act, n, k, src, off, tile0)
            norm_root(act, n)

        def norm_root(act, n):
            act.wait_ge(norm_used, DT * (n + 1))
            act_link(nc.scalar.activation(rs[:, :], ps[0][:, 0:T], ACT.Ln, scale=1.0 / D, bias=EPS))
            nc.scalar.activation(rs[:, :], rs[:, :], ACT.Exp, scale=-0.5).then_inc(norm_rs, 1)

        def squares_beside(act, g, n, src, off, tile0):
            def after(m):
                if m:
                    act.wait_ge(evacuated, g.b0 + m + 2)
                    for k in (2 * m - 2, 2 * m - 1):
                        square_tile(act, n, k, src, off, tile0)
            return after

        def sums_beside(pe, n):
            def after(m):
                if m >= 2:
                    norm_pe(pe, n, 2 * m - 4, 2 * m - 2)
            return after

        LATE = DT - 4

        def norm_split_act(act, m, x, tmp=half, k0=0, k1=DT):
            for k in range(k0, k1):
                act.wait_ge(norm_nx, DT * m + k + 1)
                nc.scalar.activation(x[:, k, 0:T], tmp[:, k % 2], ACT.Copy).then_inc(norm_hi, 1)

        def norm_pe(pe, n, k0=0, k1=DT):
            for k in range(k0, k1):
                pe.wait_ge(norm_sq, DT * n + k + 1)
                ins = nc.tensor.matmul(ps[0][:, 0:T], lhsT=const("ones"), rhs=sq[:, k % 2],
                                       start=(k == 0), stop=(k == DT - 1))
                ins.then_inc(norm_used, 1)

        def norm_rs_dve(dve, n):
            dve.wait_ge(norm_rs, n + 1)

        def norm_split_dve(dve, m, x, src, off, tile0, gain, x_tiles, tmp=half, k0=0, k1=DT):
            for k in range(k0, k1 + 1):
                if k < k1:
                    if k >= 2:
                        dve.wait_ge(x_ready, x_tiles + k - 1)
                    nc.vector.scalar_tensor_tensor(out=tmp[:, k % 2], in0=src[:, tile0 + k, off:off + T],
                                                   scalar=gain(k), in1=rs[:, :], op0=ALU.mult,
                                                   op1=ALU.mult).then_inc(norm_nx, 1)
                if k > k0:
                    dve.wait_ge(norm_hi, DT * m + k)
                    nc.vector.tensor_tensor(x[:, k - 1, T:2 * T], tmp[:, (k - 1) % 2],
                                            x[:, k - 1, 0:T].bitcast(F32), ALU.subtract).then_inc(x_ready, 1)

        def norm_add_dve(dve, n, added, tile0, gain):
            norm_rs_dve(dve, n)
            for k in range(DT + 1):
                if k < DT:
                    if k >= 2:
                        dve.wait_ge(norm_res, DT * added + k - 1)
                    seq["dve"] += 1
                    nc.vector.scalar_tensor_tensor(out=half[:, k % 2], in0=work[:, tile0 + k, PAD:COLS],
                                                   scalar=gain(k), in1=rs[:, :], op0=ALU.mult,
                                                   op1=ALU.mult).then_inc(dve_seq, 1)
                if k:
                    dve.wait_ge(dve_seq, seq["dve"] - (1 if k < DT else 0))
                    nc.vector.tensor_tensor(resid[:, k - 1], resid[:, k - 1], half[:, (k - 1) % 2],
                                            ALU.add).then_inc(norm_res, 1)

        glu = lambda t: work[:, t:t + 8, PAD:COLS]
        conv_steps = [(c, j) for c in range(8) for j in range(CONV)]

        def conv(dve, lot):
            for c, j in lot:
                acc, x = work[:, TY + c, PAD:COLS], u[:, c, j:j + T]
                if j == 0:
                    ins = nc.vector.tensor_scalar(acc, x, v1("w_dw", c), v1("b_dw", c), ALU.mult, ALU.add)
                else:
                    ins = nc.vector.scalar_tensor_tensor(out=acc, in0=x, scalar=v1("w_dw", 8 * j + c), in1=acc,
                                                         op0=ALU.mult, op1=ALU.add)
                if (c, j) == conv_steps[-1]:
                    ins.then_inc(conv_done, 1)
                else:
                    dve_link(ins)

        def share(m):
            a0 = 10 * m if m < 12 else 120 + 8 * (m - 12)
            return conv_steps[a0:a0 + (10 if m < 12 else 8)]

        diag = lambda x: x[:, 0:3 * P].rearrange("p (b c) -> p b c", c=P)[:, 0:3:2, :]
        both = lambda name: const(name)[:, None, :].to_broadcast([P, 2, P])

        def att_pe(pe, m):
            h = m // 2
            if m % 2 == 0 and h > 0:
                pe.wait_ge(att_a, h)
                if h >= 2:
                    pe.wait_ge(att_lo, h - 1)
                nc.tensor.matmul(ps[3][:, 0:P], lhsT=vt[:, 0], rhs=la[:, 0:P], start=True, stop=True)
                nc.tensor.matmul(ps[3][:, P:T], lhsT=vt[:, 0], rhs=la[:, P:T], start=True, stop=False)
                nc.tensor.matmul(ps[3][:, P:T], lhsT=vt[:, 1], rhs=la[:, T:3 * P], start=False,
                                 stop=True).then_inc(att_o, 1)
            if h >= SB_H:
                return
            if m % 2 == 0:
                q, k, v = (work[:, t + h, PAD:COLS] for t in (TQ, TK, TV))
                if h:
                    pe.wait_ge(att_zs, h)
                    pe.wait_ge(att_vt, h)
                else:
                    blocks_out(pe, g_qkv)
                nc.tensor.matmul(ps[0][:, 0:T], lhsT=k[:, 0:P], rhs=q, start=True, stop=True)
                nc.tensor.matmul(ps[0][:, T:3 * P], lhsT=k[:, P:T], rhs=q[:, P:T], start=True,
                                 stop=True).then_inc(att_z, 1)
                nc.tensor.transpose(ps[2][:, 0:P], v[:, 0:P], const("ident"))
                nc.tensor.transpose(ps[2][:, P:T], v[:, P:T], const("ident")).then_inc(att_vp, 1)
            else:
                pe.wait_ge(att_sp, h + 1)
                nc.tensor.matmul(diag(ps[1][:, 0:3 * P]), lhsT=const("upto"), rhs=diag(la), start=True, stop=True)
                nc.tensor.matmul(ps[1][:, P:T], lhsT=const("upto"), rhs=la[:, P:T], start=True, stop=False)
                nc.tensor.matmul(ps[1][:, P:T], lhsT=const("ones"), rhs=la[:, T:3 * P], start=False,
                                 stop=True).then_inc(att_s, 1)

        def att_act(act, m):
            h = m // 2
            if m % 2 == 0 and h > 0:
                act.wait_ge(att_o, h)
                nc.scalar.activation(xb[:, h - 1, 0:T], ps[3][:, 0:T], ACT.Copy).then_inc(att_hi, 1)
            if h >= SB_H:
                return
            if m % 2 == 0:
                act.wait_ge(att_vp, h + 1)
                if h:
                    act.wait_ge(att_o, h)
                nc.scalar.activation(vt[:, :, :], ps[2][:, 0:T].rearrange("p (a b) -> p a b", a=2),
                                     ACT.Copy).then_inc(att_vt, 1)
                act.wait_ge(att_zs, h + 1)
                act_link(nc.scalar.activation(la[:, :], zs[:, :], ACT.Abs))
                act_link(nc.scalar.activation(la[:, :], la[:, :], ACT.Exp, scale=-1.0))
                nc.scalar.activation(la[:, :], la[:, :], ACT.Ln, bias=1.0).then_inc(att_ln, 1)
            else:
                act.wait_ge(att_t, h + 1)
                nc.scalar.activation(la[:, :], zs[:, :], ACT.Exp).then_inc(att_a, 1)

        def att_dve(dve, m):
            h = m // 2
            if m % 2 == 0 and h > 0:
                dve.wait_ge(att_hi, h)
                nc.vector.tensor_tensor(xb[:, h - 1, T:2 * T], ps[3][:, 0:T], xb[:, h - 1, 0:T].bitcast(F32),
                                        ALU.subtract).then_inc(att_lo, 1)
            if h >= SB_H:
                return
            if m % 2 == 0:
                dve.wait_ge(att_z, h + 1)
                if h:
                    dve.wait_ge(att_a, h)
                nc.vector.tensor_scalar(zs[:, :], ps[0][:, 0:3 * P], SB_D ** -0.5, None, ALU.mult).then_inc(att_zs, 1)
                dve.wait_ge(att_ln, h + 1)
                dve_link(nc.vector.scalar_tensor_tensor(out=la[:, :], in0=zs[:, :], scalar=0.0, in1=la[:, :],
                                                        op0=ALU.max, op1=ALU.add))
                nc.vector.tensor_tensor(diag(la), diag(la), both("before"), ALU.mult).then_inc(att_sp, 1)
            else:
                dve.wait_ge(att_s, h + 1)
                dve_link(nc.vector.tensor_tensor(zs[:, :], zs[:, :], ps[1][:, 0:3 * P], ALU.subtract))
                nc.vector.tensor_tensor(diag(zs), diag(zs), both("before_big"), ALU.add).then_inc(att_t, 1)

        CV = D // 2
        conv_y = work[:, TY:TY + 8, PAD:COLS]
        ln_tmp = work[:, 16:24, PAD:COLS]

        def ln_pe(pe, m):
            if m == 0:
                pe.wait_ge(conv_done, 1)
                for c in range(8):
                    ins = nc.tensor.matmul(ps[0][:, 0:T], lhsT=const("ones"), rhs=work[:, TY + c, PAD:COLS],
                                           start=(c == 0), stop=(c == 7))
                ins.then_inc(ln_sum, 1)
            if m == 2:
                pe.wait_ge(ln_sq, 1)
                for c in range(8):
                    ins = nc.tensor.matmul(ps[1][:, 0:T], lhsT=const("ones"), rhs=work[:, 16 + c, PAD:COLS],
                                           start=(c == 0), stop=(c == 7))
                ins.then_inc(ln_var, 1)

        def ln_act(act, m):
            if m == 0:
                act.wait_ge(ln_mid, 1)
                nc.scalar.activation(ln_tmp, conv_y, ACT.Square).then_inc(ln_sq, 1)
            if m == 2:
                act.wait_ge(ln_var, 1)
                act_link(nc.scalar.activation(rs[:, :], ps[1][:, 0:T], ACT.Ln, scale=1.0 / CV, bias=EPS))
                nc.scalar.activation(rs[:, :], rs[:, :], ACT.Exp, scale=-0.5).then_inc(ln_std, 1)
            if m == 3:
                act.wait_ge(ln_y, 1)
                for c in range(8):
                    ins = nc.scalar.activation(work[:, 16 + c, PAD:COLS], work[:, TY + c, PAD:COLS], ACT.Sigmoid,
                                               scale=v1("g_conv_ln", c), bias=v1("b_conv_ln", c))
                ins.then_inc(ln_sig, 1)
            if m == 5:
                act.wait_ge(ln_f, 1)
                nc.scalar.activation(xb[:, 8:16, 0:T], conv_y, ACT.Copy).then_inc(ln_hi, 1)

        def ln_dve(dve, m):
            if m == 0:
                dve.wait_ge(ln_sum, 1)
                nc.vector.scalar_tensor_tensor(out=conv_y, in0=ps[0][:, None, 0:T].to_broadcast([P, 8, T]),
                                               scalar=-1.0 / CV, in1=conv_y, op0=ALU.mult,
                                               op1=ALU.add).then_inc(ln_mid, 1)
            if m == 2:
                dve.wait_ge(ln_std, 1)
                nc.vector.tensor_tensor(conv_y, conv_y, rs[:, None, :].to_broadcast([P, 8, T]),
                                        ALU.mult).then_inc(ln_y, 1)
            if m == 4:
                dve.wait_ge(ln_sig, 1)
                for c in range(8):
                    ins = nc.vector.tensor_scalar(work[:, TY + c, PAD:COLS], work[:, TY + c, PAD:COLS],
                                                  v1("g_conv_ln", c), v1("b_conv_ln", c), ALU.mult, ALU.add)
                dve_link(ins)
                nc.vector.tensor_tensor(conv_y, conv_y, ln_tmp, ALU.mult).then_inc(ln_f, 1)
            if m == 6:
                dve.wait_ge(ln_hi, 1)
                nc.vector.tensor_tensor(xb[:, 8:16, T:2 * T], conv_y, xb[:, 8:16, 0:T].bitcast(F32),
                                        ALU.subtract).then_inc(x_ready, 16)

        gates = lambda t0: work[:, t0:t0 + DT, PAD:COLS]

        def pair(x, m, a0=0, a1=T):
            return x[:, 2 * m:2 * m + 2, a0:a1]

        def merge_act(act, m):
            if m >= 0:
                act.wait_ge(merged, m + 1)
                nc.scalar.activation(pair(xa, m), pair(gates(TGS), m), ACT.Copy).then_inc(merged_hi, 1)

        def merge_dve(dve, m):
            if m >= 1:
                dve.wait_ge(merged_hi, m)
                nc.vector.tensor_tensor(pair(xa, m - 1, T, 2 * T), pair(gates(TGS), m - 1),
                                        pair(xa, m - 1).bitcast(F32), ALU.subtract).then_inc(x_ready, 2)
            if m < 8:
                dve.wait_ge(evacuated, g_cvo.b0 + m + 3)
                nc.vector.tensor_tensor(pair(gates(TGS), m), pair(gates(TGS), m), pair(gates(TGC), m),
                                        ALU.add).then_inc(merged, 1)

        def blocks_out(eng, g):
            eng.wait_ge(evacuated, g.b0 + g.blocks + 2)

        def v2(name, i=0):
            c = NV1 + V2[name] + i
            return vec[:, c:c + 1]

        w2in = a["w_in_2"]
        DQ, DK, DV, DZ, RR, RK, RV, RL, RG, GA, GB = 0, 8, 16, 24, 32, 40, 48, 56, 57, 58, 59
        g_dn = Gemm(plan, "dn", w2in, D, 0, 4096, xa, "store", (work, DQ, PAD))
        g_gab = Gemm(plan, "gab", w2in, D, 4096, BW, xa, "store", (work, GA, PAD), apart=DN_H)
        g_rw = Gemm(plan, "rw", w2in, D, 4112, 3328, xa, "store", (work, RR, PAD))
        g_oa = Gemm(plan, "w_out dn", a["w_out_2"], D // 2, 0, D, xb, "add", (resid, 0, 0))
        g_mk = Gemm(plan, "mem_k", a["xa_wk_2"], D, 0, 512, xa, "store", (work, 0, PAD))
        g_mv = Gemm(plan, "mem_v", a["xa_wv_2"], D, 0, 512, xa, "store", (work, 4, PAD))
        g_ob = Gemm(plan, "w_out rw", a["w_out_2"], D // 2, 0, D, xb, "add", (resid, 0, 0), x_from=8, k0=D // 2)
        g_xq = Gemm(plan, "xa_q", a["xa_wq_2"], D, 0, 512, xa, "store", (work, 8, PAD))
        g_xo = Gemm(plan, "xa_o", a["xa_wo_2"], 512, 0, D, xb, "add", (resid, 0, 0))
        ff2 = []
        for p in range(FF_PIECES):
            ff2 += [Gemm(plan, f"w1_{p}", a["ffn_w1_2"], D, p * D, D, xa, "relu2", (xb, 0, 0)),
                    Gemm(plan, f"w2_{p}", a["ffn_w2_2"], D, 0, D, xb, "add", (resid, 0, 0), k0=p * D)]

        def over(name, shape, region, byte):
            start = {"xa": xa_at, "xb": xb_at, "work": work_at}[region]
            return at(name, shape, F32, start + byte)

        masks = over("masks", [P, LEVELS, P], "work", 60 * COLS * 4)
        dnc = over("dnc", [P, 24, T], "xb", 0)
        dn_rn = over("dn_rn", [P, 2, 2 * T], "xb", 24576)
        slot = lambda name, n: over(name, [P, 8, P], "xb", 4096 * n)
        dn_at_, dn_n, dn_x, dn_xt, dn_nm, dn_tt, dn_e, dn_v = (
            slot(f"dn_{x}", n) for n, x in enumerate(("attn", "n", "x", "xt", "nm", "tt", "e", "v")))
        dn_eq = over("dn_eq", [P, 4, P], "xb", 4096 * 2)
        dn_v0 = over("dn_v0", [P, 4, P], "xb", 4096 * 6)
        dn_s1 = over("dn_s1", [P, 4, P], "xb", 4096 * 6 + 2048)
        dn_v1 = over("dn_v1", [P, 4, P], "xb", 4096 * 5)
        dn_k0 = sq[:, :, :].rearrange("p a (b c) -> p (a b) c", b=2)
        dn_sq = over("dn_sq", [P, 8, T], "xb", 0)
        dn_rr = over("dn_rr", [P, 8, T], "xb", 8192)
        dn_s8 = at("dn_s8", [P, T], F32)
        shift_d = at("shift_d", [P, 2, T], F32)
        gt, gc, eg, nbeg = small[:, 0:32], small[:, 32:48], small[:, 48:64], small[:, 64:80]
        ea, rw_mid, fac, omka = small[:, 80:81], small[:, 81:97], small[:, 97:105], small[:, 105:113]
        al = small[0:DN_H, 113:115]
        rw_c = over("rw_c", [P, 16, 132], "work", 0)
        rw_ep = over("rw_ep", [P, 16, 132], "work", 8448)
        rw_em = over("rw_em", [P, 16, 132], "work", 16896)
        rw_nm = over("rw_nm", [P, 8, P], "work", 25344)
        rw_rh = over("rw_rh", [P, 4, RW_D], "work", 29440)
        rw_sa = [over(f"rw_sa{c}", [P, 4, RW_D], "work", 30464 + 1024 * c) for c in range(2)]
        rw_st = over("rw_st", [P, 2, RW_D], "work", 32512)
        rw_bt = over("rw_bt", [P, 8, P], "work", 0)
        rw_kt = over("rw_kt", [P, 8, P], "work", 4096)
        rw_vt = over("rw_vt", [P, 8, 2, P], "work", 8192)
        rw_x = over("rw_x", [P, 8, P], "work", 16384)
        rw_xt = over("rw_xt", [P, 8, P], "work", 20480)
        rw_a = over("rw_a", [P, 8, T], "xa", 0)
        rw_kk = over("rw_kk", [P, 8, T], "xa", 8192)
        rw_mat = {n: over("rw_" + n, [P, 8, P], "xa", 16384 + 4096 * i) for i, n in enumerate(("ba", "ka", "br", "kr"))}
        rw_lw = over("rw_lw", [P, 1024], "xa", 16384)
        rw_g2 = over("rw_g2", [P, 1024], "xa", 20480)
        rw_bn = over("rw_bn", [P, 8, T], "xb", 16384)
        rw_d = over("rw_d", [P, 8, T], "xb", 16384 + 8192)
        rw_tt = over("rw_tt", [P, 8, P], "xb", 16384 + 8192)
        mem = over("mem", [P, DT, T], "work", 16 * COLS * 4)
        xs = over("xs", [P, 8, T], "work", 16 * COLS * 4)
        xp = over("xp", [P, 8, T], "work", 16 * COLS * 4 + 8192)
        xv = over("xv", [P, 4, 2, P], "work", 16 * COLS * 4 + 16384)
        xm = small[:, 120:136]

        inv_pe = [x + s_ for l in range(LEVELS) for x in ([f"t{l}", f"u{l}"] if l else ["t0"]) for s_ in "ab"]
        inv_dve = ["m0a", "m0b", "m1a", "u0a", "m1b", "u0b"]
        for l in range(1, LEVELS):
            inv_dve += ([f"m{l + 1}a", f"m{l + 1}b"] if l + 1 < LEVELS else []) + [f"u{l}a", f"u{l}b"]
        inv_act = [f"t{l}{s_}" for l in range(1, LEVELS) for s_ in "ab"]
        FOUR = {"a": (0, slice(0, 4)), "b": (1, slice(4, 8))}
        bank4 = lambda n: ps[n].rearrange("p (b c) -> p b c", b=4)

        def inverse_pe(pe, S, r, nm, x, xt, tt):
            for l in range(LEVELS):
                for s_, (n, four) in FOUR.items():
                    S.dve.wait(pe, f"m{l}{s_}", r)
                    if l:
                        S.dve.wait(pe, f"u{l - 1}{s_}", r)
                    for m in range(4):
                        ins = nc.tensor.matmul(bank4(n)[:, m], lhsT=nm[:, 4 * n + m],
                                               rhs=x[:, 4 * n + m] if l else const("ident"), start=True, stop=True)
                    S.pe.done(ins, f"t{l}{s_}", r)
                yield
                if not l:
                    continue
                for s_, (n, four) in FOUR.items():
                    S.act.wait(pe, f"t{l}{s_}", r)
                    for m in range(4 * n, 4 * n + 4):
                        if l + 1 < LEVELS:
                            nc.tensor.matmul(bank4(n)[:, m % 4], lhsT=xt[:, m], rhs=tt[:, m], start=True, stop=True)
                        ins = nc.tensor.matmul(bank4(2 + n)[:, m % 4], lhsT=tt[:, m], rhs=xt[:, m], start=True, stop=True)
                    S.pe.done(ins, f"u{l}{s_}", r)
                yield

        def inverse_act(act, S, r, tt):
            yield
            for l in range(1, LEVELS):
                for s_, (n, four) in FOUR.items():
                    S.pe.wait(act, f"t{l}{s_}", r)
                    if l > 1:
                        S.pe.wait(act, f"u{l - 1}{s_}", r)
                    S.act.done(nc.scalar.activation(tt[:, four], bank4(n), ACT.Copy), f"t{l}{s_}", r)
                yield
                yield

        mask = lambda l: masks[:, l, None, :].to_broadcast([P, 4, P])

        def inverse_m0_dve(S, r, n_, nm):
            for s_, (n, four) in FOUR.items():
                S.dve.done(nc.vector.tensor_tensor(nm[:, four], n_[:, four], mask(0), ALU.mult), f"m0{s_}", r)

        def inverse_dve(dve, S, r, n_, nm, x, xt):
            eye = const("ident")[:, None, :].to_broadcast([P, 4, P])
            for l in range(LEVELS):
                for s_, (n, four) in FOUR.items():
                    if not l:
                        S.dve.wait(dve, f"m0{s_}", r)
                        dve_link(nc.vector.tensor_tensor(xt[:, four], eye, nm[:, four], ALU.subtract))
                    S.pe.wait(dve, f"t{l}{s_}", r)
                    if l + 1 < LEVELS:
                        S.dve.done(nc.vector.tensor_tensor(nm[:, four], n_[:, four], mask(l + 1), ALU.mult),
                                   f"m{l + 1}{s_}", r)
                    if not l:
                        S.dve.done(nc.vector.tensor_tensor(x[:, four], eye, bank4(n), ALU.subtract), f"u0{s_}", r)
                yield
                if not l:
                    continue
                for s_, (n, four) in FOUR.items():
                    S.dve.wait(dve, f"u{l - 1}{s_}", r)
                    S.pe.wait(dve, f"u{l}{s_}", r)
                    if l + 1 < LEVELS:
                        nc.vector.tensor_tensor(x[:, four], x[:, four], bank4(n), ALU.subtract)
                    S.dve.done(nc.vector.tensor_tensor(xt[:, four], xt[:, four], bank4(2 + n), ALU.subtract),
                               f"u{l}{s_}", r)
                yield

        class Trio:

            def __init__(self, name, pe, dve, act):
                self.pe, self.dve, self.act = (Steps(sem(f"{name}_{e}"), x) for e, x in
                                               (("pe", pe), ("dve", dve), ("act", act)))

        dn_acc, dn_sig, dn_silu = sem("dn_acc"), sem("dn_sig"), sem("dn_silu")

        def dn_conv_dve(dve, m):
            if m >= 1:
                pair = slice(2 * (m - 1), 2 * m)
                dve.wait_ge(dn_sig, m)
                if m <= 12:
                    nc.vector.tensor_tensor(work[:, pair, PAD:COLS], work[:, pair, PAD:COLS], dnc[:, pair],
                                            ALU.mult).then_inc(dn_silu, 1)
                else:
                    nc.vector.tensor_tensor(work[:, pair, PAD:COLS], work[:, pair, PAD:COLS],
                                            dnc[:, 2 * (m - 13):2 * (m - 12)], ALU.mult).then_inc(dn_silu, 1)
            if m < 12:
                dve.wait_ge(evacuated, g_dn.b0 + m + 3)
                for j in range(4):
                    for c in (2 * m, 2 * m + 1):
                        x = work[:, c, PAD - 3 + j:PAD - 3 + j + T]
                        if j == 0:
                            ins = nc.vector.tensor_scalar(dnc[:, c], x, v2("dn_conv_w_2", c), None, ALU.mult)
                        else:
                            ins = nc.vector.scalar_tensor_tensor(out=dnc[:, c], in0=x, scalar=v2("dn_conv_w_2", 24 * j + c),
                                                                 in1=dnc[:, c], op0=ALU.mult, op1=ALU.add)
                        if j < 3:
                            seq["dve"] += 1
                            ins.then_inc(dve_seq, 1)
                    if j < 3:
                        dve.wait_ge(dve_seq, seq["dve"])
                ins.then_inc(dn_acc, 1)

        def dn_conv_act(act, m):
            if m < 12:
                act.wait_ge(dn_acc, m + 1)
                pair = slice(2 * m, 2 * m + 2)
                nc.scalar.activation(work[:, pair, PAD:COLS], dnc[:, pair], ACT.Sigmoid).then_inc(dn_sig, 1)
            else:
                act.wait_ge(evacuated, g_dn.b0 + m + 3)
                act.wait_ge(dn_silu, m - 11)
                pair = slice(2 * m, 2 * m + 2)
                nc.scalar.activation(dnc[:, 2 * (m - 12):2 * (m - 11)], work[:, pair, PAD:COLS],
                                     ACT.Sigmoid).then_inc(dn_sig, 1)

        L2 = Trio("l2", ["sum"], ["done"], ["sq", "root"])
        GT = Trio("gates2", ["t", "gc"], ["dt", "soft", "g", "t", "gc", "nbeg"], ["beta", "ln", "ea", "eg"])

        def l2_pe(pe, m):
            h = m - 9
            if 0 <= h < DN_H:
                L2.act.wait(pe, "sq", h)
                if h >= 2:
                    L2.act.wait(pe, "root", h - 2)
                L2.pe.done(nc.tensor.matmul(ps[h % 2], lhsT=const("ones"), rhs=sq[:, :, :].rearrange("p a b -> p (a b)"),
                                            start=True, stop=True), "sum", h)

        def l2_act(act, m):
            h = m - 9
            if 0 <= h < DN_H:
                L2.pe.wait(act, "sum", h)
                if h >= 2:
                    L2.dve.wait(act, "done", h - 2)
                act_link(nc.scalar.activation(dn_rn[:, h % 2], ps[h % 2], ACT.Ln, bias=EPS))
                L2.act.done(nc.scalar.activation(dn_rn[:, h % 2], dn_rn[:, h % 2], ACT.Exp, scale=-0.5), "root", h)
            h = m - 8
            if 0 <= h < DN_H:
                act.wait_ge(dn_silu, 8)
                L2.act.done(nc.scalar.activation(sq[:, :, :], work[:, DQ + h:DQ + h + 9:8, PAD:COLS], ACT.Square), "sq", h)

        def l2_dve(dve, m):
            h = m - 9
            if 0 <= h < DN_H:
                L2.act.wait(dve, "root", h)
                dve.wait_ge(dn_silu, 8)
                q, k = (work[:, t + h, PAD:COLS] for t in (DQ, DK))
                nc.vector.scalar_tensor_tensor(out=q, in0=q, scalar=128 ** -0.5, in1=dn_rn[:, h % 2, 0:T],
                                               op0=ALU.mult, op1=ALU.mult)
                L2.dve.done(nc.vector.tensor_tensor(k, k, dn_rn[:, h % 2, T:2 * T], ALU.mult), "done", h)

        ga, gb, s8 = work[0:DN_H, GA, PAD:COLS], work[0:DN_H, GB, PAD:COLS], dn_s8[0:DN_H, :]

        def gates_act(act):
            blocks_out(act, g_gab)
            act.wait_ge(masks_in, 32)
            GT.act.done(nc.scalar.activation(gb, gb, ACT.Sigmoid), "beta")
            GT.dve.wait(act, "dt")
            act_link(nc.scalar.activation(s8, ga, ACT.Abs))
            act_link(nc.scalar.activation(s8, s8, ACT.Exp, scale=-1.0))
            GT.act.done(nc.scalar.activation(s8, s8, ACT.Ln, bias=1.0), "ln")
            GT.act.done(nc.scalar.activation(ea[0:DN_H, :], al[:, 0:1], ACT.Exp), "ea")
            yield
            yield
            GT.pe.wait(act, "gc")
            GT.act.done(nc.scalar.activation(eg, ps[3][:, 0:16], ACT.Exp), "eg")
            yield

        def gates_dve(dve):
            blocks_out(dve, g_gab)
            dve.wait_ge(masks_in, 32)
            GT.dve.done(nc.vector.tensor_scalar(ga, ga, al[:, 1:2], None, ALU.add), "dt")
            GT.act.wait(dve, "ln")
            GT.dve.done(nc.vector.scalar_tensor_tensor(out=s8, in0=ga, scalar=0.0, in1=s8, op0=ALU.max, op1=ALU.add), "soft")
            GT.dve.wait(dve, "soft")
            GT.act.wait(dve, "ea")
            GT.dve.done(nc.vector.tensor_scalar(s8, s8, ea[0:DN_H, :], -1.0, ALU.mult, ALU.mult), "g")
            yield
            GT.pe.wait(dve, "t")
            GT.dve.done(nc.vector.tensor_copy(gt, ps[2][:, 0:32]), "t")
            yield
            GT.pe.wait(dve, "gc")
            GT.act.wait(dve, "eg")
            GT.dve.done(nc.vector.tensor_copy(gc, ps[3][:, 0:16]), "gc")
            GT.dve.wait(dve, "gc")
            GT.dve.done(nc.vector.scalar_tensor_tensor(out=nbeg, in0=gt[:, 16:32], scalar=-1.0, in1=eg, op0=ALU.mult,
                                                       op1=ALU.mult), "nbeg")
            yield

        def gates_pe(pe):
            yield
            L2.dve.wait(pe, "done", DN_H - 1)
            GT.dve.wait(pe, "g")
            GT.act.wait(pe, "beta")
            for c in range(2):
                for n, x in enumerate((s8, gb)):
                    ins = nc.tensor.transpose(ps[2][:, 16 * n + 8 * c:16 * n + 8 * c + 8], x[:, c * P:(c + 1) * P],
                                              const("ident")[0:DN_H, 0:DN_H])
            GT.pe.done(ins, "t")
            yield
            GT.dve.wait(pe, "t")
            GT.pe.done(nc.tensor.matmul(ps[3][:, 0:16], lhsT=const("incl"), rhs=gt[:, 0:16], start=True, stop=True), "gc")
            yield

        DN = Trio("dn",
                  ["row", "kk", "kq", "v", "k"] + inv_pe + ["v0", "s1", "m1", "v1", "o"],
                  ["min", "mask", "n", "n2", "attn", "qg"] + inv_dve + ["rhs1", "o"],
                  ["e", "eq", "v", "k"] + inv_act + ["v0", "s1", "v1"])
        quad = lambda n: p4[:, n:n + 2, :].rearrange("p a (b c) -> p (a b) c", b=4)
        units = [(hh, c) for hh in range(4) for c in range(2)]

        def chunk(tile, c):
            return work[:, tile, PAD + c * P:PAD + (c + 1) * P]

        def dn_pe(pe, r):
            H = 4 * r
            q2 = lambda base, n: p4[:, base + n // 4, (n % 4) * P:(n % 4 + 1) * P]
            if r:
                DN.dve.wait(pe, "o", r - 1)
            else:
                GT.dve.wait(pe, "nbeg")
            for n, (hh, c) in enumerate(units):
                col = gt[:, 8 * c + H + hh:8 * c + H + hh + 1]
                nc.tensor.matmul(q2(0, n), lhsT=col.to_broadcast([P, P]), rhs=const("incl"), start=True, stop=True)
            for n, (hh, c) in enumerate(units):
                col = gt[:, 16 + 8 * c + H + hh:16 + 8 * c + H + hh + 1]
                ins = nc.tensor.matmul(q2(2, n), lhsT=col.to_broadcast([P, P]), rhs=const("ident"), start=True, stop=True)
            DN.pe.done(ins, "row", r)
            yield
            DN.dve.wait(pe, "min", r)
            DN.act.wait(pe, "eq", r)
            for n, (hh, c) in enumerate(units):
                k = chunk(DK + H + hh, c)
                ins = nc.tensor.matmul(q2(0, n), lhsT=k, rhs=k, start=True, stop=True)
            DN.pe.done(ins, "kk", r)
            yield
            DN.dve.wait(pe, "n", r)
            for n, (hh, c) in enumerate(units):
                ins = nc.tensor.matmul(q2(0, n), lhsT=chunk(DK + H + hh, c), rhs=chunk(DQ + H + hh, c), start=True, stop=True)
            DN.pe.done(ins, "kq", r)
            yield
            DN.dve.wait(pe, "n2", r)
            for n, (hh, c) in enumerate(units):
                ins = nc.tensor.transpose(q2(2, n), chunk(DV + H + hh, c), const("ident"))
            DN.pe.done(ins, "v", r)
            DN.dve.wait(pe, "attn", r)
            for hh in range(4):
                ins = nc.tensor.transpose(q2(0, hh), chunk(DK + H + hh, 0), const("ident"))
            DN.pe.done(ins, "k", r)
            yield
            DN.act.wait(pe, "k", r)
            yield from inverse_pe(pe, DN, r, dn_nm, dn_x, dn_xt, dn_tt)
            DN.dve.wait(pe, f"u{LEVELS - 1}b", r)
            for hh in range(4):
                ins = nc.tensor.matmul(q2(0, hh), lhsT=dn_xt[:, 2 * hh], rhs=dn_v[:, 2 * hh], start=True, stop=True)
            DN.pe.done(ins, "v0", r)
            yield
            DN.act.wait(pe, "v0", r)
            for hh in range(4):
                ins = nc.tensor.matmul(q2(1, hh), lhsT=dn_k0[:, hh], rhs=dn_v0[:, hh], start=True, stop=True)
            DN.pe.done(ins, "s1", r)
            yield
            DN.act.wait(pe, "s1", r)
            for hh in range(4):
                ins = nc.tensor.matmul(q2(2, hh), lhsT=chunk(DK + H + hh, 1), rhs=dn_s1[:, hh], start=True, stop=True)
            DN.pe.done(ins, "m1", r)
            yield
            DN.dve.wait(pe, "rhs1", r)
            for hh in range(4):
                ins = nc.tensor.matmul(q2(3, hh), lhsT=dn_xt[:, 2 * hh + 1], rhs=dn_v[:, 2 * hh + 1], start=True, stop=True)
            DN.pe.done(ins, "v1", r)
            yield
            DN.act.wait(pe, "v1", r)
            for hh in range(4):
                o = lambda c: p4[:, hh // 2, (hh % 2) * T + c * P:(hh % 2) * T + (c + 1) * P]
                nc.tensor.matmul(o(0), lhsT=dn_v0[:, hh], rhs=dn_at_[:, 2 * hh], start=True, stop=True)
                nc.tensor.matmul(o(1), lhsT=dn_s1[:, hh], rhs=chunk(DQ + H + hh, 1), start=True, stop=False)
                ins = nc.tensor.matmul(o(1), lhsT=dn_v1[:, hh], rhs=dn_at_[:, 2 * hh + 1], start=False, stop=True)
            DN.pe.done(ins, "o", r)
            yield

        def dn_act(act, r):
            H = 4 * r
            DN.dve.wait(act, "min", r)
            DN.act.done(nc.scalar.activation(dn_e[:, :, :], dn_e[:, :, :], ACT.Exp), "e", r)
            DN.act.done(nc.scalar.activation(dn_eq[:, :, :], quad(0)[:, 1:8:2, :], ACT.Exp), "eq", r)
            yield
            yield
            yield
            DN.pe.wait(act, "v", r)
            for n, (hh, c) in enumerate(units):
                beta = gt[:, 16 + 8 * c + H + hh:16 + 8 * c + H + hh + 1]
                ins = nc.scalar.activation(dn_v[:, n], quad(2)[:, n], ACT.Copy, scale=beta)
            DN.act.done(ins, "v", r)
            DN.pe.wait(act, "k", r)
            for hh in range(4):
                ins = nc.scalar.activation(dn_k0[:, hh], quad(0)[:, hh], ACT.Copy, scale=dn_e[:, 2 * hh, P - 1:P])
            DN.act.done(ins, "k", r)
            yield
            yield from inverse_act(act, DN, r, dn_tt)
            four = lambda n: ps[n].rearrange("p (b c) -> p b c", b=4)
            for name, bank, to in (("v0", 0, dn_v0), ("s1", 1, dn_s1), ("v1", 3, dn_v1)):
                DN.pe.wait(act, name, r)
                DN.act.done(nc.scalar.activation(to[:, :, :], four(bank), ACT.Copy), name, r)
                yield
                if name == "s1":
                    yield
            yield

        def dn_dve(dve, r):
            H = 4 * r
            DN.pe.wait(dve, "row", r)
            for n, (hh, c) in enumerate(units):
                col = gc[:, 8 * c + H + hh:8 * c + H + hh + 1]
                ins = nc.vector.tensor_scalar(dn_e[:, n], quad(0)[:, n], col, 0.0, ALU.subtract, ALU.min)
            DN.dve.done(ins, "min", r)
            DN.act.wait(dve, "e", r)
            DN.dve.done(nc.vector.tensor_tensor(dn_e[:, :, :], dn_e[:, :, :],
                                                const("incl")[:, None, :].to_broadcast([P, 8, P]), ALU.mult), "mask", r)
            yield
            DN.dve.wait(dve, "mask", r)
            DN.pe.wait(dve, "kk", r)
            DN.dve.done(nc.vector.tensor_tensor(dn_n[:, :, :], quad(0), dn_e[:, :, :], ALU.mult), "n", r)
            DN.dve.wait(dve, "n", r)
            DN.dve.done(nc.vector.tensor_tensor(dn_n[:, :, :], dn_n[:, :, :], quad(2), ALU.mult), "n2", r)
            yield
            DN.pe.wait(dve, "kq", r)
            DN.dve.done(nc.vector.tensor_tensor(dn_at_[:, :, :], quad(0), dn_e[:, :, :], ALU.mult), "attn", r)
            DN.act.wait(dve, "eq", r)
            q1 = work[:, DQ + H:DQ + H + 4, PAD + P:COLS]
            DN.dve.done(nc.vector.tensor_tensor(q1, q1, dn_eq[:, :, :], ALU.mult), "qg", r)
            yield
            DN.dve.wait(dve, "qg", r)
            inverse_m0_dve(DN, r, dn_n, dn_nm)
            yield
            yield from inverse_dve(dve, DN, r, dn_n, dn_nm, dn_x, dn_xt)
            yield
            yield
            DN.pe.wait(dve, "m1", r)
            for hh in range(4):
                ins = nc.vector.scalar_tensor_tensor(out=dn_v[:, 2 * hh + 1], in0=quad(2)[:, hh],
                                                     scalar=nbeg[:, 8 + H + hh:8 + H + hh + 1], in1=dn_v[:, 2 * hh + 1],
                                                     op0=ALU.mult, op1=ALU.add)
            DN.dve.done(ins, "rhs1", r)
            yield
            yield
            DN.pe.wait(dve, "o", r)
            DN.dve.done(nc.vector.tensor_copy(work[:, DQ + H:DQ + H + 4, PAD:COLS],
                                              p4[:, 0:2, :].rearrange("p a (b c) -> p (a b) c", b=2)), "o", r)
            yield

        DF = Trio("dnf", ["sum"], ["o1", "o2", "lo"], ["sq", "ln", "root", "hi"])
        all4 = p4[:, :, :].rearrange("p a (b c) -> p (a b) c", b=2)
        dn_o = work[:, DQ:DQ + 8, PAD:COLS]

        def eight(ones, src):
            for j in range(8):
                ins = nc.tensor.matmul(all4[:, j], lhsT=const(ones), rhs=src[:, j], start=True, stop=True)
            return ins

        def dnf_pe(pe):
            yield
            DF.act.wait(pe, "sq")
            DF.pe.done(eight("ones", dn_sq), "sum")
            yield

        def dnf_act(act):
            DN.dve.wait(act, "o", 1)
            DF.act.done(nc.scalar.activation(dn_sq[:, :, :], dn_o, ACT.Square), "sq")
            yield
            DF.pe.wait(act, "sum")
            DF.act.done(nc.scalar.activation(dn_rr[:, :, :], all4, ACT.Ln, scale=1.0 / 128, bias=EPS), "ln")
            DF.act.wait(act, "ln")
            DF.act.done(nc.scalar.activation(dn_rr[:, :, :], dn_rr[:, :, :], ACT.Exp, scale=-0.5), "root")
            yield
            yield
            DF.dve.wait(act, "o2")
            DF.act.done(nc.scalar.activation(xb[:, 0:8, 0:T], dn_o, ACT.Copy), "hi")

        def dnf_dve(dve):
            yield
            DF.act.wait(dve, "root")
            DN.dve.wait(dve, "o", 1)
            DF.dve.done(nc.vector.scalar_tensor_tensor(out=dn_o, in0=dn_o, scalar=v2("dn_norm_w_2"), in1=dn_rr[:, :, :],
                                                       op0=ALU.mult, op1=ALU.mult), "o1")
            yield
            yield
            DF.dve.wait(dve, "o1")
            DF.dve.done(nc.vector.tensor_tensor(dn_o, dn_o, work[:, DZ:DZ + 8, PAD:COLS], ALU.mult), "o2")
            DF.act.wait(dve, "hi")
            DF.dve.done(nc.vector.tensor_tensor(xb[:, 0:8, T:2 * T], dn_o, xb[:, 0:8, 0:T].bitcast(F32), ALU.subtract), "lo")

        def dn_core(eng, gates, rounds, final):
            yield from gates(eng)
            for r in range(2):
                yield from rounds(eng, r)
            yield from final(eng)

        def step_of(gen):
            return lambda: next(gen, None)

        def rest_of(gen):
            for _ in gen:
                pass

        rw_r, rw_k, rw_v = (work[:, t:t + 8, PAD:COLS] for t in (RR, RK, RV))
        RP = Trio("rwp", ["kk", "w", "a", "bonus", "t0", "t1", "t2", "t3"],
                  ["shift", "max", "scan", "sc", "k", "bonus", "kk", "bn", "rho", "ba", "alpha", "beta", "kappa", "t1", "t3"],
                  ["sq", "tanh", "kkr", "w", "a", "kf", "ln", "root", "ep", "em", "t0", "t2"])
        lora_in, k_shifted = sem("lora_in"), sem("k_shifted")
        C = lambda x, a_, b_: x[:, :, a_:b_]
        ctok = lambda x, a_: x[:, :, a_:a_ + P].rearrange("p (j c) t -> p j c t", c=2)
        jc = lambda x: x.rearrange("p j (c t) -> p j c t", c=2)
        pg8 = pg[:, :, :, :].rearrange("p a b (c t) -> p (a b c) t", c=2)
        pgq = lambda n: pg[:, n].rearrange("p a (b c) -> p (a b) c", b=4)

        def shift_dve(dve, m):
            dve.wait_ge(evacuated, g_rw.b0 + m + 3)
            t0 = RR + 2 * m
            dve_link(nc.vector.tensor_tensor(shift_d[:, :, :], work[:, t0:t0 + 2, PAD - 1:COLS - 1],
                                             work[:, t0:t0 + 2, PAD:COLS], ALU.subtract))
            for j in range(2):
                x = work[:, t0 + j, PAD:COLS]
                ins = nc.vector.scalar_tensor_tensor(out=x, in0=shift_d[:, j], scalar=v2("rw_mu_2", 2 * m + j), in1=x,
                                                     op0=ALU.mult, op1=ALU.add)
            if m == 7:
                ins.then_inc(k_shifted, 1)
                dve.wait_ge(k_shifted, 1)
            elif m < g_rw.blocks - 1:
                dve_link(ins)
            else:
                RP.dve.done(ins, "shift")

        def rwp_pe(pe):
            RP.act.wait(pe, "sq")
            blocks_out(pe, g_rw)
            RP.pe.done(eight("ones_head", rw_d), "kk")
            pe.wait_ge(lora_in, 16 * 2)
            RP.act.wait(pe, "tanh")
            for j in range(8):
                ins = nc.tensor.matmul(pg8[:, j], lhsT=rw_lw[0:64, j * P:(j + 1) * P],
                                       rhs=work[0:64, RL, PAD:COLS], start=True, stop=True)
            RP.pe.done(ins, "w")
            RP.dve.wait(pe, "max")
            for j in range(8):
                ins = nc.tensor.matmul(all4[:, j], lhsT=rw_lw[64:P, j * P:(j + 1) * P],
                                       rhs=work[64:P, RL, PAD:COLS], start=True, stop=True)
            RP.pe.done(ins, "a")
            RP.act.wait(pe, "w")
            RP.dve.wait(pe, "bonus")
            for j in range(8):
                ins = nc.tensor.matmul(pg8[:, j], lhsT=const("ones_head"), rhs=rw_d[:, j], start=True, stop=True)
            RP.pe.done(ins, "bonus")
            RP.act.wait(pe, "a")
            RP.dve.wait(pe, "beta")
            for n, (src, ready) in enumerate(((rw_a, "beta"), (work[:, RK:RK + 8, PAD:COLS], "kappa"))):
                RP.dve.wait(pe, ready)
                for j in range(8):
                    ins = nc.tensor.transpose(p4[:, 2 * n + j // 4, (j % 4) * P:(j % 4 + 1) * P], src[:, j, 0:P],
                                              const("ident"))
                RP.pe.done(ins, f"t{n}")
            RP.dve.wait(pe, "bn")
            for n in range(2):
                for j in range(8):
                    ins = nc.tensor.transpose(pgq(n)[:, j], chunk(RV + 4 * n + j // 2, j % 2), const("ident"))
                RP.pe.done(ins, f"t{2 + n}")

        def rwp_first_act(act):
            act.wait_ge(k_shifted, 1)
            for j in range(8):
                ins = nc.scalar.activation(rw_d[:, j], work[:, RK + j, PAD:COLS], ACT.Square, scale=v2("rw_k_k_2", j))
            RP.act.done(ins, "sq")
            RP.dve.wait(act, "shift")
            nc.scalar.activation(work[0:64, RL, PAD:COLS], work[0:64, RL, PAD:COLS], ACT.Tanh)
            RP.act.done(nc.scalar.activation(work[:, RG, PAD:COLS], work[:, RG, PAD:COLS], ACT.Sigmoid), "tanh")

        def rwp_act(act):
            blocks_out(act, g_rw)
            for j in range(8):
                ins = nc.scalar.activation(rw_kk[:, j], work[:, RK + j, PAD:COLS], ACT.Copy, scale=v2("rw_k_k_2", j))
            RP.act.done(ins, "kkr")
            DF.dve.wait(act, "lo")
            RP.pe.wait(act, "w")
            for j in range(8):
                ins = nc.scalar.activation(rw_c[:, 2 * j:2 * j + 2, 4:132], pg8[:, j].rearrange("p (c t) -> p c t", c=2),
                                           ACT.Sigmoid, bias=v2("rw_w0_2", j))
            RP.act.done(ins, "w")
            RP.pe.wait(act, "a")
            for j in range(8):
                ins = nc.scalar.activation(rw_a[:, j], all4[:, j], ACT.Sigmoid, bias=v2("rw_a0_2", j))
            RP.act.done(ins, "a")
            RP.act.wait(act, "a")
            for j in range(8):
                ins = nc.scalar.activation(rw_d[:, j], rw_a[:, j], ACT.Identity, scale=v2("rw_k_a_2", j),
                                           bias=omka[:, j:j + 1])
            RP.act.done(ins, "kf")
            RP.dve.wait(act, "max")
            RP.act.done(nc.scalar.activation(rw_root, rw_root, ACT.Ln), "ln")
            RP.act.wait(act, "ln")
            RP.act.done(nc.scalar.activation(rw_root, rw_root, ACT.Exp, scale=-0.5), "root")
            RP.dve.wait(act, "sc")
            RP.dve.wait(act, "kk")
            RP.act.done(nc.scalar.activation(C(rw_ep, 3, 132), C(rw_c, 3, 132), ACT.Exp, scale=-RW_DECAY), "ep")
            RP.act.done(nc.scalar.activation(C(rw_em, 3, 132), C(rw_c, 3, 132), ACT.Exp, scale=RW_DECAY), "em")
            RP.pe.wait(act, "t0")
            RP.dve.wait(act, "kappa")
            RP.act.done(nc.scalar.activation(rw_bt[:, :, :], quad(0), ACT.Copy), "t0")
            RP.pe.wait(act, "t2")
            RP.act.done(nc.scalar.activation(rw_vt[:, 0:4].rearrange("p j c t -> p (j c) t"), pgq(0), ACT.Copy), "t2")

        rw_root = over("rw_root", [P, 8, T], "work", 8448)[:, :, :]

        def rwp_dve(dve):
            DF.dve.wait(dve, "lo")
            nc.vector.memset(rw_c[:, :, 3:4], 0.0)
            RP.pe.wait(dve, "kk")
            RP.dve.done(nc.vector.tensor_scalar(rw_root, all4, 1e-24, None, ALU.max), "max")
            RP.act.wait(dve, "w")
            for c in range(16):
                ins = nc.vector.tensor_tensor_scan(rw_c[:, c, 4:132], const("ones"), rw_c[:, c, 4:132], 0.0, ALU.mult,
                                                   ALU.add)
            RP.dve.done(ins, "scan")
            RP.dve.wait(dve, "scan")
            dve_link(nc.vector.tensor_copy(rw_mid, rw_c[:, :, 67]))
            RP.dve.done(nc.vector.tensor_tensor(C(rw_c, 3, 132), C(rw_c, 3, 132),
                                                rw_mid[:, :, None].to_broadcast([P, 16, 129]), ALU.subtract), "sc")
            RP.act.wait(dve, "kf")
            RP.dve.done(nc.vector.tensor_tensor(rw_k, rw_k, rw_d[:, :, :], ALU.mult), "k")
            RP.dve.wait(dve, "k")
            for j in range(8):
                ins = nc.vector.scalar_tensor_tensor(out=rw_d[:, j], in0=work[:, RR + j, PAD:COLS],
                                                     scalar=v2("rw_r_k_2", j), in1=work[:, RK + j, PAD:COLS],
                                                     op0=ALU.mult, op1=ALU.mult)
            RP.dve.done(ins, "bonus")
            RP.act.wait(dve, "root")
            RP.dve.done(nc.vector.tensor_tensor(rw_kk[:, :, :], rw_kk[:, :, :], rw_root, ALU.mult), "kk")
            RP.pe.wait(dve, "bonus")
            RP.dve.done(nc.vector.tensor_tensor(rw_bn[:, :, :], pg8, rw_v, ALU.mult), "bn")
            RP.act.wait(dve, "ep")
            RP.dve.wait(dve, "bonus")
            RP.dve.done(nc.vector.tensor_tensor(jc(rw_r), jc(rw_r), ctok(rw_ep, 4), ALU.mult), "rho")
            RP.dve.wait(dve, "kk")
            RP.dve.done(nc.vector.tensor_tensor(rw_a[:, :, :], rw_a[:, :, :], rw_kk[:, :, :], ALU.mult), "ba")
            RP.dve.wait(dve, "ba")
            RP.dve.done(nc.vector.tensor_tensor(jc(rw_kk[:, :, :]), jc(rw_kk[:, :, :]), ctok(rw_ep, 3), ALU.mult), "alpha")
            RP.act.wait(dve, "em")
            RP.dve.done(nc.vector.tensor_tensor(jc(rw_a[:, :, :]), jc(rw_a[:, :, :]), ctok(rw_em, 4), ALU.mult), "beta")
            dve_link(nc.vector.tensor_tensor(fac, rw_ep[:, 0:16:2, 131], rw_em[:, 1:16:2, 3], ALU.mult))
            RP.dve.done(nc.vector.tensor_tensor(jc(rw_k), jc(rw_k), ctok(rw_em, 4), ALU.mult), "kappa")
            RP.dve.wait(dve, "kappa")
            RP.pe.wait(dve, "t1")
            RP.dve.done(nc.vector.tensor_copy(rw_kt[:, :, :], quad(2)), "t1")
            RP.pe.wait(dve, "t3")
            RP.dve.done(nc.vector.tensor_copy(rw_vt[:, 4:8].rearrange("p j c t -> p (j c) t"), pgq(1)), "t3")

        MATS = [("ba", rw_a, rw_kk), ("ka", work[:, RK:RK + 8, PAD:COLS], rw_kk), ("br", rw_a, work[:, RR:RR + 8, PAD:COLS]),
                ("kr", work[:, RK:RK + 8, PAD:COLS], work[:, RR:RR + 8, PAD:COLS])]
        RW = Trio("rw", ["t0a", "t0b", "br", "kr"] + inv_pe[2:] + ["r0", "sa0", "st", "r1", "sa1", "y"],
                  ["m0a", "m0b", "ka", "m1a", "u0a", "m1b", "u0b", "kr"] + inv_dve[6:] + ["y"],
                  ["ba", "br"] + inv_act + ["r0", "sa0", "st", "r1", "sa1"])

        unit = lambda hh, c: 4 * (hh % 2) + 2 * (hh // 2) + c
        head = lambda hh: 2 * (hh % 2) + hh // 2

        r_of = [lambda hh: pg[:, 1, 1, head(hh) * 64:(head(hh) + 1) * 64],
                lambda hh: pg[:, 0, hh % 2, (hh // 2) * 64:(hh // 2 + 1) * 64]]
        y_bank = pg[:, 1, 0]
        st_bank, sa_bank = pg[:, 1, 1, 0:P], pg[:, 1, 1, T:2 * T]

        MT = Steps(sem("rw_mats"), ["ba", "ka"])

        def mats(pe, first, r):
            for i in range(first, first + 2):
                name, left, right = MATS[i]
                for hh, c in units:
                    n, j, hb = unit(hh, c), 2 * r + hh // 2, 64 * (hh % 2)
                    L, R = left[hb:hb + 64, j, c * P:(c + 1) * P], right[hb:hb + 64, j, c * P:(c + 1) * P]
                    bank = p4[:, 2 * i + n // 4] if i < 2 else pg[:, i - 2, n // 4]
                    o = (n % 4) * P
                    nc.tensor.matmul(bank[0:64, o:o + P], lhsT=L[:, 0:64], rhs=R, start=True, stop=True)
                    ins = nc.tensor.matmul(bank[64:P, o + 64:o + P], lhsT=L[:, 64:P], rhs=R[:, 64:P], start=True,
                                           stop=True)
                    if (hh, c) == units[-1]:
                        (MT if i < 2 else RW.pe).done(ins, name, r)
                    if c:
                        yield

        def rw_pe(pe, r):
            if not r:
                rest_of(mats(pe, 0, 0))
            RW.act.wait(pe, "ba", r)
            inverse = inverse_pe(pe, RW, r, rw_nm, rw_x, rw_xt, rw_tt)
            next(inverse)
            if r:
                RW.dve.wait(pe, "y", r - 1)
            rest_of(mats(pe, 2, r))
            rest_of(inverse)
            RW.act.wait(pe, "br", r)
            RW.dve.wait(pe, "kr", r)
            ka, br, kr = rw_mat["ka"], rw_mat["br"], rw_mat["kr"]
            place = lambda hh: (2 * r + hh // 2, 64 * (hh % 2))
            vtok = lambda hh, c: rw_vt[:, 2 * r + hh // 2, c, 64 * (hh % 2):64 * (hh % 2) + 64]
            y_of = lambda hh, c: y_bank[64 * (hh % 2):64 * (hh % 2) + 64, (hh // 2) * T + c * P:(hh // 2) * T + (c + 1) * P]
            for hh in range(4):
                for c in range(2):
                    nc.tensor.matmul(y_of(hh, c), lhsT=vtok(hh, c), rhs=kr[:, unit(hh, c)],
                                     start=(hh < 2 and not c), stop=False)
                nc.tensor.matmul(r_of[1](hh), lhsT=ka[:, unit(hh, 1)], rhs=vtok(hh, 1), start=(hh < 2), stop=False)
            for hh in range(4):
                ins = nc.tensor.matmul(r_of[0](hh), lhsT=ka[:, unit(hh, 0)], rhs=vtok(hh, 0), start=True, stop=True)
            RW.pe.done(ins, "r0", r)
            RW.dve.wait(pe, f"u{LEVELS - 1}b", r)
            ahead = mats(pe, 0, r + 1) if r < 3 else iter(())
            next(ahead, None)
            RW.act.wait(pe, "r0", r)
            for hh in range(4):
                ins = nc.tensor.matmul(sa_bank[:, hh * 64:(hh + 1) * 64], lhsT=rw_xt[:, unit(hh, 0)], rhs=rw_rh[:, head(hh)],
                                       start=True, stop=True)
            RW.pe.done(ins, "sa0", r)
            next(ahead, None)
            next(ahead, None)
            RW.act.wait(pe, "sa0", r)
            for hh in range(4):
                j, hb = place(hh)
                o = st_bank[hb:hb + 64, (hh // 2) * 64:(hh // 2) * 64 + 64]
                nc.tensor.matmul(o, lhsT=rw_bt[:, j, hb:hb + 64], rhs=rw_sa[0][:, hh], start=True, stop=False)
                ins = nc.tensor.matmul(o, lhsT=rw_kt[:, j, hb:hb + 64], rhs=vtok(hh, 0), start=False, stop=True)
            RW.pe.done(ins, "st", r)
            next(ahead, None)
            next(ahead, None)
            RW.act.wait(pe, "st", r)
            for hh in range(4):
                j, hb = place(hh)
                ins = nc.tensor.matmul(r_of[1](hh), lhsT=rw_kk[hb:hb + 64, j, P:T], rhs=rw_st[hb:hb + 64, hh // 2],
                                       start=False, stop=(hh >= 2))
            RW.pe.done(ins, "r1", r)
            next(ahead, None)
            next(ahead, None)
            RW.act.wait(pe, "r1", r)
            for hh in range(4):
                ins = nc.tensor.matmul(sa_bank[:, hh * 64:(hh + 1) * 64], lhsT=rw_xt[:, unit(hh, 1)], rhs=rw_rh[:, head(hh)],
                                       start=True, stop=True)
            RW.pe.done(ins, "sa1", r)
            for hh in range(4):
                j, hb = place(hh)
                nc.tensor.matmul(y_of(hh, 1), lhsT=rw_st[hb:hb + 64, hh // 2], rhs=work[hb:hb + 64, RR + j, PAD + P:COLS],
                                 start=False, stop=False)
                nc.tensor.matmul(y_of(hh, 0), lhsT=rw_sa[0][:, hh], rhs=br[:, unit(hh, 0)], start=False, stop=False)
            rest_of(ahead)
            RW.act.wait(pe, "sa1", r)
            for hh in range(4):
                ins = nc.tensor.matmul(y_of(hh, 1), lhsT=rw_sa[1][:, hh], rhs=br[:, unit(hh, 1)], start=False, stop=(hh >= 2))
            RW.pe.done(ins, "y", r)

        def two_parts(copy, name, q):
            m = rw_mat[name]
            copy(m[0:64, :, :], q[0:64], slice(0, 64), slice(0, P))
            return copy(m[64:P, :, 64:P], q[64:P, :, 64:P], slice(64, P), slice(64, P))

        def rw_act(act, r):
            copy = lambda o, i, *_: nc.scalar.activation(o, i, ACT.Copy)
            MT.wait(act, "ba", r)
            RW.act.done(two_parts(copy, "ba", quad(0)), "ba", r)
            RW.pe.wait(act, "br", r)
            RW.act.done(two_parts(copy, "br", pgq(0)), "br", r)
            rest_of(inverse_act(act, RW, r, rw_tt))
            by_head = lambda c: (pg[:, 0, :, 0:P].rearrange("p a (b c) -> p a b c", b=2) if c else
                                 pg[:, 1, 1, 0:T].rearrange("p (a b c) -> p a b c", a=2, b=2))
            for c in range(2):
                RW.pe.wait(act, f"r{c}", r)
                RW.act.done(nc.scalar.activation(rw_rh[:, :, :].rearrange("p (a b) c -> p a b c", a=2), by_head(c),
                                                 ACT.Copy, scale=-1.0), f"r{c}", r)
                RW.pe.wait(act, f"sa{c}", r)
                RW.act.done(nc.scalar.activation(rw_sa[c][:, :, :], sa_bank.rearrange("p (b c) -> p b c", b=4),
                                                 ACT.Copy), f"sa{c}", r)
                if not c:
                    RW.pe.wait(act, "st", r)
                    for j in range(2):
                        ins = nc.scalar.activation(rw_st[:, j], st_bank[:, 64 * j:64 * j + 64], ACT.Copy,
                                                   scale=fac[:, 2 * r + j:2 * r + j + 1])
                    RW.act.done(ins, "st", r)

        def rw_dve(dve, r):
            if not r:
                for m in rw_mat.values():
                    ins = nc.vector.memset(m[64:P, :, 0:64], 0.0)
                dve_link(ins)
            masked = lambda name: (lambda o, i, p_, c_: nc.vector.tensor_tensor(
                o, i, const(name)[p_, None, c_].to_broadcast([64, 8, c_.stop - c_.start]), ALU.mult))

            RW.act.wait(dve, "ba", r)
            inverse_m0_dve(RW, r, rw_mat["ba"], rw_nm)
            MT.wait(dve, "ka", r)
            RW.dve.done(two_parts(masked("before"), "ka", quad(2)), "ka", r)
            inverse = inverse_dve(dve, RW, r, rw_mat["ba"], rw_nm, rw_x, rw_xt)
            next(inverse)
            RW.act.wait(dve, "br", r)
            br = rw_mat["br"]
            dve_link(nc.vector.tensor_tensor(br[:, :, :], br[:, :, :], const("incl")[:, None, :].to_broadcast([P, 8, P]),
                                             ALU.mult))
            RW.pe.wait(dve, "kr", r)
            RW.dve.done(two_parts(masked("incl"), "kr", pgq(1)), "kr", r)
            rest_of(inverse)
            if not r:
                for j in range(8):
                    ins = nc.vector.tensor_scalar(rw_bn[:, j], rw_bn[:, j], v2("rw_ln_b_2", j), None, ALU.add)
                dve_link(ins)
            RW.pe.wait(dve, "y", r)
            RW.dve.done(nc.vector.tensor_copy(work[:, RR + 2 * r:RR + 2 * r + 2, PAD:COLS],
                                              y_bank.rearrange("p (j t) -> p j t", j=2)), "y", r)

        RN = Trio("rwn", ["mean", "var", "gate"], ["mid", "y1", "y3", "y4", "lo"], ["sq", "ln", "root", "hi"])

        def rwn_pe(pe):
            RW.dve.wait(pe, "y", 3)
            RN.pe.done(eight("ones_head", rw_r), "mean")
            yield
            RN.act.wait(pe, "sq")
            RN.pe.done(eight("ones_head", rw_d), "var")
            yield
            RN.act.wait(pe, "ln")
            pe.wait_ge(lora_in, 16 * 3)
            for j in range(8):
                ins = nc.tensor.matmul(all4[:, j], lhsT=rw_g2[:, j * P:(j + 1) * P], rhs=work[:, RG, PAD:COLS], start=True,
                                       stop=True)
            RN.pe.done(ins, "gate")
            yield
            RN.dve.wait(pe, "y4")
            for n in range(4):
                norm_pe(pe, 5, 4 * n, 4 * n + 4)
                yield

        def rwn_act(act):
            RN.dve.wait(act, "mid")
            RN.act.done(nc.scalar.activation(rw_d[:, :, :], rw_r, ACT.Square), "sq")
            yield
            RN.pe.wait(act, "var")
            RN.act.done(nc.scalar.activation(rw_a[:, :, :], all4, ACT.Ln, scale=1.0 / RW_D, bias=64e-5), "ln")
            RN.act.wait(act, "ln")
            RN.act.done(nc.scalar.activation(rw_a[:, :, :], rw_a[:, :, :], ACT.Exp, scale=-0.5), "root")
            yield
            RN.dve.wait(act, "y4")
            RN.act.done(nc.scalar.activation(xb[:, 8:16, 0:T], rw_r, ACT.Copy), "hi")
            yield
            act.wait_ge(mem_in, 16)
            for n in range(4):
                for k in range(4 * n, 4 * n + 4):
                    square_tile(act, 5, k, mem, 0, 0)
                if n == 3:
                    norm_root(act, 5)
                yield
            for n in range(8):
                norm_split_act(act, 3, xa, sq, 2 * n, 2 * n + 2)
                yield

        def rwn_dve(dve):
            RN.pe.wait(dve, "mean")
            RN.dve.done(nc.vector.scalar_tensor_tensor(out=rw_r, in0=all4, scalar=-1.0 / RW_D, in1=rw_r, op0=ALU.mult,
                                                       op1=ALU.add), "mid")
            yield
            yield
            RN.act.wait(dve, "root")
            for j in range(8):
                y = work[:, RR + j, PAD:COLS]
                ins = nc.vector.scalar_tensor_tensor(out=y, in0=y, scalar=v2("rw_ln_w_2", j), in1=rw_a[:, j],
                                                     op0=ALU.mult, op1=ALU.mult)
            RN.dve.done(ins, "y1")
            RN.dve.wait(dve, "y1")
            RN.dve.done(nc.vector.tensor_tensor(rw_r, rw_r, rw_bn[:, :, :], ALU.add), "y3")
            RN.dve.wait(dve, "y3")
            RN.pe.wait(dve, "gate")
            RN.dve.done(nc.vector.tensor_tensor(rw_r, rw_r, all4, ALU.mult), "y4")
            yield
            RN.act.wait(dve, "hi")
            RN.dve.done(nc.vector.tensor_tensor(xb[:, 8:16, T:2 * T], rw_r, xb[:, 8:16, 0:T].bitcast(F32), ALU.subtract),
                        "lo")
            for n in range(4):
                yield
            norm_rs_dve(dve, 5)
            for n in range(8):
                norm_split_dve(dve, 3, xa, mem, 0, 0, lambda k: v2("mem_norm_w_2", k), 80, sq, 2 * n, 2 * n + 2)
                yield

        XA_ = Trio("xat", ["s", "v", "p", "o"], ["max", "sub", "sum", "div", "p", "lo"], ["v", "exp", "hi"])
        xs4 = xs[:, :, :].rearrange("p (h m) k -> p h m k", m=2)

        def xat_pe(pe):
            blocks_out(pe, g_xq)
            for h in range(XA_H):
                for m in range(2):
                    ins = nc.tensor.matmul(all4[:, 2 * h + m], lhsT=chunk(8 + h, m), rhs=work[:, h, PAD:COLS], start=True,
                                           stop=True)
            XA_.pe.done(ins, "s")
            for n in range(8):
                ins = nc.tensor.transpose(pgq(0)[:, n], chunk(4 + n // 2, n % 2), const("ident"))
            XA_.pe.done(ins, "v")
            XA_.dve.wait(pe, "div")
            for kh in range(2):
                for h in range(XA_H):
                    for m in range(2):
                        ins = nc.tensor.transpose(all4[:, 4 * kh + h, m * P:(m + 1) * P], xs[:, 2 * h + m, kh * P:(kh + 1) * P],
                                                  const("ident"))
            XA_.pe.done(ins, "p")
            XA_.act.wait(pe, "v")
            XA_.dve.wait(pe, "p")
            for h in range(XA_H):
                for kh in range(2):
                    ins = nc.tensor.matmul(all4[:, 4 + h], lhsT=xv[:, h, kh], rhs=xp[:, 4 * kh + h], start=(kh == 0),
                                           stop=(kh == 1))
            XA_.pe.done(ins, "o")

        def xat_act(act):
            XA_.pe.wait(act, "v")
            XA_.act.done(nc.scalar.activation(xv[:, :, :, :].rearrange("p h m d -> p (h m) d"), pgq(0), ACT.Copy), "v")
            XA_.dve.wait(act, "sub")
            XA_.act.done(nc.scalar.activation(xs[:, :, :], xs[:, :, :], ACT.Exp, scale=XA_D ** -0.5), "exp")
            XA_.pe.wait(act, "o")
            XA_.act.done(nc.scalar.activation(xb[:, 0:4, 0:T], all4[:, 4:8], ACT.Copy), "hi")

        def xat_dve(dve):
            XA_.pe.wait(dve, "s")
            XA_.dve.done(nc.vector.tensor_reduce(xm[:, 0:8], all4, AX.X, ALU.max), "max")
            XA_.dve.wait(dve, "max")
            XA_.dve.done(nc.vector.tensor_tensor(xs[:, :, :], all4, xm[:, 0:8, None].to_broadcast([P, 8, T]), ALU.subtract),
                         "sub")
            XA_.act.wait(dve, "exp")
            XA_.dve.done(nc.vector.tensor_reduce(xm[:, 8:16], xs[:, :, :], AX.X, ALU.add), "sum")
            XA_.dve.wait(dve, "sum")
            dve_link(nc.vector.reciprocal(xm[:, 8:16], xm[:, 8:16]))
            XA_.dve.done(nc.vector.tensor_tensor(xs[:, :, :], xs[:, :, :], xm[:, 8:16, None].to_broadcast([P, 8, T]),
                                                 ALU.mult), "div")
            XA_.pe.wait(dve, "p")
            XA_.dve.done(nc.vector.tensor_copy(xp[:, :, :], all4), "p")
            XA_.act.wait(dve, "hi")
            XA_.dve.done(nc.vector.tensor_tensor(xb[:, 0:4, T:2 * T], all4[:, 4:8], xb[:, 0:4, 0:T].bitcast(F32),
                                                 ALU.subtract), "lo")

        block = ctx.enter_context(nc.Block())

        @block.sync
        def _(sp):
            for n in range(4):
                sp.dma_start(resid[:, 4 * n:4 * n + 4], a["x"][:, 4 * n:4 * n + 4]).then_inc(resid_in[n], 16)
            sp.dma_start(cst[:, :, :], a["consts"]).then_inc(consts_in, 16)
            sp.dma_start(vec[:, :], a["vecs"]).then_inc(consts_in, 16)
            for g in plan.stages:
                load_weights(sp, g)
            for n in range(4):
                sp.wait_ge(out_ready, 4 * n + 4)
                sp.dma_start(out.rearrange("(k p) t -> p k t", p=P)[:, 4 * n:4 * n + 4],
                             work[:, 4 * n:4 * n + 4, PAD:COLS]).then_inc(out_done, 16)
            sp.wait_ge(out_done, 64)

        @block.gpsimd
        def _(pool):
            pool.wait_ge(x_ready, 48)
            pool.dma_start(masks[:, :, :], a["masks"]).then_inc(masks_in, 16)
            pool.dma_start(al, a["dn_ab"]).then_inc(masks_in, 16)
            blocks_out(pool, g_rw)
            pool.dma_start(rw_lw[0:64, :], a["rw_w2_2"]).then_inc(lora_in, 16)
            pool.dma_start(rw_lw[64:P, :], a["rw_a2_2"]).then_inc(lora_in, 16)
            RW.dve.wait(pool, "y", 3)
            pool.dma_start(rw_g2[:, :], a["rw_g2_2"]).then_inc(lora_in, 16)
            pool.dma_start(mem[:, :, :], a["mem"]).then_inc(mem_in, 16)

        @block.scalar
        def _(act):
            act.wait_ge(consts_in, 32)
            norm_act(act, 0, resid, 0, 0, lambda e, k: e.wait_ge(resid_in[k // 4], 16))
            split_hi(act, g_glu, 0, 0)
            norm_split_act(act, 0, xa)
            gemm_act(act, g_glu, follows=g_qkv)
            blocks_out(act, g_glu)
            nc.scalar.activation(glu(TB), glu(TB), ACT.Sigmoid).then_inc(glu_sig, 1)
            gemm_act(act, g_qkv, follows=g_gsb)
            gemm_act(act, g_gsb, lambda m: att_act(act, m), follows=g_gcv)
            gemm_act(act, g_gcv, lambda m: att_act(act, m + 8), follows=g_sbo)
            att_act(act, 16)
            blocks_out(act, g_gcv)
            nc.scalar.activation(gates(TGS), gates(TGS), ACT.Sigmoid).then_inc(gates_done, 1)
            nc.scalar.activation(gates(TGC), gates(TGC), ACT.Sigmoid).then_inc(gates_done, 1)
            gemm_act(act, g_sbo, lambda m: ln_act(act, m), follows=g_cvo)
            gemm_act(act, g_cvo, lambda m: merge_act(act, m - 1), follows=g_wo)
            merge_act(act, 7)
            gemm_act(act, g_wo, squares_beside(act, g_wo, 1, work, PAD, 16), follows=ff1[0])
            norm_act(act, 1, work, PAD, 16, lambda e, k: blocks_out(e, g_wo), DT - 2)
            norm_act(act, 2, resid, 0, 0, lambda e, k: e.wait_ge(norm_res, k + 1))
            norm_split_act(act, 1, xa)
            for g, n in zip(ff1, ff1[1:] + [g_dn]):
                gemm_act(act, g, squares_beside(act, g, 3, work, PAD, 16) if g is ff1[-1] else None, follows=n)
            norm_act(act, 3, work, PAD, 16, lambda e, k: blocks_out(e, ff1[-1]), DT - 2)
            norm_act(act, 4, resid, 0, 0, lambda e, k: e.wait_ge(norm_res, DT + k + 1))
            norm_split_act(act, 2, xa)

            def conv_l2(m):
                dn_conv_act(act, m)
                l2_act(act, m)
            gemm_act(act, g_dn, conv_l2, follows=g_gab)
            gemm_act(act, g_gab, lambda m: l2_act(act, 16), follows=g_rw)
            core = dn_core(act, gates_act, dn_act, dnf_act)
            gemm_act(act, g_rw, follows=g_oa, each=step_of(core))
            rwp_first_act(act)
            rest_of(core)
            rwp_act(act)
            for r in range(4):
                rw_act(act, r)
            tail = rwn_act(act)
            gemm_act(act, g_oa, follows=g_mk, each=step_of(tail))
            rest_of(tail)
            gemm_act(act, g_mk, follows=g_mv)
            gemm_act(act, g_mv, follows=g_ob)
            gemm_act(act, g_ob, squares_beside(act, g_ob, 6, resid, 0, 0), follows=g_xq)
            norm_act(act, 6, resid, 0, 0, lambda e, k: blocks_out(e, g_ob), DT - 2)
            norm_split_act(act, 4, xa)
            gemm_act(act, g_xq, follows=g_xo)
            xat_act(act)
            gemm_act(act, g_xo, squares_beside(act, g_xo, 7, resid, 0, 0), follows=ff2[0])
            norm_act(act, 7, resid, 0, 0, lambda e, k: blocks_out(e, g_xo), DT - 2)
            norm_split_act(act, 5, xa)
            for g, n in zip(ff2, ff2[1:] + [None]):
                gemm_act(act, g, squares_beside(act, g, 8, resid, 0, 0) if g is ff2[-1] else None, follows=n)
            norm_act(act, 8, resid, 0, 0, lambda e, k: blocks_out(e, ff2[-1]), DT - 2)

        @block.vector
        def _(dve):
            dve.sem_inc(lo_ready, RING)
            dve.sem_inc(slab_used, RING)
            dve.sem_inc(evacuated, 2)
            dve_link(nc.vector.memset(u[:, :, 0:UPAD], 0.0))
            dve_link(nc.vector.memset(work[:, :, 0:PAD], 0.0))
            dve.wait_ge(consts_in, 32)
            split_lo(dve, g_glu, 0, 0)
            norm_rs_dve(dve, 0)
            norm_split_dve(dve, 0, xa, resid, 0, 0, lambda k: v1("g_pre_mix", k), 0)
            gemm_dve(dve, g_glu, follows=g_qkv)
            dve.wait_ge(glu_sig, 1)
            dve_link(nc.vector.tensor_tensor(u[:, :, UPAD:UCOLS], glu(TA), glu(TB), ALU.mult))
            gemm_dve(dve, g_qkv, lambda m: conv(dve, share(m)), follows=g_gsb)

            def beside(m):
                att_dve(dve, m)
                conv(dve, share(12 + m))
            gemm_dve(dve, g_gsb, beside, follows=g_gcv)
            gemm_dve(dve, g_gcv, lambda m: beside(m + 8), follows=g_sbo)
            att_dve(dve, 16)
            dve.wait_ge(gates_done, 2)
            gemm_dve(dve, g_sbo, lambda m: ln_dve(dve, m), follows=g_cvo)
            gemm_dve(dve, g_cvo, lambda m: merge_dve(dve, m), follows=g_wo)
            merge_dve(dve, 8)
            gemm_dve(dve, g_wo, follows=ff1[0])
            norm_add_dve(dve, 1, 0, 16, lambda k: v1("g_post_mix", k))
            norm_rs_dve(dve, 2)
            norm_split_dve(dve, 1, xa, resid, 0, 0, lambda k: v1("g_pre_mlp", k), 48)
            for g, n in zip(ff1, ff1[1:] + [g_dn]):
                gemm_dve(dve, g, follows=n)
            norm_add_dve(dve, 3, 1, 16, lambda k: v1("g_post_mlp", k))
            norm_rs_dve(dve, 4)
            norm_split_dve(dve, 2, xa, resid, 0, 0, lambda k: v2("mix_norm_w_2", k), 64)

            def conv_l2(m):
                dn_conv_dve(dve, m)
                l2_dve(dve, m)
            gemm_dve(dve, g_dn, conv_l2, follows=g_gab)
            gemm_dve(dve, g_gab, lambda m: conv_l2(16), follows=g_rw)
            core = dn_core(dve, gates_dve, dn_dve, dnf_dve)
            dve_link(nc.vector.tensor_scalar(omka, vec[:, NV1 + V2["rw_k_a_2"]:NV1 + V2["rw_k_a_2"] + 8], -1.0, 1.0,
                                             ALU.mult, ALU.add))
            gemm_dve(dve, g_rw, lambda m: shift_dve(dve, m), follows=g_oa, each=step_of(core))
            rest_of(core)
            rwp_dve(dve)
            for r in range(4):
                rw_dve(dve, r)
            tail = rwn_dve(dve)
            gemm_dve(dve, g_oa, follows=g_mk, each=step_of(tail))
            rest_of(tail)
            gemm_dve(dve, g_mk, follows=g_mv)
            gemm_dve(dve, g_mv, follows=g_ob)
            gemm_dve(dve, g_ob, follows=g_xq)
            norm_rs_dve(dve, 6)
            norm_split_dve(dve, 4, xa, resid, 0, 0, lambda k: v2("xa_norm_w_2", k), 96)
            gemm_dve(dve, g_xq, follows=g_xo)
            xat_dve(dve)
            gemm_dve(dve, g_xo, follows=ff2[0])
            norm_rs_dve(dve, 7)
            norm_split_dve(dve, 5, xa, resid, 0, 0, lambda k: v2("ffn_norm_w_2", k), 112)
            for g, n in zip(ff2, ff2[1:] + [None]):
                gemm_dve(dve, g, follows=n)
            norm_rs_dve(dve, 8)
            for k in range(DT):
                nc.vector.scalar_tensor_tensor(out=work[:, k, PAD:COLS], in0=resid[:, k], scalar=v2("final_norm_w_2", k),
                                               in1=rs[:, :], op0=ALU.mult, op1=ALU.mult).then_inc(out_ready, 1)

        @block.tensor
        def _(pe):
            pe.wait_ge(consts_in, 32)
            norm_pe(pe, 0)
            gemm_pe(pe, g_glu, x_tiles=0)
            gemm_pe(pe, g_qkv)
            gemm_pe(pe, g_gsb, lambda m: att_pe(pe, m))
            gemm_pe(pe, g_gcv, lambda m: att_pe(pe, m + 8))
            att_pe(pe, 16)
            pe.wait_ge(att_lo, SB_H)
            gemm_pe(pe, g_sbo, lambda m: ln_pe(pe, m))
            pe.wait_ge(x_ready, 32)
            gemm_pe(pe, g_cvo)
            gemm_pe(pe, g_wo, sums_beside(pe, 1), x_tiles=32)
            norm_pe(pe, 1, LATE)
            norm_pe(pe, 2)
            gemm_pe(pe, ff1[0], x_tiles=48)
            for n, g in enumerate(ff1[1:]):
                gemm_pe(pe, g, sums_beside(pe, 3) if g is ff1[-1] else None, of=None if n % 2 else ff1[n])
            norm_pe(pe, 3, LATE)
            norm_pe(pe, 4)
            gemm_pe(pe, g_dn, lambda m: l2_pe(pe, m), x_tiles=64)
            gemm_pe(pe, g_gab, lambda m: l2_pe(pe, 16))
            core = dn_core(pe, gates_pe, dn_pe, dnf_pe)
            gemm_pe(pe, g_rw, each=step_of(core))
            rest_of(core)
            rwp_pe(pe)
            RP.dve.wait(pe, "t3")
            RP.act.wait(pe, "t2")
            for r in range(4):
                rw_pe(pe, r)
            DF.dve.wait(pe, "lo")
            tail = rwn_pe(pe)
            gemm_pe(pe, g_oa, each=step_of(tail))
            rest_of(tail)
            gemm_pe(pe, g_mk, x_tiles=80)
            gemm_pe(pe, g_mv)
            RN.dve.wait(pe, "lo")
            gemm_pe(pe, g_ob, sums_beside(pe, 6))
            norm_pe(pe, 6, LATE)
            gemm_pe(pe, g_xq, x_tiles=96)
            blocks_out(pe, g_mv)
            xat_pe(pe)
            XA_.dve.wait(pe, "lo")
            gemm_pe(pe, g_xo, sums_beside(pe, 7))
            norm_pe(pe, 7, LATE)
            gemm_pe(pe, ff2[0], x_tiles=112)
            for n, g in enumerate(ff2[1:]):
                gemm_pe(pe, g, sums_beside(pe, 8) if g is ff2[-1] else None, of=None if n % 2 else ff2[n])
            norm_pe(pe, 8, LATE)


def kernel(**inputs):
    import numpy as _np
    import concourse.bacc as _bacc
    from concourse import mybir as _mybir
    from concourse.bass_utils import run_bass_kernel_spmd as _run

    def tiles(x):
        x = _np.asarray(x)
        return x.reshape(-1, P).T

    nc = _bacc.Bacc("TRN2", target_bir_lowering=False, num_devices=1)
    arrays = {
        "x": _np.ascontiguousarray(_np.asarray(inputs["x"])[0].T.reshape(DT, P, T).transpose(1, 0, 2)),
        "consts": constants().reshape(P, len(CONSTS), P),
        "masks": level_masks(),
        "vecs": _np.concatenate([tiles(inputs[n]) for n, _ in VEC1 + VEC2], axis=1),
        "mem": _np.asarray(inputs["mem_2"])[0].T.reshape(DT, P, T).transpose(1, 0, 2),
        "dn_ab": _np.stack([_np.asarray(inputs[n])[0] for n in ("dn_a_log_2", "dn_dt_bias_2")], axis=1),
    }
    for name in ("w_in", "w_sb_out", "w_conv_out", "w_o", "w_up", "w_down", "w_in_2", "w_out_2", "xa_wq_2", "xa_wk_2",
                 "xa_wv_2", "xa_wo_2", "ffn_w1_2", "ffn_w2_2", "rw_w2_2", "rw_a2_2", "rw_g2_2"):
        arrays[name] = _np.asarray(inputs[name])[0]
    arrays = {k: _np.ascontiguousarray(v) for k, v in arrays.items()}
    aps = {k: nc.dram_tensor(k, v.shape, _mybir.dt.from_np(v.dtype), kind="ExternalInput").ap() for k, v in arrays.items()}
    out = nc.dram_tensor("out", (D, T), F32, kind="ExternalOutput").ap()
    build_program(nc, aps, out)
    r = _run(nc, [arrays], core_ids=[0])
    return _np.ascontiguousarray(r.results[0]["out"].T).reshape(1, T, D)
```
